# Optimizing a Trainium2 kernel written in Bass

```python
import jax, jax.numpy as jnp
from jax import lax
import numpy as np

D_MODEL = 1024
BATCH = 1
SEQ = 128
DEPTH = 2
DEC_BATCH = 1
DEC_SEQ = 512
PAST_LEN = 128

GRID_W = 64
HEAD_DIM = 64
BRANCH_W = 256
N_BRANCH = 4
CHUNK = 128
GMLP_GROUPS = 4
CONV_W = 31
RWKV_HEADS = 4
N_DIR = 2
DECAY_LORA = 64
ICL_LORA = 64
GATE_LORA = 128
ATT_HEADS = 4
KV_HEADS = 2
Q_PER_KV = ATT_HEADS // KV_HEADS
WINDOW = 128
BLOCK = 128
ROPE_BASE = 10000.0
ATT_SCALE = HEAD_DIM ** -0.5
NEG_INF = -1e30
N_GROUPS = 4
EXPERTS_PER_GROUP = 4
N_EXPERTS = N_GROUPS * EXPERTS_PER_GROUP
TOP_K = 2
EXPERT_FF = 256
N_MOD = 6
RMS_EPS = 1e-6
LN_EPS = 1e-5
GN_EPS = 64e-5
SPLIT_SIZES = (BRANCH_W, BRANCH_W, BRANCH_W, BRANCH_W, BRANCH_W, BRANCH_W, BRANCH_W, N_DIR * DECAY_LORA, N_DIR * ICL_LORA, GATE_LORA, ATT_HEADS * HEAD_DIM, KV_HEADS * HEAD_DIM, KV_HEADS * HEAD_DIM)
IN_COLS = sum(SPLIT_SIZES)

kernel_name = 'hybrid_prefix_diffusion_step'

def rmsnorm(x, g):
    xf = x.astype(jnp.float32)
    y = xf * lax.rsqrt(jnp.mean(xf * xf, axis=-1, keepdims=True) + RMS_EPS)
    return (y * g.astype(jnp.float32)).astype(x.dtype)

def layernorm(x, g, b=None, eps=LN_EPS):
    xf = x.astype(jnp.float32)
    mu = jnp.mean(xf, axis=-1, keepdims=True)
    var = jnp.mean(jnp.square(xf - mu), axis=-1, keepdims=True)
    y = (xf - mu) * lax.rsqrt(var + eps) * g.astype(jnp.float32)
    if b is not None:
        y = y + b.astype(jnp.float32)
    return y.astype(x.dtype)

def split_cols(z):
    idx, acc = [], 0
    for s in SPLIT_SIZES[:-1]:
        acc += s
        idx.append(acc)
    return jnp.split(z, idx, axis=-1)

def rope_axis(x, pos):
    half = x.shape[-1] // 2
    inv = ROPE_BASE ** (-jnp.arange(half, dtype=jnp.float32) / half)
    ang = pos.astype(jnp.float32)[:, None] * inv[None, :]
    cos = jnp.cos(ang)[None, :, None, :].astype(x.dtype)
    sin = jnp.sin(ang)[None, :, None, :].astype(x.dtype)
    x1, x2 = x[..., :half], x[..., half:]
    return jnp.concatenate([x1 * cos - x2 * sin, x2 * cos + x1 * sin], axis=-1)

def rope_2d(x, row, col):
    r = HEAD_DIM // 2
    return jnp.concatenate([rope_axis(x[..., :r], row), rope_axis(x[..., r:], col)], axis=-1)

def gmlp_spatial_gate(u, v, ln_g, ws, bs):
    B, L, W = v.shape
    vn = layernorm(v, ln_g).reshape(B, L // CHUNK, CHUNK, GMLP_GROUPS, W // GMLP_GROUPS)
    mixed = jnp.einsum('gpq,bcqgd->bcpgd', ws, vn) + bs.T[:, :, None]
    return u * mixed.reshape(B, L, W)

def conformer_conv(val, gate, conv_w, conv_b, ln_g, ln_b):
    y = val * jax.nn.sigmoid(gate)
    y = lax.conv_general_dilated(y, conv_w[:, None, :], window_strides=(1,), padding=[(CONV_W // 2, CONV_W // 2)], dimension_numbers=('NWC', 'WIO', 'NWC'), feature_group_count=BRANCH_W) + conv_b
    return jax.nn.silu(layernorm(y, ln_g, ln_b))

def rwkv_scan(r, w, k, v, kk, a, s0, reverse):
    def step(S, inp):
        r_t, w_t, k_t, v_t, kk_t, a_t = inp
        sa = jnp.einsum('bhvk,bhk->bhv', S, -kk_t)
        S = S * w_t[:, :, None, :] + sa[..., None] * (kk_t * a_t)[:, :, None, :] + v_t[..., None] * k_t[:, :, None, :]
        return S, jnp.einsum('bhvk,bhk->bhv', S, r_t)
    xs = tuple(jnp.moveaxis(t, 1, 0) for t in (r, w, k, v, kk, a))
    s_fin, ys = lax.scan(step, s0, xs, reverse=reverse)
    return s_fin, jnp.moveaxis(ys, 0, 1)

def rwkv7_bidir(r, k, v, wd, ad, gd, lp, s_init):
    B, L, W = r.shape
    f32 = jnp.float32
    heads = lambda t: t.reshape(B, L, RWKV_HEADS, HEAD_DIM)
    w_raw = lp['rwkv_w0'] + jnp.einsum('bldr,drc->bldc', jnp.tanh(wd.reshape(B, L, N_DIR, DECAY_LORA)), lp['rwkv_w2'])
    decay = jnp.exp(-jnp.exp(-jax.nn.softplus(-w_raw.astype(f32)) - 0.5))
    a = jax.nn.sigmoid((lp['rwkv_a0'] + jnp.einsum('bldr,drc->bldc', ad.reshape(B, L, N_DIR, ICL_LORA), lp['rwkv_a2'])).astype(f32))
    g = jax.nn.sigmoid(gd) @ lp['rwkv_g2']
    kk = heads((k * lp['rwkv_kk']).astype(f32))
    kk = kk / jnp.maximum(jnp.sqrt(jnp.sum(kk * kk, axis=-1, keepdims=True)), 1e-12)
    k_dir = k.astype(f32)[:, :, None, :] * (1.0 + (a - 1.0) * lp['rwkv_ka'].astype(f32))
    rf, vf = heads(r.astype(f32)), heads(v.astype(f32))
    s0 = jnp.zeros((B, N_DIR, RWKV_HEADS, HEAD_DIM, HEAD_DIM), f32) if s_init is None else s_init.astype(f32)
    s_f, y_f = rwkv_scan(rf, heads(decay[:, :, 0]), heads(k_dir[:, :, 0]), vf, kk, heads(a[:, :, 0]), s0[:, 0], False)
    s_b, y_b = rwkv_scan(rf, heads(decay[:, :, 1]), heads(k_dir[:, :, 1]), vf, kk, heads(a[:, :, 1]), s0[:, 1], True)
    y = y_f + y_b
    mu = jnp.mean(y, axis=-1, keepdims=True)
    var = jnp.mean(jnp.square(y - mu), axis=-1, keepdims=True)
    y = ((y - mu) * lax.rsqrt(var + GN_EPS)).reshape(B, L, W) * lp['rwkv_lnx_g'].astype(f32) + lp['rwkv_lnx_b'].astype(f32)
    bonus = jnp.sum(rf * heads(k_dir[:, :, 0] + k_dir[:, :, 1]) * lp['rwkv_rk'].astype(f32), axis=-1, keepdims=True) * vf
    y = y + bonus.reshape(B, L, W)
    return y.astype(r.dtype) * g, jnp.stack([s_f, s_b], axis=1)

def sink_attend(q, keys, vals, masks, sink):
    scores = []
    for kx, mk in zip(keys, masks):
        s = jnp.einsum('bqkgd,bskd->bkgqs', q, kx).astype(jnp.float32) * ATT_SCALE
        scores.append(s if mk is None else jnp.where(mk, s, NEG_INF))
    sink_col = jnp.broadcast_to(sink.astype(jnp.float32)[None, :, :, None, None], scores[0].shape[:-1] + (1,))
    p = jax.nn.softmax(jnp.concatenate(scores + [sink_col], axis=-1), axis=-1)
    out, off = None, 0
    for s, vx in zip(scores, vals):
        n = s.shape[-1]
        o = jnp.einsum('bkgqs,bskd->bqkgd', p[..., off:off + n].astype(vx.dtype), vx)
        out = o if out is None else out + o
        off += n
    return out

def context_attention(q, k, v, sink):
    B, L = q.shape[:2]
    nb = L // BLOCK
    qb = jnp.moveaxis(q.reshape(B, nb, BLOCK, KV_HEADS, Q_PER_KV, HEAD_DIM), 1, 0)
    o = lax.map(lambda qi: sink_attend(qi, [k], [v], [None], sink), qb)
    return jnp.moveaxis(o, 0, 1).reshape(B, L, ATT_HEADS * HEAD_DIM)

def latent_attention(q, k, v, ctx_k, ctx_v, sink):
    B, T = q.shape[:2]
    nb = T // BLOCK
    qb = jnp.moveaxis(q.reshape(B, nb, BLOCK, KV_HEADS, Q_PER_KV, HEAD_DIM), 1, 0)

    def band(t):
        tp = jnp.pad(t, ((0, 0), (BLOCK, BLOCK), (0, 0), (0, 0))).reshape(B, nb + 2, BLOCK, KV_HEADS, HEAD_DIM)
        return jnp.moveaxis(jnp.concatenate([tp[:, :-2], tp[:, 1:-1], tp[:, 2:]], axis=2), 1, 0)

    i_rel = jnp.arange(BLOCK)[:, None]
    j_rel = jnp.arange(3 * BLOCK)[None, :]

    def one_block(args):
        qi, kw, vw, n = args
        i_abs = n * BLOCK + i_rel
        j_abs = n * BLOCK - BLOCK + j_rel
        mask = (jnp.abs(i_abs - j_abs) <= WINDOW) & (j_abs >= 0) & (j_abs < T)
        return sink_attend(qi, [kw, ctx_k], [vw, ctx_v], [mask, None], sink)

    o = lax.map(one_block, (qb, band(k), band(v), jnp.arange(nb)))
    return jnp.moveaxis(o, 0, 1).reshape(B, T, ATT_HEADS * HEAD_DIM)

def mixing_sublayer(h, lp, ctx):
    B, L, _ = h.shape
    (a_u, a_v, b_val, b_gate, c_r, c_k, c_v, c_wd, c_ad, c_gd, d_q, d_k, d_v) = split_cols(h @ lp['w_in'])
    o_a = gmlp_spatial_gate(jax.nn.gelu(a_u), jax.nn.gelu(a_v), lp['gmlp_ln_g'], lp['gmlp_ws'], lp['gmlp_bs'])
    o_b = conformer_conv(b_val, b_gate, lp['conv_w'], lp['conv_b'], lp['conv_ln_g'], lp['conv_ln_b'])
    o_c, s_fin = rwkv7_bidir(c_r, c_k, c_v, c_wd, c_ad, c_gd, lp, None if ctx is None else ctx[2])
    q = d_q.reshape(B, L, ATT_HEADS, HEAD_DIM)
    k = d_k.reshape(B, L, KV_HEADS, HEAD_DIM)
    v = d_v.reshape(B, L, KV_HEADS, HEAD_DIM)
    sink = lp['attn_sink'].reshape(KV_HEADS, Q_PER_KV)
    if ctx is None:
        o_d = context_attention(q, k, v, sink)
    else:
        ctx_k, ctx_v, _, row, col = ctx
        o_d = latent_attention(rope_2d(q, row, col), rope_2d(k, row, col), v, ctx_k, ctx_v, sink)
    branches = jnp.stack([o_a, o_b, o_c, o_d], axis=2)
    proj = jnp.einsum('blnw,nwd->blnd', branches, lp['w_branch'])
    gates = jax.nn.sigmoid(h @ lp['w_gate'] + lp['b_gate']).reshape(B, L, N_BRANCH, D_MODEL)
    out = jnp.einsum('blnd,blnd->bld', gates, proj) @ lp['w_out']
    return out, (k, v, s_fin)

def hier_moe(h, lp):
    B, L, D = h.shape
    t = h.reshape(B * L, D)
    g_logit = (t @ lp['w_rg'] + lp['b_rg']).astype(jnp.float32)
    g_prob = jax.nn.softmax(g_logit, axis=-1)
    _, g_idx = lax.top_k(g_logit, 1)
    g_sel = jax.nn.one_hot(g_idx[:, 0], N_GROUPS, dtype=jnp.float32)
    g_w = jnp.sum(g_prob * g_sel, axis=-1, keepdims=True)
    e_logit = (t @ lp['w_re'] + lp['b_re']).astype(jnp.float32).reshape(-1, N_GROUPS, EXPERTS_PER_GROUP)
    e_in = jnp.einsum('ng,nge->ne', g_sel, e_logit)
    e_val, e_idx = lax.top_k(e_in, TOP_K)
    w = g_w * jax.nn.softmax(e_val, axis=-1)
    expert = g_idx * EXPERTS_PER_GROUP + e_idx
    combine = jnp.einsum('nk,nke->ne', w, jax.nn.one_hot(expert, N_EXPERTS, dtype=jnp.float32)).astype(h.dtype)
    hid = jax.nn.silu(jnp.einsum('nd,edf->nef', t, lp['w_e_gate'])) * jnp.einsum('nd,edf->nef', t, lp['w_e_up'])
    out = jnp.einsum('nef,efd->nd', hid * combine[:, :, None], lp['w_e_down'])
    return out.reshape(B, L, D)

def trunk_layer(x, mod, lp, ctx):
    h = rmsnorm(x, lp['norm1_g']) * (1 + mod[:, 1, None]) + mod[:, 0, None]
    mix, ctx_out = mixing_sublayer(h, lp, ctx)
    x = x + mod[:, 2, None] * mix
    h = rmsnorm(x, lp['norm2_g']) * (1 + mod[:, 4, None]) + mod[:, 3, None]
    x = x + mod[:, 5, None] * hier_moe(h, lp)
    return x, ctx_out

def setup_inputs(seed: int = 0) -> dict:
    key = jax.random.key(seed)
    ks = iter(jax.random.split(key, 64))

    def nrm(shape, scale=1.0):
        return jax.random.normal(next(ks), shape, jnp.float32) * scale

    D, W = D_MODEL, BRANCH_W
    return {
        'x_prompt': nrm((BATCH, SEQ, D)),
        'x_sample': nrm((DEC_BATCH, DEC_SEQ, D)),
        'cache_k': nrm((DEC_BATCH, DEPTH, PAST_LEN, KV_HEADS, HEAD_DIM)),
        'cache_v': nrm((DEC_BATCH, DEPTH, PAST_LEN, KV_HEADS, HEAD_DIM)),
        'state_rwkv': nrm((DEC_BATCH, DEPTH, N_DIR, RWKV_HEADS, HEAD_DIM, HEAD_DIM), 0.5),
        'c': nrm((DEC_BATCH, D)),
        'c_ctx': nrm((D,)),
        'norm1_g': 1.0 + nrm((DEPTH, D), 0.02),
        'norm2_g': 1.0 + nrm((DEPTH, D), 0.02),
        'final_norm_g': 1.0 + nrm((D,), 0.02),
        'w_mod': nrm((DEPTH, D, N_MOD * D), 0.5 * D ** -0.5),
        'b_mod': nrm((DEPTH, N_MOD * D), 0.02),
        'w_in': nrm((DEPTH, D, IN_COLS), D ** -0.5),
        'gmlp_ln_g': 1.0 + nrm((DEPTH, W), 0.02),
        'gmlp_ws': nrm((DEPTH, GMLP_GROUPS, CHUNK, CHUNK), CHUNK ** -0.5),
        'gmlp_bs': 1.0 + nrm((DEPTH, GMLP_GROUPS, CHUNK), 0.02),
        'conv_w': nrm((DEPTH, CONV_W, W), CONV_W ** -0.5),
        'conv_b': nrm((DEPTH, W), 0.02),
        'conv_ln_g': 1.0 + nrm((DEPTH, W), 0.02),
        'conv_ln_b': nrm((DEPTH, W), 0.02),
        'rwkv_w0': -2.0 + nrm((DEPTH, N_DIR, W), 0.5),
        'rwkv_w2': nrm((DEPTH, N_DIR, DECAY_LORA, W), 0.5 * DECAY_LORA ** -0.5),
        'rwkv_a0': nrm((DEPTH, N_DIR, W), 0.5),
        'rwkv_a2': nrm((DEPTH, N_DIR, ICL_LORA, W), 0.5 * ICL_LORA ** -0.5),
        'rwkv_g2': nrm((DEPTH, GATE_LORA, W), GATE_LORA ** -0.5),
        'rwkv_kk': 1.0 + nrm((DEPTH, W), 0.1),
        'rwkv_ka': 1.0 + nrm((DEPTH, W), 0.1),
        'rwkv_rk': nrm((DEPTH, RWKV_HEADS, HEAD_DIM), 0.1),
        'rwkv_lnx_g': 1.0 + nrm((DEPTH, W), 0.02),
        'rwkv_lnx_b': nrm((DEPTH, W), 0.02),
        'attn_sink': nrm((DEPTH, ATT_HEADS), 0.5),
        'w_gate': nrm((DEPTH, D, N_BRANCH * D), D ** -0.5),
        'b_gate': nrm((DEPTH, N_BRANCH * D), 0.02),
        'w_branch': nrm((DEPTH, N_BRANCH, W, D), W ** -0.5),
        'w_out': nrm((DEPTH, D, D), D ** -0.5),
        'w_rg': nrm((DEPTH, D, N_GROUPS), D ** -0.5),
        'b_rg': nrm((DEPTH, N_GROUPS), 0.01),
        'w_re': nrm((DEPTH, D, N_EXPERTS), D ** -0.5),
        'b_re': nrm((DEPTH, N_EXPERTS), 0.01),
        'w_e_gate': nrm((DEPTH, N_EXPERTS, D, EXPERT_FF), D ** -0.5),
        'w_e_up': nrm((DEPTH, N_EXPERTS, D, EXPERT_FF), D ** -0.5),
        'w_e_down': nrm((DEPTH, N_EXPERTS, EXPERT_FF, D), EXPERT_FF ** -0.5),
    }

def reference(x_prompt, x_sample, cache_k, cache_v, state_rwkv, c, c_ctx, norm1_g, norm2_g, final_norm_g, w_mod, b_mod, w_in, gmlp_ln_g, gmlp_ws, gmlp_bs, conv_w, conv_b, conv_ln_g, conv_ln_b, rwkv_w0, rwkv_w2, rwkv_a0, rwkv_a2, rwkv_g2, rwkv_kk, rwkv_ka, rwkv_rk, rwkv_lnx_g, rwkv_lnx_b, attn_sink, w_gate, b_gate, w_branch, w_out, w_rg, b_rg, w_re, b_re, w_e_gate, w_e_up, w_e_down):
    layer_params = {
        'norm1_g': norm1_g, 'norm2_g': norm2_g, 'w_mod': w_mod, 'b_mod': b_mod, 'w_in': w_in,
        'gmlp_ln_g': gmlp_ln_g, 'gmlp_ws': gmlp_ws, 'gmlp_bs': gmlp_bs,
        'conv_w': conv_w, 'conv_b': conv_b, 'conv_ln_g': conv_ln_g, 'conv_ln_b': conv_ln_b,
        'rwkv_w0': rwkv_w0, 'rwkv_w2': rwkv_w2, 'rwkv_a0': rwkv_a0, 'rwkv_a2': rwkv_a2, 'rwkv_g2': rwkv_g2,
        'rwkv_kk': rwkv_kk, 'rwkv_ka': rwkv_ka, 'rwkv_rk': rwkv_rk, 'rwkv_lnx_g': rwkv_lnx_g, 'rwkv_lnx_b': rwkv_lnx_b,
        'attn_sink': attn_sink, 'w_gate': w_gate, 'b_gate': b_gate, 'w_branch': w_branch, 'w_out': w_out,
        'w_rg': w_rg, 'b_rg': b_rg, 'w_re': w_re, 'b_re': b_re,
        'w_e_gate': w_e_gate, 'w_e_up': w_e_up, 'w_e_down': w_e_down,
    }
    n_lat = x_sample.shape[1]
    rows = n_lat // GRID_W
    row = jnp.repeat(jnp.arange(rows), GRID_W)
    col = jnp.tile(jnp.arange(GRID_W), rows)

    xp, xs = x_prompt, x_sample
    ks_out, vs_out, ss_out = [], [], []
    for l in range(DEPTH):
        lp = {name: arr[l] for name, arr in layer_params.items()}
        mod_ctx = (jax.nn.silu(c_ctx) @ lp['w_mod'] + lp['b_mod']).reshape(1, N_MOD, D_MODEL)
        mod_lat = (jax.nn.silu(c) @ lp['w_mod'] + lp['b_mod']).reshape(-1, N_MOD, D_MODEL)
        xp, (k_l, v_l, s_l) = trunk_layer(xp, mod_ctx, lp, None)
        ks_out.append(k_l)
        vs_out.append(v_l)
        ss_out.append(s_l.astype(x_prompt.dtype))
        xs, _ = trunk_layer(xs, mod_lat, lp, (cache_k[:, l], cache_v[:, l], state_rwkv[:, l], row, col))

    y_prompt = rmsnorm(xp, final_norm_g)
    y_sample = rmsnorm(xs, final_norm_g)
    new_cache_k = jnp.stack(ks_out, axis=1)
    new_cache_v = jnp.stack(vs_out, axis=1)
    new_state_rwkv = jnp.stack(ss_out, axis=1)
    return (y_prompt, y_sample, new_cache_k, new_cache_v, new_state_rwkv)


_drawn_inputs = setup_inputs


def setup_inputs(seed=0):
    import zlib

    import numpy as np

    out = dict(_drawn_inputs(seed))
    spreads = {}
    factors = {'cache_k': 3.815,
     'cache_v': 3.64,
     'state_rwkv': 8.0,
     'norm2_g': 3.883,
     'final_norm_g': 2.83,
     'gmlp_ln_g': 8.0,
     'gmlp_bs': 8.0,
     'conv_b': 7.056,
     'conv_ln_g': 8.0,
     'conv_ln_b': 8.0,
     'rwkv_lnx_g': 8.0,
     'rwkv_lnx_b': 8.0,
     'attn_sink': 8.0,
     'b_gate': 8.0,
     'b_rg': 6.485,
     'b_re': 7.971}
    for name, (base, spread) in spreads.items():
        noise = np.random.default_rng([zlib.crc32(name.encode()), seed]).standard_normal(out[name].shape)
        drawn = base * np.exp(spread * noise) if base else spread * noise
        out[name] = __import__('jax').numpy.asarray(drawn.astype(out[name].dtype))
    for name, factor in factors.items():
        out[name] = (out[name] * factor).astype(out[name].dtype)
    return out
```

```python
from contextlib import ExitStack

import numpy as np
import concourse.bass as bass
from concourse import mybir

F32 = mybir.dt.float32
ALU = mybir.AluOpType
ACT = mybir.ActivationFunctionType
AX = mybir.AxisListType

P = 128
D = 1024
DEPTH = 2
KT = D // P
NB = 5
LAT = NB - 1
TOK = NB * P
W = 256
FT = W // P
HD = 64
NE = 16
FF = 256
TAPS = 31
PAD = TAPS // 2
LINE = PAD + P + PAD + LAT * P + PAD
OUTS = LINE - 2 * PAD
LAT_OUT = P + PAD
LEVELS = 7
SLOT = KT * 512
MODS = 12
SLOTS_MOD, SLOTS_IN, SLOTS_BEHIND, SLOTS_BACK, SLOTS_OUT, SLOTS_UP, SLOTS_DOWN = 4, 6, 16, KT, 2, NE, 8
AT_IN = SLOTS_MOD
AT_BEHIND = AT_IN + SLOTS_IN
AT_BACK = AT_BEHIND + SLOTS_BEHIND
AT_OUT = AT_BACK + SLOTS_BACK
AT_UP = AT_OUT + SLOTS_OUT
AT_DOWN = AT_UP + SLOTS_UP
SLOTS = AT_DOWN + SLOTS_DOWN
RING = 2
HALF = TOK // 2
PIECES = KT * 4 * 2
STAGES = 4
STEPS = [(0, 0), (1, 4), (2, 3), (3, 2), (4, 1)]
CONV_PARTS, STEP_PARTS = 22, 26
RMS_EPS, LN_EPS, GN_EPS = 1e-6, 1e-5, 64e-5
NEG = -1e30
SCALE = HD ** -0.5


def parts_behind():
    parts, turn = [], None
    for n in range(SLOTS_BEHIND // 2 * 9):
        bank = 6 + n % 2
        if n % 9 == 0:
            i = SLOTS_MOD + n // 9
            parts += [("rows", i, 0, bank), ("rows", i, 1, bank)]
            turn = ("cols", i, 0, bank)
            if len(parts) == CONV_PARTS - 1:
                parts.append(turn)
                turn = None
        else:
            i = n // 9 * 8 + n % 9 - 1
            parts += [("gate", i, 0, bank), ("gate", i, 1, bank)]
            if turn:
                parts.append(turn)
                turn = None
    return parts


PARTS = parts_behind()
assert len(PARTS) == CONV_PARTS + STEP_PARTS * 5


def closed(n):
    return n + (n < len(PARTS) and PARTS[n][2])


def counted(what, n):
    return sum(p[0] == what and (p[2] == 1 or what == "cols") for p in PARTS[:n])


def fields(sizes):
    at, out = 0, {}
    for name, n in sizes:
        out[name] = (at, n)
        at += n
    return out, at


COLS, NCOLS = fields([("norm1", KT), ("norm2", KT), ("bmod", 48), ("bgate", 32), ("gmlp_bs", 4), ("conv_w", FT * TAPS),
                      ("conv_b", FT), ("wsT", 4 * P), ("w2", 2 * W), ("a2", 2 * W), ("g2", W), ("ckT", P), ("cv", P),
                      ("router", KT * 20), ("state", 4 * HD)])
ROWS, NROWS = fields([("gmlp_g", W), ("conv_g", W), ("conv_lb", W), ("w0", 2 * W), ("a0", 2 * W), ("kkw", W), ("ka", W),
                      ("rk", W), ("lnx_g", W), ("lnx_b", W), ("sink", 4), ("br", 20)])
FIX, NFIX = fields([("ident", P), ("cos", LAT * HD), ("sin", LAT * HD), ("band", 3 * P), ("iota", 4)])
SCANF, NSCANF = fields([("incl", 2 * P), ("excl", 2 * P), ("halves", 2)])
SCANB, NSCANB = fields([("gram", 4 * P), ("lev", (LEVELS - 1) * 2 * P), ("lev0", 4 * P)])
PER = {
    **{name: 1 for name in (
        "pads_zeroed", "pool_chain", "keys_ready", "scan_ready", "state_ready", "vn_done", "gmlp_mm", "oA_done",
        "glu_done", "cin_mm", "cin_done", "cln_done", "conv_done", "convT_mm", "oB_done", "rope_done", "qkT_mm", "qT_done",
        "lora_done", "lorT_mm", "lorT_done", "g_mm", "oC_done", "gelu_done", "bsig_done", "router_mm", "comb_done",
        "combT_mm", "combT_done", "route_max", "route_exp")},
    **{name: 2 for name in ("ssq_done", "mod_scale_done", "mrow_mm", "mrow_done")},
    "xn_done": 2 * NB, "hT_mm": 2 * KT, "hT_act": KT, "hT_dve": KT,
    "brT_mm": 4, "brT_done": 4,
    **{name: NB for name in ("scores_mm", "smax_done", "probs_done", "probsT_mm", "probsT_done", "att_mm", "att_done")},
    **{name: len(STEPS) for name in (
        "wa_mm", "wa_pre", "wa_done", "decay_mm", "exp_done", "tilde_done", "s0_done", "tildeT_mm", "tildeT_act", "tildeT_dve",
        "gramB_mm", "gramK_mm", "gb_done", "gk_done", "n_mm", "u_mm", "u_done", "sa_mm", "sa_done", "step_mm", "step_done")},
    **{name: len(STEPS) * (LEVELS - 1) for name in ("nl_ready", "x_mm", "xm_done", "y_mm")},
    "t_done": len(STEPS) * LEVELS,
    "var_ready": 5 + len(STEPS), "std_ready": 5 + len(STEPS),
    "slot_loaded": 16 * SLOTS // RING,
    **{name: MODS for name in ("mod_mm", "mod_rows", "modT_mm", "modc_done")},
    "gate_mm": 2 * PIECES, "sig_done": 2 * PIECES, "gates_kept": 16 * PIECES // STAGES,
    "z_mm": 2 * SLOTS_IN * NB, "z_act": SLOTS_IN * NB // 2, "z_dve": SLOTS_IN * NB // 2,
    "proj_mm": KT * 4, "mix_done": KT * 4,
    "wout_mm": SLOTS_OUT * NB, "xo_done": SLOTS_OUT * NB, "down_mm": SLOTS_DOWN, "x_done": 2 * NB,
    **{name: NE for name in ("cb_mm", "cb_done")},
    **{name: NE * 4 for name in ("egate_mm", "up_mm", "silu_done", "hid_done")},
    "params_loaded": 2 * 16, "x_kept": 16, "cache_out": 2 * 16, "state_stored": 16, "x_back": 16, "wb0_loaded": 16, "wb1_loaded": 16,
    "dve_chain": 291,
}


class Place:

    def __init__(self):
        self.layer, self.seen = 0, {}

    def value(self, name, k):
        return self.layer * PER[name] + k + (1 if name == "x_done" else 0)

    def next(self, name, n=1):
        self.seen[name] = self.seen.get(name, 0) + n
        return self.value(name, self.seen[name])

    def load(self, u):
        return self.layer * PER["slot_loaded"] + 16 * (u // RING + 1)


def build(nc, a):
    ctx = ExitStack()
    with ctx:
        def sb(name, cols, dt=F32):
            return ctx.enter_context(nc.sbuf_tensor(name, [P, cols], dt))

        def sem(name):
            return ctx.enter_context(nc.semaphore(name))

        slot_loaded = [sem(f"slot{u}_loaded") for u in range(RING)]
        att_done = sem("att_done")
        att_mm = sem("att_mm")
        brT_done = sem("brT_done")
        brT_mm = sem("brT_mm")
        bsig_done = sem("bsig_done")
        cache_out = sem("cache_out")
        cb_done = sem("cb_done")
        cb_mm = sem("cb_mm")
        cin_done = sem("cin_done")
        cin_mm = sem("cin_mm")
        cln_done = sem("cln_done")
        combT_done = sem("combT_done")
        combT_mm = sem("combT_mm")
        comb_done = sem("comb_done")
        convT_mm = sem("convT_mm")
        conv_done = sem("conv_done")
        decay_mm = sem("decay_mm")
        down_mm = sem("down_mm")
        dve_chain = sem("dve_chain")
        egate_mm = sem("egate_mm")
        exp_done = sem("exp_done")
        final_chain = sem("final_chain")
        final_done = sem("final_done")
        final_g_loaded = sem("final_g_loaded")
        final_std = sem("final_std")
        final_sums = sem("final_sums")
        final_var = sem("final_var")
        g_mm = sem("g_mm")
        gate_mm = sem("gate_mm")
        gates_kept = [sem(f"gates_kept{i}") for i in range(STAGES)]
        gb_done = sem("gb_done")
        gelu_done = sem("gelu_done")
        gk_done = sem("gk_done")
        glu_done = sem("glu_done")
        gmlp_mm = sem("gmlp_mm")
        gramB_mm = sem("gramB_mm")
        gramK_mm = sem("gramK_mm")
        hT_act = sem("hT_act")
        hT_dve = sem("hT_dve")
        hT_mm = sem("hT_mm")
        hid_done = sem("hid_done")
        keys_ready = sem("keys_ready")
        lorT_done = sem("lorT_done")
        lorT_mm = sem("lorT_mm")
        lora_done = sem("lora_done")
        mix_done = sem("mix_done")
        modT_mm = sem("modT_mm")
        mod_mm = sem("mod_mm")
        mod_rows = sem("mod_rows")
        mod_scale_done = sem("mod_scale_done")
        modc_done = sem("modc_done")
        mrow_done = sem("mrow_done")
        mrow_mm = sem("mrow_mm")
        n_mm = sem("n_mm")
        nl_ready = sem("nl_ready")
        oA_done = sem("oA_done")
        oB_done = sem("oB_done")
        oC_done = sem("oC_done")
        pads_zeroed = sem("pads_zeroed")
        params_loaded = sem("params_loaded")
        pool_chain = sem("pool_chain")
        probsT_done = sem("probsT_done")
        probsT_mm = sem("probsT_mm")
        probs_done = sem("probs_done")
        proj_mm = sem("proj_mm")
        qT_done = sem("qT_done")
        qkT_mm = sem("qkT_mm")
        rope_done = sem("rope_done")
        route_exp = sem("route_exp")
        route_max = sem("route_max")
        router_mm = sem("router_mm")
        s0_done = sem("s0_done")
        sa_done = sem("sa_done")
        sa_mm = sem("sa_mm")
        scan_ready = sem("scan_ready")
        scores_mm = sem("scores_mm")
        sig_done = sem("sig_done")
        silu_c_done = sem("silu_c_done")
        silu_done = sem("silu_done")
        smax_done = sem("smax_done")
        ssq_done = sem("ssq_done")
        start_loaded = sem("start_loaded")
        state_ready = sem("state_ready")
        state_stored = sem("state_stored")
        std_ready = sem("std_ready")
        step_done = sem("step_done")
        step_mm = sem("step_mm")
        t_done = sem("t_done")
        tildeT_act = sem("tildeT_act")
        tildeT_dve = sem("tildeT_dve")
        tildeT_mm = sem("tildeT_mm")
        tilde_done = sem("tilde_done")
        u_done = sem("u_done")
        u_mm = sem("u_mm")
        up_mm = sem("up_mm")
        var_ready = sem("var_ready")
        vn_done = sem("vn_done")
        wa_done = sem("wa_done")
        wa_mm = sem("wa_mm")
        wa_pre = sem("wa_pre")
        wb0_loaded = sem("wb0_loaded")
        wb1_loaded = sem("wb1_loaded")
        wout_mm = sem("wout_mm")
        x_back = sem("x_back")
        x_done = sem("x_done")
        x_kept = sem("x_kept")
        x_mm = sem("x_mm")
        xm_done = sem("xm_done")
        xn_done = sem("xn_done")
        xo_done = sem("xo_done")
        y_mm = sem("y_mm")
        y_stored = sem("y_stored")
        z_act = sem("z_act")
        z_dve = sem("z_dve")
        z_mm = sem("z_mm")
        waits_settled = sem("waits_settled")

        Xt = sb("x", NB * D)
        Ht = sb("h", KT * TOK)
        ring = sb("ring", RING * SLOT)
        arena = sb("arena", 20480)
        cols = sb("cols", NCOLS)
        rows = sb("rows", NROWS)
        fix = sb("fix", NFIX)
        scanf = sb("scan_sums", NSCANF)
        scanb = sb("scan_masks", NSCANB)
        mbc_t = sb("mod_rows", 2 * D)
        modc_t = sb("mod_cols", 96)
        sml = sb("small", 640)
        ps = ctx.enter_context(nc.psum_tensor("ps", [P, 4096], F32))

        x = Xt[:, :].rearrange("p (b d) -> p b d", b=NB)
        h = Ht[:, :].rearrange("p (k t) -> p k t", k=KT)

        def bank(b, n=512):
            return ps[:, b * 512:b * 512 + n]

        def col(name):
            o, n = COLS[name]
            return cols[:, o:o + n]

        def row(name):
            o, n = ROWS[name]
            return rows[:, o:o + n]

        def fixed(name):
            o, n = FIX[name]
            return fix[:, o:o + n]

        ident = fixed("ident")

        zab = arena[:, 0:NB * 1024].rearrange("p (b c) -> p b c", b=NB)
        zc = arena[:, 5120:5120 + NB * 768].rearrange("p (b c) -> p b c", b=NB)
        zl = arena[:, 8960:8960 + NB * 384].rearrange("p (b c) -> p b c", b=NB)
        lorT = arena[:, 8960:8960 + 3 * TOK].rearrange("p (g t) -> p g t", g=3)
        zd = arena[:, 10880:10880 + NB * 512].rearrange("p (b c) -> p b c", b=NB)
        brT = arena[:, 13440:13440 + 8 * TOK].rearrange("p (k t) -> p k t", k=8)
        stage = arena[:, 18560:18560 + STAGES * HALF].rearrange("p (i t) -> p i t", i=STAGES)
        xn = arena[:, 0:NB * D].rearrange("p (b d) -> p b d", b=NB)
        wb = arena[:, 0:8192].rearrange("p (f n k c) -> p f n k c", f=KT, n=4, k=2)
        mixT = arena[:, 8192:8192 + KT * TOK].rearrange("p (k t) -> p k t", k=KT)
        hid = arena[:, :].rearrange("p (k t) -> p k t", k=32)
        cin = [Xt[:, f * LINE:(f + 1) * LINE] for f in range(FT)]
        cacc = [Xt[:, 1400 + f * OUTS:1400 + (f + 1) * OUTS] for f in range(FT)]
        qkr = Xt[:, 0:NB * 384].rearrange("p (b c) -> p b c", b=NB)
        qT = Xt[:, 1920:1920 + 2 * TOK].rearrange("p (g t) -> p g t", g=2)
        kTz = Xt[:, 3200:3200 + 2 * (P + TOK)].rearrange("p (g t) -> p g t", g=2)
        sc = arena[:, 0:2048].rearrange("p (h s) -> p h s", h=4)
        pT = arena[:, 2048:4096].rearrange("p (s h q) -> p s h q", s=4, h=4)
        ropet = mbc_t[:, 0:LAT * 384].rearrange("p (b c) -> p b c", b=LAT)
        gb = Xt[:, 0:2048].rearrange("p (g e t) -> p g e t", g=8, e=2)
        gk = Xt[:, 2048:4096].rearrange("p (g e t) -> p g e t", g=8, e=2)
        nl = Xt[:, 4096:5120].rearrange("p (g t) -> p g t", g=8)
        Tm = arena[:, 0:1024].rearrange("p (g t) -> p g t", g=8)
        TT = arena[:, 1024:2048].rearrange("p (g t) -> p g t", g=8)
        Xm = arena[:, 2048:3072].rearrange("p (g t) -> p g t", g=8)
        ar = arena[:, 3072:5120].rearrange("p (g r e t) -> p g r e t", g=4, r=2, e=2)
        bT = arena[:, 10880:10880 + 512].rearrange("p (g t) -> p g t", g=4)
        kT = arena[:, 11392:11392 + 512].rearrange("p (g t) -> p g t", g=4)
        sw = arena[:, 11904:11904 + 512].rearrange("p (d c) -> p d c", d=2)
        aa = arena[:, 12416:12416 + 512].rearrange("p (d c) -> p d c", d=2)
        kks = arena[:, 12928:12928 + 512].rearrange("p (d c) -> p d c", d=2)
        rt = mbc_t[:, 0:512].rearrange("p (d c) -> p d c", d=2)
        at_ = mbc_t[:, 512:1024].rearrange("p (d c) -> p d c", d=2)
        bt = mbc_t[:, 1024:1536].rearrange("p (d c) -> p d c", d=2)
        kt_ = mbc_t[:, 1536:2048].rearrange("p (d c) -> p d c", d=2)
        ub = nl[:, 0:4, :].rearrange("p a t -> p (a t)").rearrange("p (g v) -> p g v", g=8)
        sa = nl[:, 4:8, :].rearrange("p a t -> p (a t)").rearrange("p (g v) -> p g v", g=8)
        y = brT[:, 4:6, :].rearrange("p k t -> p (k t)").rearrange("p (b c) -> p b c", b=NB)
        sil = mbc_t[:, 0:640].rearrange("p (i t) -> p i t", i=2)
        cbs = mbc_t[:, 640:640 + 1280].rearrange("p (i t) -> p i t", i=2)
        mrow = mbc_t[:, :].rearrange("p (g d) -> p g d", g=2)
        modc = modc_t[:, :].rearrange("p (j g) -> p j g", g=2)

        off = [0]

        def small(n):
            off[0] += n
            assert off[0] <= 640
            return sml[:, off[0] - n:off[0]]

        cS = small(16).rearrange("p (k g) -> p k g", g=2)
        A1 = small(16).rearrange("p (k g) -> p k g", g=2)
        ssq, rstd = small(NB), small(NB)
        stats, mv = small(NB * 6), small(NB * 2)
        mx, smx, rsm, snk = small(4), small(4), small(4), small(4)
        kss = small(8)
        bon = small(NB * 8).rearrange("p (b d h) -> p b d h", b=NB, d=2)
        S = sb("scan_state", 256)[:, :].rearrange("p (g v) -> p g v", g=4)
        S0 = sb("scan_state_scaled", 256)[:, :].rearrange("p (g v) -> p g v", g=4)
        gm = small(8).rearrange("p (g e) -> p g e", g=4)
        gst = small(20)
        gs2 = small(20)
        lg = small(100).rearrange("p (b e) -> p b e", b=NB)
        t20 = small(20).rearrange("p (b e) -> p b e", b=NB)
        gsel = small(20).rearrange("p (b e) -> p b e", b=NB)
        t16 = small(80).rearrange("p (b g e) -> p b g e", b=NB, g=4)
        ein = small(20).rearrange("p (b e) -> p b e", b=NB)
        oh1 = small(20).rearrange("p (b e) -> p b e", b=NB)
        oh2 = small(20).rearrange("p (b e) -> p b e", b=NB)
        m1, m2_, gw, ix = small(NB), small(NB), small(NB), small(NB)
        comb = arena[:, 5120:5120 + NB * P].rearrange("p (b e) -> p b e", b=NB)
        combT_t = sb("combT", TOK)
        combT = combT_t[:, :]

        state_out = sb("scan_state_out", 256)[:, :].rearrange("p (g v) -> p g v", g=4)
        mod_row = combT_t[0:2, 0:512]
        gates_dram = nc.dram_tensor("gates", [KT, P, 4 * TOK], F32, kind="Internal").ap()
        x_kept_dram = nc.dram_tensor("x_kept", [P, NB * D], F32, kind="Internal").ap()

        def slot(u):
            return ring[:, (u % RING) * SLOT:(u % RING + 1) * SLOT].rearrange("p (k c) -> p k c", k=KT)

        def over(ap, at, n):
            v = ap.unsqueeze(at)
            return v.broadcast_to([n if i == at else c for i, c in enumerate(v.shape)])

        block = ctx.enter_context(nc.Block())

        def z_copies(g, copy):
            j, b = g // NB, g % NB
            parts = {0: [(0, 512, zab, 0)], 1: [(0, 512, zab, 512)], 2: [(0, 512, zc, 0)],
                     3: [(0, 256, zc, 512), (256, 256, zl, 0)], 4: [(0, 128, zl, 256), (128, 384, zd, 0)],
                     5: [(0, 128, zd, 384)]}[j]
            for at, n, dst, to in parts:
                ins = copy(dst[:, b, to:to + n], bank(g % 8)[:, at:at + n])
            return ins

        @block.sync
        def _(sp):
            now = Place()

            def load(u):
                if AT_BACK <= u < AT_OUT:
                    return sp.dma_start(ring[:, (u % RING) * SLOT:(u % RING) * SLOT + 4 * TOK], gates_dram[u - AT_BACK])
                at = u if u < AT_BACK else u - SLOTS_BACK
                src = a["stream"][bass.ds(now.layer * (SLOTS - SLOTS_BACK) + at, 1)].rearrange("o p c -> (o p) c")
                return sp.dma_start(ring[:, (u % RING) * SLOT:(u % RING + 1) * SLOT], src)

            for u in range(RING):
                load(u).then_inc(slot_loaded[u], 16)
            with sp.Fori(0, DEPTH) as layer:
                now.layer = layer
                u = RING
                for _ in range(SLOTS_MOD):
                    sp.wait_ge(mod_mm, now.next("mod_mm"))
                    load(u).then_inc(slot_loaded[u % RING], 16)
                    u += 1
                for _ in range(SLOTS_IN):
                    sp.wait_ge(z_mm, now.next("z_mm", 2 * NB))
                    load(u).then_inc(slot_loaded[u % RING], 16)
                    u += 1
                for f in range(KT):
                    sp.wait_ge(mod_mm, now.next("mod_mm"))
                    load(u).then_inc(slot_loaded[u % RING], 16)
                    u += 1
                    for i in range(8 * f, 8 * f + 8):
                        sp.wait_ge(sig_done, now.next("sig_done", 2))
                        at = i % 8 * HALF
                        sp.dma_start(gates_dram[f, :, at:at + HALF], stage[:, i % STAGES]).then_inc(gates_kept[i % STAGES], 16)
                    if u >= AT_BACK:
                        for i in range(STAGES):
                            sp.wait_ge(gates_kept[i], now.value("gates_kept", 16 * 2 * (u - AT_BACK + 1)))
                            sp.sem_inc(waits_settled, 1)
                    load(u).then_inc(slot_loaded[u % RING], 16)
                    u += 1
                for f in range(KT):
                    sp.wait_ge(mix_done, now.next("mix_done", 4))
                    sp.sem_inc(waits_settled, 1)
                    if u < AT_OUT:
                        for i in range(STAGES):
                            sp.wait_ge(gates_kept[i], now.value("gates_kept", 16 * 2 * (u - AT_BACK + 1)))
                            sp.sem_inc(waits_settled, 1)
                    load(u).then_inc(slot_loaded[u % RING], 16)
                    u += 1
                for _ in range(SLOTS_OUT):
                    sp.wait_ge(wout_mm, now.next("wout_mm", NB))
                    load(u).then_inc(slot_loaded[u % RING], 16)
                    u += 1
                for _ in range(SLOTS_UP):
                    sp.wait_ge(up_mm, now.next("up_mm", 4))
                    load(u).then_inc(slot_loaded[u % RING], 16)
                    u += 1
                for _ in range(SLOTS_DOWN):
                    sp.wait_ge(down_mm, now.next("down_mm"))
                    load(u).then_inc(slot_loaded[u % RING], 16)
                    u += 1
            for u in range(RING):
                sp.wait_ge(slot_loaded[u], 16 * (DEPTH * SLOTS // RING + 1))

        @block.gpsimd
        def _(pool):
            now = Place()
            pool.dma_start(fix[:, :], a["fix"]).then_inc(start_loaded, 16)
            pool.dma_start(scanf[:, :], a["scanf"]).then_inc(start_loaded, 16)
            pool.dma_start(scanb[:, :], a["scanb"]).then_inc(start_loaded, 16)
            pool.dma_start(Xt[:, :], a["x"]).then_inc(start_loaded, 16)
            pool.dma_start(sml[:, 0:16], a["c"]).then_inc(start_loaded, 16)
            with pool.Fori(0, DEPTH) as layer:
                now.layer = layer
                pool.wait_ge(x_done, now.value("x_done", 0))
                pick = bass.ds(layer, 1)
                pool.sem_inc(waits_settled, 1)
                pool.dma_start(cols[:, :], a["cols"][pick].rearrange("o p c -> (o p) c")).then_inc(params_loaded, 16)
                pool.dma_start(rows[:, :], a["rows"][pick].rearrange("o p c -> (o p) c").broadcast_to([P, NROWS])).then_inc(params_loaded, 16)
                pool.wait_ge(x_kept, now.next("x_kept", 16))
                pool.wait_ge(xn_done, now.value("xn_done", NB))
                pool.sem_inc(waits_settled, 1)
                for f in range(FT):
                    for at, n in ((0, PAD), (PAD + P, PAD), (LINE - PAD, PAD)):
                        ins = nc.gpsimd.memset(cin[f][:, at:at + n], 0.0)
                ins.then_inc(pads_zeroed, 1)
                pool.sem_inc(waits_settled, 1)
                nc.gpsimd.memset(kTz, 0.0).then_inc(pool_chain, 1)
                pool.wait_ge(pool_chain, now.next("pool_chain"))
                pool.wait_ge(params_loaded, now.next("params_loaded", 32))
                pool.sem_inc(waits_settled, 1)
                nc.gpsimd.tensor_copy(kTz[0:64, 0, 0:P], col("ckT")[0:64, :])
                nc.gpsimd.tensor_copy(kTz[64:128, 1, 0:P], col("ckT")[64:128, :]).then_inc(keys_ready, 1)
                pool.wait_ge(z_act, now.next("z_act", 15))
                pool.wait_ge(z_dve, now.next("z_dve", 15))
                pool.sem_inc(waits_settled, 1)
                pool.dma_start(a["new_k"][pick].rearrange("o p c -> (o p) c"), zd[:, 0, 256:384]).then_inc(cache_out, 16)
                pool.dma_start(a["new_v"][pick].rearrange("o p c -> (o p) c"), zd[:, 0, 384:512]).then_inc(cache_out, 16)
                pool.wait_ge(cache_out, now.next("cache_out", 32))
                pool.wait_ge(brT_done, now.next("brT_done", 3))
                pool.sem_inc(waits_settled, 1)
                nc.gpsimd.memset(ar[0:64, :, 1], 0.0)
                nc.gpsimd.memset(ar[64:128, :, 0], 0.0).then_inc(scan_ready, 1)
                for s, blocks in enumerate(STEPS):
                    pool.wait_ge(gb_done, now.next("gb_done"))
                    for lev in range(LEVELS - 1):
                        if lev:
                            pool.wait_ge(x_mm, now.next("x_mm"))
                        for d in range(2):
                            o = SCANB["lev"][0] + (lev * 2 + d) * P
                            ins = nc.gpsimd.tensor_tensor(nl[:, 4 * d:4 * d + 4], gb[:, 4 * d:4 * d + 4, 0, :],
                                                          over(scanb[:, o:o + P], 1, 4), ALU.mult)
                        ins.then_inc(nl_ready, 1)
                    pool.wait_ge(x_mm, now.next("x_mm"))
                    if s == 0:
                        pool.wait_ge(state_ready, now.next("state_ready"))
                        pool.sem_inc(waits_settled, 1)
                        pool.dma_start(a["new_s"][pick].rearrange("o p c -> (o p) c"),
                                                            state_out.rearrange("p g v -> p (g v)")).then_inc(state_stored, 16)
                        pool.wait_ge(state_stored, now.next("state_stored", 16))
                pool.wait_ge(brT_done, now.next("brT_done"))
                pool.sem_inc(waits_settled, 1)
                wbranch = a["wbranch"][pick].rearrange("o p c -> (o p) c")
                pool.dma_start(arena[:, 0:1024], wbranch[:, 0:1024]).then_inc(wb0_loaded, 16)
                pool.dma_start(arena[:, 1024:8192], wbranch[:, 1024:8192]).then_inc(wb1_loaded, 16)
                pool.dma_start(Xt[:, :], x_kept_dram).then_inc(x_back, 16)
            pool.wait_ge(x_done, 1 + DEPTH * PER["x_done"])
            pool.dma_start(arena[:, 10240:10240 + D], a["final_g"].broadcast_to([P, D])).then_inc(final_g_loaded, 16)
            pool.wait_ge(final_done, 1)
            yv = arena[:, 0:NB * D].rearrange("p (b d) -> p b d", b=NB)
            pool.dma_start(a["y_prompt"], yv[:, 0]).then_inc(y_stored, 16)
            pool.dma_start(a["y_sample"].rearrange("(b p) d -> p b d", p=P), yv[:, 1:NB]).then_inc(y_stored, 16)
            pool.wait_ge(y_stored, 32)

        @block.tensor
        def _(pe):
            now = Place()

            def mm(out, lhsT, rhs, start=True, stop=True):
                return nc.tensor.matmul(out, lhsT, rhs, start=start, stop=stop)

            def transpose(out, in_):
                return nc.tensor.transpose(out, in_, ident)

            def h_transposes():
                pe.wait_ge(xn_done, now.next("xn_done", NB))
                for f in range(KT):
                    if f >= 4:
                        if f % 2 == 0:
                            pe.wait_ge(hT_act, now.next("hT_act"))
                        else:
                            pe.wait_ge(hT_dve, now.next("hT_dve"))
                    for b in range(NB):
                        ins = transpose(ps[:, 1024 * (f % 4) + b * P:1024 * (f % 4) + (b + 1) * P], xn[:, b, f * P:(f + 1) * P])
                    ins.then_inc(hT_mm, 1)
                pe.wait_ge(hT_act, now.next("hT_act", 2))
                pe.wait_ge(hT_dve, now.next("hT_dve", 2))

            def branch_transposes(src):
                for f in range(FT):
                    for b in range(NB):
                        ins = transpose(ps[:, 2048 + 1024 * f + b * P:2048 + 1024 * f + (b + 1) * P], src[:, b, f * P:(f + 1) * P])
                ins.then_inc(brT_mm, 1)

            def mod_row_products(j0):
                for g in range(2):
                    for f in range(KT):
                        ins = mm(ps[:, 2048 + g * D + f * P:2048 + g * D + (f + 1) * P],
                                 modc[:, j0 + f, g:g + 1].broadcast_to([P, P]), ident)
                ins.then_inc(mrow_mm, 1)

            def mod_rows_products(i, u, bk, ks):
                for k in ks:
                    ins = mm(bank(bk)[0:2, :], cS[:, k, :], slot(u)[:, k, :], k == 0, k == KT - 1)
                return ins

            def mod_columns(i, bk):
                pe.wait_ge(mod_rows, now.value("mod_rows", i + 1))
                for j in range(4):
                    ins = mm(bank(bk)[:, 2 * j:2 * j + 2], mod_row[:, j * P:(j + 1) * P], ident[0:2, 0:2])
                ins.then_inc(modT_mm, 1)

            def bank_left(what, i):
                if what == "rows":
                    pe.wait_ge(sig_done, now.value("sig_done", 2 * (8 * (i - SLOTS_MOD) - 1)))
                elif i % 8 == 1:
                    pe.wait_ge(modc_done, now.value("modc_done", SLOTS_MOD + i // 8 + 1))
                elif i >= 2:
                    pe.wait_ge(sig_done, now.value("sig_done", 2 * (i - 1)))

            def behind(lo, hi):
                for what, i, part, bk in PARTS[lo:hi]:
                    ks = range(4 * part, 4 * part + 4)
                    if what == "cols":
                        mod_columns(i, bk)
                        continue
                    f = i - SLOTS_MOD if what == "rows" else i // 8
                    u = AT_BEHIND + 2 * f + (what == "gate")
                    if part == 0:
                        pe.wait_ge(slot_loaded[u % RING], now.load(u))
                        if (what, i) != ("rows", SLOTS_MOD):
                            bank_left(what, i)
                    if what == "rows":
                        ins = mod_rows_products(i, u, bk, ks)
                        if part:
                            ins.then_inc(mod_mm, 1)
                    else:
                        n, at = i % 8 // 2, i % 2 * HALF
                        for k in ks:
                            ins = mm(bank(bk, HALF), slot(u)[:, k, n * P:(n + 1) * P], h[:, k, at:at + HALF], k == 0, k == KT - 1)
                        ins.then_inc(gate_mm, 1)

            pe.wait_ge(silu_c_done, 1)
            with pe.Fori(0, DEPTH) as layer:
                now.layer = layer
                pe.wait_ge(x_done, now.value("x_done", 0))
                pe.wait_ge(slot_loaded[0], now.load(0))
                mod_rows_products(0, 0, 4, range(KT)).then_inc(mod_mm, 1)
                for i in range(1, SLOTS_MOD):
                    pe.wait_ge(slot_loaded[i % RING], now.load(i))
                    mod_rows_products(i, i, 4 + i, range(KT)).then_inc(mod_mm, 1)
                    mod_columns(i - 1, 3 + i)
                mod_columns(SLOTS_MOD - 1, 3 + SLOTS_MOD)
                pe.wait_ge(modc_done, now.value("modc_done", SLOTS_MOD))
                h_transposes()
                for j in range(SLOTS_IN):
                    u = AT_IN + j
                    n = 512 if j < SLOTS_IN - 1 else P
                    pe.wait_ge(slot_loaded[(u) % RING], now.load(u))
                    for b in range(NB):
                        g = j * NB + b
                        if g >= 8:
                            if g % 2 == 0:
                                pe.wait_ge(z_act, now.next("z_act"))
                            else:
                                pe.wait_ge(z_dve, now.next("z_dve"))
                        for k in range(KT):
                            ins = mm(bank(g % 8, n), h[:, k, b * P:(b + 1) * P], slot(u)[:, k, 0:n], k == 0, k == KT - 1)
                        ins.then_inc(z_mm, 2)
                pe.wait_ge(z_act, now.next("z_act", 4))
                pe.wait_ge(z_dve, now.next("z_dve", 4))
                pe.wait_ge(vn_done, now.next("vn_done"))
                wsT = col("wsT").rearrange("p (g t) -> p g t", g=4)
                for g in range(4):
                    ins = mm(bank(g, NB * HD).rearrange("p (b c) -> p b c", b=NB), wsT[:, g], zab[:, :, 256 + g * HD:256 + (g + 1) * HD])
                ins.then_inc(gmlp_mm, 1)
                pe.wait_ge(oA_done, now.next("oA_done"))
                branch_transposes(zab[:, :, 0:256])
                pe.wait_ge(glu_done, now.next("glu_done"))
                for f in range(FT):
                    for b in range(NB):
                        ins = transpose(ps[:, 1024 * f + b * P:1024 * f + (b + 1) * P], zab[:, b, 512 + f * P:512 + (f + 1) * P])
                ins.then_inc(cin_mm, 1)
                pe.wait_ge(brT_done, now.next("brT_done"))
                behind(0, CONV_PARTS)
                pe.wait_ge(conv_done, now.next("conv_done"))
                for b in range(NB):
                    at = 0 if b == 0 else LAT_OUT + (b - 1) * P
                    for f in range(FT):
                        ins = transpose(ps[:, b * W + f * P:b * W + (f + 1) * P], cacc[f][:, at:at + P])
                ins.then_inc(convT_mm, 1)
                pe.wait_ge(oB_done, now.next("oB_done"))
                pe.wait_ge(sig_done, now.value("sig_done", 2 * 8))
                pe.wait_ge(modc_done, now.value("modc_done", SLOTS_MOD + 2))
                branch_transposes(zab[:, :, 512:768])
                pe.wait_ge(rope_done, now.next("rope_done"))
                pe.wait_ge(brT_done, now.next("brT_done"))
                for g in range(3):
                    for b in range(NB):
                        src = zd[:, 0] if b == 0 else qkr[:, b]
                        ins = transpose(ps[:, 1024 * g + b * P:1024 * g + (b + 1) * P], src[:, g * P:(g + 1) * P])
                ins.then_inc(qkT_mm, 1)
                pe.wait_ge(qT_done, now.next("qT_done"))
                for b in range(NB):
                    lo, hi = (0, 0) if b == 0 else (max(1, b - 1), min(LAT, b + 1))
                    nband = (hi - lo + 1) * P
                    segs = ([] if b == 0 else [None]) + list(range(lo, hi + 1))
                    for hd in range(4):
                        q = qT[:, hd % 2, b * P:(b + 1) * P]
                        o = 0 if b == 0 else P
                        if b:
                            mm(bank(hd)[:, 0:P], q, kTz[:, hd // 2, 0:P])
                        ins = mm(bank(hd)[:, o:o + nband], q, kTz[:, hd // 2, P + lo * P:P + lo * P + nband])
                    ins.then_inc(scores_mm, 1)
                    pe.wait_ge(probs_done, now.next("probs_done"))
                    for s in range(len(segs)):
                        for hd in range(4):
                            ins = transpose(bank(4 + s)[:, hd * P:(hd + 1) * P], sc[:, hd, s * P:(s + 1) * P])
                    ins.then_inc(probsT_mm, 1)
                    pe.wait_ge(probsT_done, now.next("probsT_done"))
                    for hd in range(4):
                        for s, blk in enumerate(segs):
                            kv = hd // 2
                            v = col("cv")[:, kv * HD:(kv + 1) * HD] if blk is None else zd[:, blk, 384 + kv * HD:384 + (kv + 1) * HD]
                            ins = mm(ps[:, hd * HD:(hd + 1) * HD], pT[:, s, hd, :], v, s == 0, s == len(segs) - 1)
                    ins.then_inc(att_mm, 1)
                    pe.wait_ge(att_done, now.next("att_done"))
                branch_transposes(zd[:, :, 0:256])
                pe.wait_ge(lora_done, now.next("lora_done"))
                pe.wait_ge(brT_done, now.next("brT_done"))
                for g in range(3):
                    for b in range(NB):
                        ins = transpose(ps[:, 1024 * g + b * P:1024 * g + (b + 1) * P], zl[:, b, g * P:(g + 1) * P])
                ins.then_inc(lorT_mm, 1)
                pe.wait_ge(lorT_done, now.next("lorT_done"))
                pe.wait_ge(scan_ready, now.next("scan_ready"))
                for s, blocks in enumerate(STEPS):
                    part = CONV_PARTS + s * STEP_PARTS
                    for i, w in enumerate(("w2", "a2")):
                        for d, blk in enumerate(blocks):
                            ins = mm(bank(i)[:, d * W:(d + 1) * W], lorT[:, i, blk * P:(blk + 1) * P], col(w)[:, d * W:(d + 1) * W])
                    ins.then_inc(wa_mm, 1)
                    behind(part, part + 2)
                    pe.wait_ge(wa_done, now.next("wa_done"))
                    for i, name in enumerate(("incl", "excl")):
                        for d in range(2):
                            o = SCANF[name][0] + d * P
                            mm(bank(2 + i)[:, d * W:(d + 1) * W], scanf[:, o:o + P], sw[:, d, :])
                    o = SCANF["halves"][0]
                    for g in range(4):
                        ins = mm(bank(4)[:, 2 * g:2 * g + 2], sw[:, g // 2, (g % 2) * P:(g % 2 + 1) * P], scanf[:, o:o + 2])
                    ins.then_inc(decay_mm, 1)
                    behind(part + 2, part + 10)
                    pe.wait_ge(tilde_done, now.next("tilde_done"))
                    for i, src in enumerate((at_, rt, bt, kt_)):
                        for g in range(4):
                            ins = transpose(bank(i)[:, g * P:(g + 1) * P], src[:, g // 2, (g % 2) * P:(g % 2 + 1) * P])
                    ins.then_inc(tildeT_mm, 1)
                    behind(part + 10, closed(part + 12))
                    pe.wait_ge(tildeT_act, now.next("tildeT_act"))
                    pe.wait_ge(tildeT_dve, now.next("tildeT_dve"))
                    for half, src, made in ((0, bT, gramB_mm), (2048, kT, gramK_mm)):
                        if made is gramK_mm:
                            pe.wait_ge(sig_done, now.value("sig_done", 2 * counted("gate", closed(part + 12))))
                            pe.wait_ge(mod_rows, now.value("mod_rows", SLOTS_MOD + counted("rows", closed(part + 12))))
                            pe.wait_ge(modc_done, now.value("modc_done", SLOTS_MOD + counted("cols", closed(part + 12))))
                        for g in range(4):
                            for par in range(2):
                                o = half + (2 * g + par) * 256
                                ins = mm(ps[:, o:o + 256].rearrange("p (e t) -> p e t", e=2), src[:, g], ar[:, g, par])
                        ins.then_inc(made, 1)
                    pe.wait_ge(gb_done, now.next("gb_done"))
                    for g in range(4):
                        for par in range(2):
                            o = (2 * g + par) * P
                            ins = mm(ps[:, o:o + P], ar[:, g, par, 0, :], bT[:, g])
                    ins.then_inc(n_mm, 1)
                    pe.wait_ge(gk_done, now.next("gk_done"))
                    behind(closed(part + 12), part + 14)
                    for lev in range(LEVELS - 1):
                        pe.wait_ge(t_done, now.next("t_done"))
                        pe.wait_ge(nl_ready, now.next("nl_ready"))
                        for g in range(8):
                            ins = mm(ps[:, g * P:(g + 1) * P], nl[:, g], Tm[:, g])
                        ins.then_inc(x_mm, 1)
                        behind(part + 14 + 2 * lev, part + 15 + 2 * lev)
                        pe.wait_ge(xm_done, now.next("xm_done"))
                        if lev < LEVELS - 2:
                            for g in range(8):
                                mm(ps[:, 1024 + g * P:1024 + (g + 1) * P], TT[:, g], Xm[:, g])
                        for g in range(8):
                            ins = mm(ps[:, 2048 + g * P:2048 + (g + 1) * P], Xm[:, g], TT[:, g])
                        ins.then_inc(y_mm, 1)
                        behind(part + 15 + 2 * lev, part + 16 + 2 * lev)
                    pe.wait_ge(t_done, now.next("t_done"))
                    pe.wait_ge(s0_done, now.next("s0_done"))

                    def v_of(g8):
                        hd = g8 % 4
                        return zc[:, blocks[g8 // 4], 512 + hd * HD:512 + (hd + 1) * HD]

                    for g in range(8):
                        mm(bank(2)[:, g * HD:(g + 1) * HD], ar[:, g // 2, g % 2, 0, :], S0[:, g // 2], True, False)
                        ins = mm(bank(2)[:, g * HD:(g + 1) * HD], gk[:, g, 0, :], v_of(g), False, True)
                    ins.then_inc(u_mm, 1)
                    pe.wait_ge(u_done, now.next("u_done"))
                    for g in range(8):
                        ins = mm(bank(3)[:, g * HD:(g + 1) * HD], TT[:, g], ub[:, g])
                    ins.then_inc(sa_mm, 1)
                    pe.wait_ge(sa_done, now.next("sa_done"))
                    for g in range(8):
                        o = bank(0)[:, g * HD:(g + 1) * HD]
                        mm(o, ar[:, g // 2, g % 2, 1, :], S0[:, g // 2], True, False)
                        mm(o, gb[:, g, 1, :], sa[:, g], False, False)
                        mm(o, gk[:, g, 1, :], v_of(g), False, True)
                    for g in range(8):
                        d, par, hd = g // 4, g % 2, g % 4
                        o = ps[par * 64:(par + 1) * 64, 512 + (g // 2) * HD:512 + (g // 2 + 1) * HD]
                        mm(o, bt[:, d, hd * HD:(hd + 1) * HD], sa[:, g], True, False)
                        ins = mm(o, kt_[:, d, hd * HD:(hd + 1) * HD], v_of(g), False, True)
                    ins.then_inc(step_mm, 1)
                    pe.wait_ge(step_done, now.next("step_done"))
                for b in range(NB):
                    ins = mm(ps[:, b * W:(b + 1) * W], lorT[:, 2, b * P:(b + 1) * P], col("g2"))
                ins.then_inc(g_mm, 1)
                pe.wait_ge(oC_done, now.next("oC_done"))
                pe.wait_ge(sig_done, now.value("sig_done", 2 * PIECES))
                pe.wait_ge(modc_done, now.value("modc_done", MODS))
                branch_transposes(y)
                pe.wait_ge(brT_done, now.next("brT_done"))
                mod_row_products(2 * KT)
                pe.wait_ge(wb0_loaded, now.next("wb0_loaded", 16))
                for f in range(KT):
                    if f == 1:
                        pe.wait_ge(wb1_loaded, now.next("wb1_loaded", 16))
                    for n in range(4):
                        unit = 4 * f + n
                        if unit == 2:
                            pe.wait_ge(mrow_done, now.next("mrow_done"))
                        if unit >= 4:
                            pe.wait_ge(mix_done, now.next("mix_done"))
                        o = 1024 * (unit % 4)
                        for k in range(FT):
                            for lo, hi in ((0, 512), (512, TOK)):
                                ins = mm(ps[:, o + lo:o + hi], wb[:, f, n, k, :], brT[:, 2 * n + k, lo:hi], k == 0, k == FT - 1)
                        ins.then_inc(proj_mm, 1)
                pe.wait_ge(mix_done, now.next("mix_done", 4))
                for c in range(SLOTS_OUT):
                    pe.wait_ge(slot_loaded[(AT_OUT + c) % RING], now.load(AT_OUT + c))
                    for b in range(NB):
                        g = c * NB + b
                        if g >= 8:
                            pe.wait_ge(xo_done, now.next("xo_done"))
                        for k in range(KT):
                            ins = mm(bank(g % 8), mixT[:, k, b * P:(b + 1) * P], slot(AT_OUT + c)[:, k, :], k == 0, k == KT - 1)
                        ins.then_inc(wout_mm, 1)
                pe.wait_ge(xo_done, now.next("xo_done", 8))
                h_transposes()
                router = col("router").rearrange("p (k e) -> p k e", k=KT)
                for b in range(NB):
                    for k in range(KT):
                        ins = mm(ps[:, b * 20:(b + 1) * 20], h[:, k, b * P:(b + 1) * P], router[:, k, :], k == 0, k == KT - 1)
                ins.then_inc(router_mm, 1)
                pe.wait_ge(comb_done, now.next("comb_done"))
                for b in range(NB):
                    ins = transpose(ps[:, 1024 + b * P:1024 + (b + 1) * P], comb[:, b, :])
                ins.then_inc(combT_mm, 1)
                pe.wait_ge(combT_done, now.next("combT_done"))
                for e in range(NE):
                    if e:
                        pe.wait_ge(cb_done, now.next("cb_done"))
                    for lo, hi in ((0, 512), (512, TOK)):
                        ins = mm(ps[:, 3072 + lo:3072 + hi], ident[:, e:e + 1].broadcast_to([P, P]), combT[:, lo:hi])
                    ins.then_inc(cb_mm, 1)
                    pe.wait_ge(slot_loaded[(AT_UP + e) % RING], now.load(AT_UP + e))
                    w = slot(AT_UP + e)
                    for f in range(2):
                        for hf in range(2):
                            unit = 4 * e + 2 * f + hf
                            if unit >= 3:
                                pe.wait_ge(hid_done, now.next("hid_done"))
                            for i, made in enumerate((egate_mm, up_mm)):
                                for k in range(KT):
                                    ins = mm(bank(2 * (unit % 3) + i, 320), w[:, k, i * FF + f * P:i * FF + (f + 1) * P],
                                             h[:, k, hf * 320:(hf + 1) * 320], k == 0, k == KT - 1)
                                ins.then_inc(made, 1)
                pe.wait_ge(hid_done, now.next("hid_done", 3))
                pe.wait_ge(cb_done, now.next("cb_done"))
                mod_row_products(5 * KT)
                pe.wait_ge(mrow_done, now.next("mrow_done"))
                for c in range(2):
                    if c:
                        pe.wait_ge(x_done, now.next("x_done", 2))
                    for s4 in range(4):
                        u = AT_DOWN + 4 * c + s4
                        pe.wait_ge(slot_loaded[(u) % RING], now.load(u))
                        for k in range(KT):
                            kt = s4 * KT + k
                            for b in range(NB):
                                ins = mm(bank((c * NB + b) % 8), hid[:, kt, b * P:(b + 1) * P], slot(u)[:, k, :],
                                         kt == 0, kt == 31)
                        ins.then_inc(down_mm, 1)

        @block.scalar
        def _(act):
            now = Place()
            A = nc.scalar.activation

            def squares():
                for b in range(NB):
                    ins = A(xn[:, b, :], x[:, b, :], ACT.Square, accum_out=ssq[:, b:b + 1])
                ins.then_inc(ssq_done, 1)

            def root(ap):
                act.wait_ge(var_ready, now.next("var_ready"))
                A(ap, ap, ACT.Sqrt).then_inc(std_ready, 1)

            def h_scaled(b_at):
                for f in range(0, KT, 2):
                    act.wait_ge(hT_mm, now.next("hT_mm"))
                    if f == 0:
                        act.wait_ge(mod_scale_done, now.next("mod_scale_done"))
                    o = 1024 * (f % 4)
                    A(h[:, f, 0:P], ps[:, o:o + P], ACT.Identity, bias=modc[:, b_at + f, 0:1], scale=A1[:, f, 0:1])
                    A(h[:, f, P:TOK], ps[:, o + P:o + TOK], ACT.Identity, bias=modc[:, b_at + f, 1:2],
                                     scale=A1[:, f, 1:2]).then_inc(hT_act, 1)
                    act.wait_ge(hT_mm, now.next("hT_mm"))

            def branch_out(n):
                act.wait_ge(brT_mm, now.next("brT_mm"))
                for f in range(FT):
                    ins = nc.scalar.copy(brT[:, 2 * n + f, :], ps[:, 2048 + 1024 * f:2048 + 1024 * f + TOK])
                ins.then_inc(brT_done, 1)

            def mod_row_out(i, bk):
                act.wait_ge(mod_mm, now.value("mod_mm", i + 1))
                nc.scalar.copy(mod_row, bank(bk)[0:2, :]).then_inc(mod_rows, 1)

            def mod_column_out(i, bk):
                act.wait_ge(modT_mm, now.value("modT_mm", i + 1))
                for j in range(4 * i, 4 * i + 4):
                    ins = A(modc[:, j, :], bank(bk)[:, 2 * (j - 4 * i):2 * (j - 4 * i) + 2], ACT.Identity, bias=col("bmod")[:, j:j + 1])
                ins.then_inc(modc_done, 1)

            def behind_out(lo, hi):
                for what, i, part, bk in PARTS[lo:hi]:
                    if what == "rows" and part:
                        mod_row_out(i, bk)
                    elif what == "cols":
                        mod_column_out(i, bk)
                    elif what == "gate" and part:
                        f, n = i // 8, i % 8 // 2
                        act.wait_ge(gate_mm, now.value("gate_mm", 2 * (i + 1)))
                        if i >= STAGES:
                            act.wait_ge(gates_kept[i % STAGES], now.value("gates_kept", 16 * (i // STAGES)))
                        A(stage[:, i % STAGES], bank(bk, HALF), ACT.Sigmoid,
                          bias=col("bgate")[:, n * KT + f:n * KT + f + 1]).then_inc(sig_done, 2)

            act.wait_ge(start_loaded, 5 * 16)
            A(cS, cS, ACT.Silu).then_inc(silu_c_done, 1)
            with act.Fori(0, DEPTH) as layer:
                now.layer = layer
                act.wait_ge(x_done, now.value("x_done", 0))
                squares()
                act.dma_start(x_kept_dram, Xt[:, :]).then_inc(x_kept, 16)
                root(rstd)
                act.wait_ge(params_loaded, now.next("params_loaded", 32))
                for i in range(SLOTS_MOD):
                    mod_row_out(i, 4 + i)
                    mod_column_out(i, 4 + i)
                h_scaled(0)
                for g in range(0, 30, 2):
                    act.wait_ge(z_mm, now.next("z_mm", 2))
                    z_copies(g, nc.scalar.copy).then_inc(z_act, 1)
                    act.wait_ge(z_mm, now.next("z_mm", 2))
                act.wait_ge(z_act, now.next("z_act", 15))
                act.wait_ge(z_dve, now.next("z_dve", 15))
                A(zab[:, :, 0:512], zab[:, :, 0:512], ACT.Gelu_apprx_tanh).then_inc(gelu_done, 1)
                A(zab[:, :, 768:1024], zab[:, :, 768:1024], ACT.Sigmoid).then_inc(bsig_done, 1)
                A(zl[:, :, 256:384], zl[:, :, 256:384], ACT.Sigmoid)
                A(zl[:, :, 0:128], zl[:, :, 0:128], ACT.Tanh).then_inc(lora_done, 1)
                root(rstd)
                branch_out(0)
                act.wait_ge(cin_mm, now.next("cin_mm"))
                act.wait_ge(pads_zeroed, now.next("pads_zeroed"))
                for f in range(FT):
                    nc.scalar.copy(cin[f][:, PAD:PAD + P], ps[:, 1024 * f:1024 * f + P])
                    ins = nc.scalar.copy(cin[f][:, PAD + P + PAD:PAD + P + PAD + LAT * P], ps[:, 1024 * f + P:1024 * f + TOK])
                ins.then_inc(cin_done, 1)
                behind_out(0, CONV_PARTS)
                root(rstd)
                act.wait_ge(cln_done, now.next("cln_done"))
                A(zab[:, :, 512:768], zab[:, :, 512:768], ACT.Silu).then_inc(oB_done, 1)
                branch_out(1)
                act.wait_ge(qkT_mm, now.next("qkT_mm"))
                act.wait_ge(keys_ready, now.next("keys_ready"))
                for g in range(2):
                    nc.scalar.copy(qT[:, g, :], ps[:, 1024 * g:1024 * g + TOK])
                nc.scalar.copy(kTz[0:64, 0, P:P + TOK], ps[0:64, 2048:2048 + TOK])
                nc.scalar.copy(kTz[64:128, 1, P:P + TOK], ps[64:128, 2048:2048 + TOK]).then_inc(qT_done, 1)
                for b in range(NB):
                    n = P if b == 0 else P * (2 + min(LAT, b + 1) - max(1, b - 1))
                    act.wait_ge(smax_done, now.next("smax_done"))
                    for hd in range(4):
                        A(sc[:, hd, 0:n], sc[:, hd, 0:n], ACT.Exp, bias=smx[:, hd:hd + 1], accum_out=rsm[:, hd:hd + 1])
                    A(snk, snk, ACT.Exp).then_inc(probs_done, 1)
                branch_out(3)
                act.wait_ge(lorT_mm, now.next("lorT_mm"))
                for g in range(3):
                    ins = nc.scalar.copy(lorT[:, g, :], ps[:, 1024 * g:1024 * g + TOK])
                ins.then_inc(lorT_done, 1)
                for s, blocks in enumerate(STEPS):
                    part = CONV_PARTS + s * STEP_PARTS
                    act.wait_ge(wa_pre, now.next("wa_pre"))
                    A(sw, sw, ACT.Sigmoid)
                    A(aa, aa, ACT.Sigmoid).then_inc(wa_done, 1)
                    behind_out(part, part + 2)
                    act.wait_ge(decay_mm, now.next("decay_mm"))
                    A(rt.rearrange("p d c -> p (d c)"), bank(2), ACT.Exp)
                    A(bt.rearrange("p d c -> p (d c)"), bank(2), ACT.Exp, scale=-1.0)
                    A(at_.rearrange("p d c -> p (d c)"), bank(3), ACT.Exp)
                    A(gm.rearrange("p g e -> p (g e)"), bank(4, 8), ACT.Exp).then_inc(exp_done, 1)
                    root(kss)
                    behind_out(part + 2, part + 10)
                    act.wait_ge(tildeT_mm, now.next("tildeT_mm"))
                    for par in range(2):
                        r = slice(64 * par, 64 * par + 64)
                        nc.scalar.copy(ar[r, :, par, 0, :], bank(0)[r].rearrange("p (g t) -> p g t", g=4))
                    nc.scalar.copy(bT, bank(2).rearrange("p (g t) -> p g t", g=4)).then_inc(tildeT_act, 1)
                    behind_out(part + 10, part + 14)
                    for lev in range(LEVELS - 1):
                        act.wait_ge(x_mm, now.next("x_mm"))
                        nc.scalar.copy(Xm.rearrange("p g t -> p (g t)"), ps[:, 0:1024]).then_inc(xm_done, 1)
                        behind_out(part + 14 + 2 * lev, part + 16 + 2 * lev)
                    act.wait_ge(u_mm, now.next("u_mm"))
                    nc.scalar.copy(ub.rearrange("p g v -> p (g v)"), bank(2)).then_inc(u_done, 1)
                    act.wait_ge(sa_mm, now.next("sa_mm"))
                    nc.scalar.mul(sa.rearrange("p g v -> p (g v)"), bank(3), -1.0).then_inc(sa_done, 1)
                root(gs2)
                branch_out(2)
                act.wait_ge(mrow_mm, now.next("mrow_mm"))
                nc.scalar.copy(mrow[:, 0, :], ps[:, 2048:3072])
                nc.scalar.copy(mrow[:, 1, :], ps[:, 3072:4096]).then_inc(mrow_done, 1)
                act.wait_ge(xo_done, now.next("xo_done", 10))
                squares()
                root(rstd)
                h_scaled(3 * KT)
                act.wait_ge(route_max, now.next("route_max"))
                A(lg[:, :, 0:4], lg[:, :, 0:4], ACT.Exp)
                A(ein[:, :, 0:1], ein[:, :, 0:1], ACT.Exp).then_inc(route_exp, 1)
                act.wait_ge(combT_mm, now.next("combT_mm"))
                nc.scalar.copy(combT, ps[:, 1024:1024 + TOK]).then_inc(combT_done, 1)
                for e in range(NE):
                    act.wait_ge(cb_mm, now.next("cb_mm"))
                    if e >= 2:
                        act.wait_ge(hid_done, now.value("hid_done", 4 * (e - 1)))
                    nc.scalar.copy(cbs[:, e % 2, :], ps[:, 3072:3072 + TOK]).then_inc(cb_done, 1)
                    for i in range(4):
                        unit = 4 * e + i
                        act.wait_ge(egate_mm, now.next("egate_mm"))
                        if unit >= 2:
                            act.wait_ge(hid_done, now.value("hid_done", unit - 1))
                        A(sil[:, unit % 2, :], bank(2 * (unit % 3), 320), ACT.Silu).then_inc(silu_done, 1)
                act.wait_ge(mrow_mm, now.next("mrow_mm"))
                act.wait_ge(hid_done, now.value("hid_done", 4 * NE))
                nc.scalar.copy(mrow[:, 0, :], ps[:, 2048:3072])
                nc.scalar.copy(mrow[:, 1, :], ps[:, 3072:4096]).then_inc(mrow_done, 1)
            act.wait_ge(x_done, 1 + DEPTH * PER["x_done"])
            for b in range(NB):
                ins = A(xn[:, b, :], x[:, b, :], ACT.Square, accum_out=ssq[:, b:b + 1])
            ins.then_inc(final_sums, 1)
            act.wait_ge(final_var, 1)
            A(rstd, rstd, ACT.Sqrt).then_inc(final_std, 1)

        @block.vector
        def _(dve):
            now = Place()
            V = nc.vector

            def inverse_root(ap):
                dve.wait_ge(std_ready, now.next("std_ready"))
                V.reciprocal(ap, ap).then_inc(dve_chain, 1)
                dve.wait_ge(dve_chain, now.next("dve_chain"))

            def x_scaled():
                dve.wait_ge(ssq_done, now.next("ssq_done"))
                V.tensor_scalar(rstd, ssq, 1.0 / D, RMS_EPS, ALU.mult, ALU.add).then_inc(var_ready, 1)
                inverse_root(rstd)
                for b in range(NB):
                    V.tensor_scalar(xn[:, b, :], x[:, b, :], rstd[:, b:b + 1], None, ALU.mult).then_inc(xn_done, 1)

            def h_scaled(b_at):
                for f in range(1, KT, 2):
                    dve.wait_ge(hT_mm, now.next("hT_mm", 2))
                    o = 1024 * (f % 4)
                    V.tensor_scalar(h[:, f, 0:P], ps[:, o:o + P], A1[:, f, 0:1], modc[:, b_at + f, 0:1], ALU.mult, ALU.add)
                    V.tensor_scalar(h[:, f, P:TOK], ps[:, o + P:o + TOK], A1[:, f, 1:2],
                                                   modc[:, b_at + f, 1:2], ALU.mult, ALU.add).then_inc(hT_dve, 1)

            def mod_scale(s_at, norm):
                V.scalar_tensor_tensor(A1, modc[:, s_at:s_at + KT, :], 1.0, over(col(norm), 2, 2),
                                                              ALU.add, ALU.mult).then_inc(mod_scale_done, 1)
                dve.wait_ge(mod_scale_done, now.next("mod_scale_done"))

            def layer_stats(src):
                for b in range(NB):
                    ins = V.bn_stats(stats[:, 6 * b:6 * b + 6], src(b))
                ins.then_inc(dve_chain, 1)
                dve.wait_ge(dve_chain, now.next("dve_chain"))
                dve.sem_inc(waits_settled, 1)
                for b in range(NB):
                    ins = V.bn_aggr(mv[:, 2 * b:2 * b + 2], stats[:, 6 * b:6 * b + 6])
                ins.then_inc(dve_chain, 1)
                dve.wait_ge(dve_chain, now.next("dve_chain"))
                var = mv.rearrange("p (b e) -> p b e", e=2)[:, :, 1]
                V.tensor_scalar(rstd, var, LN_EPS, None, ALU.add).then_inc(var_ready, 1)
                inverse_root(rstd)

            def masked_gram(dst, half):
                for d in range(2):
                    o = SCANB["gram"][0] + 2 * d * P
                    ins = V.tensor_tensor(dst[:, 4 * d:4 * d + 4].rearrange("p g e t -> p g (e t)"),
                                          ps[:, half + 1024 * d:half + 1024 * d + 1024].rearrange("p (g c) -> p g c", g=4),
                                          over(scanb[:, o:o + 2 * P], 1, 4), ALU.mult)
                return ins

            def first_max(vals, n, best, onehot):
                iota = over(fixed("iota")[:, 0:n], 1, NB)
                V.tensor_reduce(best, vals, AX.X, ALU.max).then_inc(dve_chain, 1)
                dve.wait_ge(dve_chain, now.next("dve_chain"))
                V.tensor_tensor(t20, vals, over(best, 2, n), ALU.is_equal).then_inc(dve_chain, 1)
                dve.wait_ge(dve_chain, now.next("dve_chain"))
                V.scalar_tensor_tensor(t20, t20, -16.0, iota, ALU.mult, ALU.add).then_inc(dve_chain, 1)
                dve.wait_ge(dve_chain, now.next("dve_chain"))
                V.tensor_reduce(ix, t20, AX.X, ALU.min).then_inc(dve_chain, 1)
                dve.wait_ge(dve_chain, now.next("dve_chain"))
                V.tensor_tensor(onehot, t20, over(ix, 2, n), ALU.is_equal).then_inc(dve_chain, 1)
                dve.wait_ge(dve_chain, now.next("dve_chain"))

            dve.wait_ge(start_loaded, 5 * 16)
            V.memset(stats, 0.0).then_inc(x_done, 1)
            with dve.Fori(0, DEPTH) as layer:
                now.layer = layer
                x_scaled()
                dve.wait_ge(params_loaded, now.next("params_loaded", 32))
                dve.wait_ge(modc_done, now.next("modc_done", SLOTS_MOD))
                mod_scale(KT, "norm1")
                h_scaled(0)
                for g in range(1, 30, 2):
                    dve.wait_ge(z_mm, now.next("z_mm", 4))
                    z_copies(g, V.tensor_copy).then_inc(z_dve, 1)
                dve.wait_ge(gelu_done, now.next("gelu_done"))
                v = zab[:, :, 256:512]
                layer_stats(lambda b: zab[:, b, 256:512])
                for b in range(NB):
                    ins = V.tensor_scalar(zab[:, b, 256:512], zab[:, b, 256:512], mv[:, 2 * b:2 * b + 1], rstd[:, b:b + 1],
                                          ALU.subtract, ALU.mult)
                ins.then_inc(dve_chain, 1)
                dve.wait_ge(dve_chain, now.next("dve_chain"))
                V.tensor_tensor(v, v, over(row("gmlp_g"), 1, NB), ALU.mult).then_inc(vn_done, 1)
                dve.wait_ge(bsig_done, now.next("bsig_done"))
                V.tensor_tensor(zab[:, :, 512:768], zab[:, :, 512:768], zab[:, :, 768:1024], ALU.mult).then_inc(glu_done, 1)
                dve.wait_ge(gmlp_mm, now.next("gmlp_mm"))
                for g in range(4):
                    u = zab[:, :, g * HD:(g + 1) * HD]
                    ins = V.scalar_tensor_tensor(u, bank(g, NB * HD).rearrange("p (b c) -> p b c", b=NB),
                                                 col("gmlp_bs")[:, g:g + 1], u, ALU.add, ALU.mult)
                ins.then_inc(oA_done, 1)
                dve.wait_ge(cin_done, now.next("cin_done"))
                cw = col("conv_w").rearrange("p (f t) -> p f t", f=FT)
                for t in range(TAPS):
                    for f in range(FT):
                        src = cin[f][:, t:t + OUTS]
                        if t == 0:
                            ins = V.tensor_scalar(cacc[f], src, cw[:, f, 0:1], col("conv_b")[:, f:f + 1], ALU.mult, ALU.add)
                        else:
                            ins = V.scalar_tensor_tensor(cacc[f], src, cw[:, f, t:t + 1], cacc[f], ALU.mult, ALU.add)
                    if t < TAPS - 1:
                        ins.then_inc(dve_chain, 1)
                        dve.wait_ge(dve_chain, now.next("dve_chain"))
                ins.then_inc(conv_done, 1)
                dve.wait_ge(convT_mm, now.next("convT_mm"))
                layer_stats(lambda b: ps[:, b * W:(b + 1) * W])
                for b in range(NB):
                    ins = V.tensor_scalar(zab[:, b, 512:768], ps[:, b * W:(b + 1) * W], mv[:, 2 * b:2 * b + 1],
                                          rstd[:, b:b + 1], ALU.subtract, ALU.mult)
                ins.then_inc(dve_chain, 1)
                dve.wait_ge(dve_chain, now.next("dve_chain"))
                ob = zab[:, :, 512:768]
                V.tensor_tensor(ob, ob, over(row("conv_g"), 1, NB), ALU.mult).then_inc(dve_chain, 1)
                dve.wait_ge(dve_chain, now.next("dve_chain"))
                V.tensor_tensor(ob, ob, over(row("conv_lb"), 1, NB), ALU.add).then_inc(cln_done, 1)
                cos = fixed("cos").rearrange("p (b c) -> p b c", b=LAT)
                sin = fixed("sin").rearrange("p (b a e c) -> p b a e c", b=LAT, a=2, e=2)
                zq = zd[:, 1:NB, 0:384]
                zq5 = zq.rearrange("p b (h a e c) -> p b h a e c", h=6, a=2, e=2)
                rp5 = ropet.rearrange("p b (h a e c) -> p b h a e c", h=6, a=2, e=2)
                for ax in range(2):
                    for e in range(2):
                        V.tensor_tensor(rp5[:, :, :, ax, e, :], zq5[:, :, :, ax, 1 - e, :], over(sin[:, :, ax, e, :], 2, 6), ALU.mult)
                V.tensor_tensor(qkr[:, 1:NB].rearrange("p b (h c) -> p b h c", h=6), zq.rearrange("p b (h c) -> p b h c", h=6),
                                       over(cos, 2, 6), ALU.mult).then_inc(dve_chain, 1)
                dve.wait_ge(dve_chain, now.next("dve_chain"))
                V.tensor_tensor(qkr[:, 1:NB], qkr[:, 1:NB], ropet, ALU.add).then_inc(rope_done, 1)
                dve.wait_ge(brT_done, now.next("brT_done", 2))
                for b in range(NB):
                    lo, hi = (0, 0) if b == 0 else (max(1, b - 1), min(LAT, b + 1))
                    nband = (hi - lo + 1) * P
                    n = nband + (P if b else 0)
                    S4 = ps[:, 0:2048].rearrange("p (h s) -> p h s", h=4)
                    dve.wait_ge(scores_mm, now.next("scores_mm"))
                    if b == 0:
                        V.tensor_scalar(sc[:, :, 0:n], S4[:, :, 0:n], SCALE, None, ALU.mult).then_inc(dve_chain, 1)
                        dve.wait_ge(dve_chain, now.next("dve_chain"))
                    else:
                        V.tensor_scalar(sc[:, :, 0:P], S4[:, :, 0:P], SCALE, None, ALU.mult)
                        o = (lo - b + 1) * P
                        V.scalar_tensor_tensor(sc[:, :, P:n], S4[:, :, P:n], SCALE, over(fixed("band")[:, o:o + nband], 1, 4),
                                                      ALU.mult, ALU.add).then_inc(dve_chain, 1)
                        dve.wait_ge(dve_chain, now.next("dve_chain"))
                    V.tensor_reduce(mx, sc[:, :, 0:n], AX.X, ALU.max).then_inc(dve_chain, 1)
                    dve.wait_ge(dve_chain, now.next("dve_chain"))
                    V.tensor_tensor(mx, mx, row("sink"), ALU.max).then_inc(dve_chain, 1)
                    dve.wait_ge(dve_chain, now.next("dve_chain"))
                    V.tensor_tensor(snk, row("sink"), mx, ALU.subtract)
                    V.tensor_scalar(smx, mx, -1.0, None, ALU.mult).then_inc(smax_done, 1)
                    dve.wait_ge(probs_done, now.next("probs_done"))
                    V.tensor_tensor(rsm, rsm, snk, ALU.add).then_inc(dve_chain, 1)
                    dve.wait_ge(dve_chain, now.next("dve_chain"))
                    V.reciprocal(rsm, rsm).then_inc(dve_chain, 1)
                    dve.wait_ge(dve_chain, now.next("dve_chain"))
                    dve.wait_ge(probsT_mm, now.next("probsT_mm"))
                    V.tensor_copy(pT[:, 0:n // P].rearrange("p s h q -> p (s h q)"), ps[:, 2048:2048 + 4 * n]).then_inc(probsT_done, 1)
                    dve.wait_ge(att_mm, now.next("att_mm"))
                    V.tensor_tensor(zd[:, b, 0:256].rearrange("p (h c) -> p h c", h=4),
                                                     ps[:, 0:256].rearrange("p (h c) -> p h c", h=4), over(rsm, 2, HD), ALU.mult).then_inc(att_done, 1)
                dve.wait_ge(scan_ready, now.next("scan_ready"))
                dve.wait_ge(cache_out, now.next("cache_out", 32))
                heads8 = "p d (h c) -> p (d h) c"
                for s, blocks in enumerate(STEPS):
                    if s == 0:
                        V.memset(S, 0.0).then_inc(dve_chain, 1)
                        dve.wait_ge(dve_chain, now.next("dve_chain"))
                    if s == 1:
                        V.tensor_copy(S.rearrange("p g v -> p (g v)"), col("state")).then_inc(dve_chain, 1)
                        dve.wait_ge(dve_chain, now.next("dve_chain"))
                    dve.wait_ge(wa_mm, now.next("wa_mm"))
                    V.tensor_tensor(sw.rearrange("p d c -> p (d c)"), bank(0), row("w0"), ALU.add)
                    V.tensor_tensor(aa.rearrange("p d c -> p (d c)"), bank(1), row("a0"), ALU.add).then_inc(wa_pre, 1)
                    for d, blk in enumerate(blocks):
                        ins = V.tensor_tensor(kks[:, d], zc[:, blk, 256:512], row("kkw"), ALU.mult)
                    ins.then_inc(dve_chain, 1)
                    dve.wait_ge(dve_chain, now.next("dve_chain"))
                    V.tensor_tensor(kt_, kks, kks, ALU.mult).then_inc(dve_chain, 1)
                    dve.wait_ge(dve_chain, now.next("dve_chain"))
                    V.tensor_reduce(kss, kt_.rearrange(heads8, h=4), AX.X, ALU.add).then_inc(dve_chain, 1)
                    dve.wait_ge(dve_chain, now.next("dve_chain"))
                    dve.wait_ge(exp_done, now.next("exp_done"))
                    V.tensor_scalar(kss, kss, 0.0, None, ALU.add).then_inc(var_ready, 1)
                    dve.wait_ge(std_ready, now.next("std_ready"))
                    V.tensor_scalar(kss, kss, 1e-12, None, ALU.max).then_inc(dve_chain, 1)
                    dve.wait_ge(dve_chain, now.next("dve_chain"))
                    V.reciprocal(kss, kss).then_inc(dve_chain, 1)
                    dve.wait_ge(dve_chain, now.next("dve_chain"))
                    V.tensor_tensor(kks.rearrange(heads8, h=4), kks.rearrange(heads8, h=4), over(kss, 2, HD), ALU.mult).then_inc(dve_chain, 1)
                    dve.wait_ge(dve_chain, now.next("dve_chain"))
                    V.scalar_tensor_tensor(kt_, aa, -1.0, over(row("ka"), 1, 2), ALU.add, ALU.mult).then_inc(dve_chain, 1)
                    dve.wait_ge(dve_chain, now.next("dve_chain"))
                    for d, blk in enumerate(blocks):
                        ins = V.scalar_tensor_tensor(kt_[:, d], kt_[:, d], 1.0, zc[:, blk, 256:512], ALU.add, ALU.mult)
                    ins.then_inc(dve_chain, 1)
                    dve.wait_ge(dve_chain, now.next("dve_chain"))
                    tmp = Xm[:, 0:4, :].rearrange("p a t -> p (a t)").rearrange("p (d c) -> p d c", d=2)
                    V.tensor_tensor(tmp, kt_, over(row("rk"), 1, 2), ALU.mult).then_inc(dve_chain, 1)
                    dve.wait_ge(dve_chain, now.next("dve_chain"))
                    for d, blk in enumerate(blocks):
                        ins = V.tensor_tensor(tmp[:, d], tmp[:, d], zc[:, blk, 0:256], ALU.mult)
                    ins.then_inc(dve_chain, 1)
                    dve.wait_ge(dve_chain, now.next("dve_chain"))
                    for d, blk in enumerate(blocks):
                        V.tensor_reduce(bon[:, blk, d], tmp[:, d].rearrange("p (h c) -> p h c", h=4), AX.X, ALU.add)
                    V.tensor_tensor(aa, aa, kks, ALU.mult).then_inc(dve_chain, 1)
                    dve.wait_ge(dve_chain, now.next("dve_chain"))
                    for d, blk in enumerate(blocks):
                        V.tensor_tensor(rt[:, d], rt[:, d], zc[:, blk, 0:256], ALU.mult)
                    V.tensor_tensor(at_, at_, kks, ALU.mult)
                    V.tensor_tensor(kt_, kt_, bt, ALU.mult).then_inc(dve_chain, 1)
                    dve.wait_ge(dve_chain, now.next("dve_chain"))
                    V.tensor_tensor(bt, bt, aa, ALU.mult).then_inc(tilde_done, 1)
                    for d in range(2):
                        ins = V.tensor_tensor(S0[:, 2 * d:2 * d + 2], S[:, 2 * d:2 * d + 2], over(gm[:, 2 * d:2 * d + 2, d], 2, HD), ALU.mult)
                    ins.then_inc(s0_done, 1)
                    dve.wait_ge(tildeT_mm, now.next("tildeT_mm"))
                    for par in range(2):
                        r = slice(64 * par, 64 * par + 64)
                        V.tensor_copy(ar[r, :, par, 1, :], bank(1)[r].rearrange("p (g t) -> p g t", g=4))
                    V.tensor_copy(kT, bank(3).rearrange("p (g t) -> p g t", g=4)).then_inc(tildeT_dve, 1)
                    dve.wait_ge(gramB_mm, now.next("gramB_mm"))
                    masked_gram(gb, 0).then_inc(gb_done, 1)
                    dve.wait_ge(gramK_mm, now.next("gramK_mm"))
                    masked_gram(gk, 2048).then_inc(gk_done, 1)
                    dve.wait_ge(gb_done, now.next("gb_done"))
                    lv = SCANB["lev0"][0]
                    for d in range(2):
                        V.tensor_tensor(TT[:, 4 * d:4 * d + 4], gb[:, 4 * d:4 * d + 4, 0, :],
                                        over(scanb[:, lv + (2 + d) * P:lv + (3 + d) * P], 1, 4), ALU.mult)
                    dve.wait_ge(n_mm, now.next("n_mm"))
                    for d in range(2):
                        ins = V.tensor_tensor(Tm[:, 4 * d:4 * d + 4], ps[:, 512 * d:512 * d + 512].rearrange("p (g t) -> p g t", g=4),
                                              over(scanb[:, lv + d * P:lv + (d + 1) * P], 1, 4), ALU.mult)
                    ins.then_inc(dve_chain, 1)
                    dve.wait_ge(dve_chain, now.next("dve_chain"))
                    V.tensor_tensor(TT, TT, over(ident, 1, 8), ALU.add)
                    V.tensor_tensor(Tm, Tm, over(ident, 1, 8), ALU.add).then_inc(t_done, 1)
                    for lev in range(LEVELS - 1):
                        dve.wait_ge(y_mm, now.next("y_mm"))
                        dve.wait_ge(t_done, now.next("t_done"))
                        if lev < LEVELS - 2:
                            V.tensor_tensor(Tm, Tm, ps[:, 1024:2048].rearrange("p (g t) -> p g t", g=8), ALU.subtract)
                        V.tensor_tensor(TT, TT, ps[:, 2048:3072].rearrange("p (g t) -> p g t", g=8), ALU.subtract).then_inc(t_done, 1)
                    dve.wait_ge(t_done, now.next("t_done"))
                    dve.wait_ge(step_mm, now.next("step_mm"))
                    for d, blk in enumerate(blocks):
                        first = (s < 3) and not (s == 0 and d == 1)
                        if s == 0 and d == 1:
                            ins.then_inc(dve_chain, 1)
                            dve.wait_ge(dve_chain, now.next("dve_chain"))
                        src = bank(0)[:, d * W:(d + 1) * W]
                        if first:
                            ins = V.tensor_copy(y[:, blk], src)
                        else:
                            ins = V.tensor_tensor(y[:, blk], y[:, blk], src, ALU.add)
                    V.tensor_tensor(S0, S0, bank(1, 256).rearrange("p (g v) -> p g v", g=4), ALU.add).then_inc(dve_chain, 1)
                    dve.wait_ge(dve_chain, now.next("dve_chain"))
                    dst = state_out if s == 0 else S
                    for d in range(2):
                        ins = V.tensor_tensor(dst[:, 2 * d:2 * d + 2], S0[:, 2 * d:2 * d + 2],
                                              over(gm[:, 2 * d:2 * d + 2, 1 - d], 2, HD), ALU.mult)
                        if d == 0:
                            ins.then_inc(dve_chain, 1)
                            dve.wait_ge(dve_chain, now.next("dve_chain"))
                    if s == 0:
                        ins.then_inc(state_ready, 1)
                        dve.wait_ge(state_ready, now.next("state_ready"))
                        V.memset(stats, 0.0).then_inc(step_done, 1)
                    else:
                        ins.then_inc(step_done, 1)
                    dve.wait_ge(step_done, now.next("step_done"))
                y20 = y.rearrange("p b (h c) -> p (b h) c", h=4)
                tmp = Xt[:, 0:NB * W].rearrange("p (b c) -> p b c", b=NB)
                tmp20 = tmp.rearrange("p b (h c) -> p (b h) c", h=4)
                V.tensor_reduce(gst, y20, AX.X, ALU.add).then_inc(dve_chain, 1)
                dve.wait_ge(dve_chain, now.next("dve_chain"))
                V.tensor_scalar(gst, gst, 1.0 / HD, None, ALU.mult).then_inc(dve_chain, 1)
                dve.wait_ge(dve_chain, now.next("dve_chain"))
                V.tensor_tensor(y20, y20, over(gst, 2, HD), ALU.subtract).then_inc(dve_chain, 1)
                dve.wait_ge(dve_chain, now.next("dve_chain"))
                V.tensor_tensor(tmp, y, y, ALU.mult).then_inc(dve_chain, 1)
                dve.wait_ge(dve_chain, now.next("dve_chain"))
                V.tensor_reduce(gs2, tmp20, AX.X, ALU.add).then_inc(dve_chain, 1)
                dve.wait_ge(dve_chain, now.next("dve_chain"))
                V.tensor_scalar(gs2, gs2, 1.0 / HD, GN_EPS, ALU.mult, ALU.add).then_inc(var_ready, 1)
                inverse_root(gs2)
                V.tensor_tensor(y20, y20, over(gs2, 2, HD), ALU.mult).then_inc(dve_chain, 1)
                dve.wait_ge(dve_chain, now.next("dve_chain"))
                V.tensor_tensor(y, y, over(row("lnx_g"), 1, NB), ALU.mult).then_inc(dve_chain, 1)
                dve.wait_ge(dve_chain, now.next("dve_chain"))
                V.tensor_tensor(y, y, over(row("lnx_b"), 1, NB), ALU.add).then_inc(dve_chain, 1)
                dve.wait_ge(dve_chain, now.next("dve_chain"))
                V.tensor_tensor(bon[:, :, 0], bon[:, :, 0], bon[:, :, 1], ALU.add).then_inc(dve_chain, 1)
                dve.wait_ge(dve_chain, now.next("dve_chain"))
                for b in range(NB):
                    ins = V.tensor_tensor(tmp[:, b].rearrange("p (h c) -> p h c", h=4), zc[:, b, 512:768].rearrange("p (h c) -> p h c", h=4),
                                          over(bon[:, b, 0], 2, HD), ALU.mult)
                ins.then_inc(dve_chain, 1)
                dve.wait_ge(dve_chain, now.next("dve_chain"))
                V.tensor_tensor(y, y, tmp, ALU.add).then_inc(dve_chain, 1)
                dve.wait_ge(dve_chain, now.next("dve_chain"))
                dve.wait_ge(g_mm, now.next("g_mm"))
                V.tensor_tensor(y, y, ps[:, 0:NB * W].rearrange("p (b c) -> p b c", b=NB), ALU.mult).then_inc(oC_done, 1)
                dve.wait_ge(brT_done, now.next("brT_done", 2))
                for unit in range(4 * KT):
                    f, n = unit // 4, unit % 4
                    u = AT_BACK + f
                    if n == 0:
                        dve.wait_ge(slot_loaded[u % RING], now.load(u))
                    gate = ring[:, (u % RING) * SLOT + n * TOK:(u % RING) * SLOT + (n + 1) * TOK]
                    dve.wait_ge(proj_mm, now.next("proj_mm"))
                    o = 1024 * (unit % 4)
                    if n == 0:
                        V.tensor_tensor(mixT[:, f, :], gate, ps[:, o:o + TOK], ALU.mult).then_inc(mix_done, 1)
                    else:
                        V.tensor_tensor(gate, gate, ps[:, o:o + TOK], ALU.mult).then_inc(dve_chain, 1)
                        dve.wait_ge(dve_chain, now.next("dve_chain"))
                        V.tensor_tensor(mixT[:, f, :], mixT[:, f, :], gate, ALU.add).then_inc(mix_done, 1)
                    dve.wait_ge(mix_done, now.next("mix_done"))
                dve.wait_ge(mrow_done, now.next("mrow_done"))
                dve.wait_ge(x_back, now.next("x_back", 16))

                def add_to_x(g):
                    c, b = g // NB, g % NB
                    acc, xv = bank(g % 8), x[:, b, c * 512:(c + 1) * 512]
                    V.tensor_tensor(acc, acc, mrow[:, 0 if b == 0 else 1, c * 512:(c + 1) * 512], ALU.mult).then_inc(dve_chain, 1)
                    dve.wait_ge(dve_chain, now.next("dve_chain"))
                    return V.tensor_tensor(xv, xv, acc, ALU.add)

                for g in range(10):
                    dve.wait_ge(wout_mm, now.next("wout_mm"))
                    add_to_x(g).then_inc(xo_done, 1)
                dve.wait_ge(xo_done, now.next("xo_done", 10))
                x_scaled()
                dve.wait_ge(modc_done, now.next("modc_done", MODS - SLOTS_MOD))
                mod_scale(4 * KT, "norm2")
                h_scaled(3 * KT)
                dve.wait_ge(router_mm, now.next("router_mm"))
                V.tensor_tensor(lg, ps[:, 0:100].rearrange("p (b e) -> p b e", b=NB), over(row("br"), 1, NB), ALU.add).then_inc(dve_chain, 1)
                dve.wait_ge(dve_chain, now.next("dve_chain"))
                first_max(lg[:, :, 0:4], 4, m1, gsel)
                elog = lg[:, :, 4:20].rearrange("p b (g e) -> p b g e", g=4)
                for b in range(NB):
                    V.tensor_tensor(lg[:, b, 0:4], lg[:, b, 0:4], m1[:, b:b + 1].broadcast_to([P, 4]), ALU.subtract)
                    ins = V.tensor_tensor(t16[:, b], elog[:, b], over(gsel[:, b], 2, 4), ALU.mult)
                ins.then_inc(dve_chain, 1)
                dve.wait_ge(dve_chain, now.next("dve_chain"))
                for b in range(NB):
                    ins = V.tensor_reduce(ein[:, b], t16[:, b].rearrange("p g e -> p e g"), AX.X, ALU.add)
                ins.then_inc(dve_chain, 1)
                dve.wait_ge(dve_chain, now.next("dve_chain"))
                first_max(ein, 4, m1, oh1)
                V.scalar_tensor_tensor(ein, oh1, NEG, ein, ALU.mult, ALU.add).then_inc(dve_chain, 1)
                dve.wait_ge(dve_chain, now.next("dve_chain"))
                first_max(ein, 4, m2_, oh2)
                V.tensor_tensor(ein[:, :, 0], m2_, m1, ALU.subtract).then_inc(route_max, 1)
                dve.wait_ge(route_exp, now.next("route_exp"))
                V.tensor_reduce(gw, lg[:, :, 0:4], AX.X, ALU.add)
                V.tensor_scalar(m1, ein[:, :, 0], 1.0, None, ALU.add).then_inc(dve_chain, 1)
                dve.wait_ge(dve_chain, now.next("dve_chain"))
                V.tensor_tensor(gw, gw, m1, ALU.mult).then_inc(dve_chain, 1)
                dve.wait_ge(dve_chain, now.next("dve_chain"))
                V.reciprocal(gw, gw).then_inc(dve_chain, 1)
                dve.wait_ge(dve_chain, now.next("dve_chain"))
                V.tensor_tensor(m2_, gw, ein[:, :, 0], ALU.mult).then_inc(dve_chain, 1)
                dve.wait_ge(dve_chain, now.next("dve_chain"))
                V.tensor_tensor(oh1, oh1, over(gw, 2, 4), ALU.mult)
                V.tensor_tensor(oh2, oh2, over(m2_, 2, 4), ALU.mult).then_inc(dve_chain, 1)
                dve.wait_ge(dve_chain, now.next("dve_chain"))
                V.tensor_tensor(oh1, oh1, oh2, ALU.add).then_inc(dve_chain, 1)
                dve.wait_ge(dve_chain, now.next("dve_chain"))
                V.memset(comb, 0.0).then_inc(dve_chain, 1)
                dve.wait_ge(dve_chain, now.next("dve_chain"))
                for b in range(NB):
                    ins = V.tensor_tensor(comb[:, b, 0:16].rearrange("p (g e) -> p g e", g=4), over(gsel[:, b], 2, 4),
                                          over(oh1[:, b], 1, 4), ALU.mult)
                ins.then_inc(comb_done, 1)
                for unit in range(4 * NE):
                    e, i = unit // 4, unit % 4
                    f, hf = i // 2, i % 2
                    s_ = sil[:, unit % 2, :]
                    dve.wait_ge(silu_done, now.next("silu_done"))
                    dve.wait_ge(up_mm, now.next("up_mm"))
                    V.tensor_tensor(s_, s_, bank(2 * (unit % 3) + 1, 320), ALU.mult).then_inc(dve_chain, 1)
                    dve.wait_ge(dve_chain, now.next("dve_chain"))
                    if i == 0:
                        dve.wait_ge(cb_done, now.next("cb_done"))
                    V.tensor_tensor(hid[:, 2 * e + f, hf * 320:(hf + 1) * 320], s_,
                                                     cbs[:, e % 2, hf * 320:(hf + 1) * 320], ALU.mult).then_inc(hid_done, 1)
                dve.wait_ge(mrow_done, now.next("mrow_done"))
                for g in range(10):
                    if g % NB == 0:
                        dve.wait_ge(down_mm, now.next("down_mm", 4))
                    add_to_x(g).then_inc(x_done, 1)
                dve.wait_ge(x_done, now.next("x_done", 10))
            dve.wait_ge(final_sums, 1)
            V.tensor_scalar(rstd, ssq, 1.0 / D, RMS_EPS, ALU.mult, ALU.add).then_inc(final_var, 1)
            dve.wait_ge(final_std, 1)
            V.reciprocal(rstd, rstd).then_inc(final_chain, 1)
            dve.wait_ge(final_chain, 1)
            dve.wait_ge(final_g_loaded, 16)
            for b in range(NB):
                ins = V.scalar_tensor_tensor(xn[:, b, :], x[:, b, :], rstd[:, b:b + 1], arena[:, 10240:10240 + D],
                                             ALU.mult, ALU.mult)
            ins.then_inc(final_done, 1)




def shape_constants():
    t = np.arange(P)
    fix = np.zeros((P, NFIX), np.float32)
    o = FIX["ident"][0]
    fix[:, o:o + P] = np.eye(P)
    half = HD // 4
    inv = 10000.0 ** (-np.arange(half, dtype=np.float32) / np.float32(half))
    tok = np.arange(LAT * P)
    ang = np.stack([(tok // 64)[:, None] * inv, (tok % 64)[:, None] * inv], 1).astype(np.float32)
    cos, sin = np.cos(ang), np.sin(ang)
    c = np.stack([cos, cos], 2).reshape(LAT, P, HD).transpose(1, 0, 2)
    s = np.stack([-sin, sin], 2).reshape(LAT, P, HD).transpose(1, 0, 2)
    for name, v in (("cos", c), ("sin", s)):
        o, n = FIX[name]
        fix[:, o:o + n] = v.reshape(P, n)
    o = FIX["band"][0]
    fix[:, o:o + P] = np.where(t[None, :] >= t[:, None], 0.0, NEG)
    fix[:, o + 2 * P:o + 3 * P] = np.where(t[None, :] <= t[:, None], 0.0, NEG)
    o = FIX["iota"][0]
    fix[:, o:o + 4] = np.arange(4)
    scanf = np.zeros((P, NSCANF), np.float32)
    s_, t_ = t[:, None], t[None, :]
    rate = -np.exp(-0.5)
    for d in range(2):
        lead = (s_ < 64) if d == 0 else (s_ >= 64)
        up, before = (s_ <= t_, s_ < t_) if d == 0 else (s_ >= t_, s_ > t_)
        for name, m in (("incl", up), ("excl", before)):
            o = SCANF[name][0] + d * P
            scanf[:, o:o + P] = rate * (m.astype(np.float32) - lead.astype(np.float32))
    o = SCANF["halves"][0]
    scanf[:, o] = rate * (t < 64)
    scanf[:, o + 1] = rate * (t >= 64)
    scanb = np.zeros((P, NSCANB), np.float32)
    for d in range(2):
        strict, incl = (s_ < t_, s_ <= t_) if d == 0 else (s_ > t_, s_ >= t_)
        o = SCANB["gram"][0] + 2 * d * P
        scanb[:, o:o + P], scanb[:, o + P:o + 2 * P] = strict, incl
        for lev in range(LEVELS):
            m = 1 << lev
            pair = (s_ // (2 * m) == t_ // (2 * m)) & (s_ // m != t_ // m) & strict
            if lev:
                o = SCANB["lev"][0] + ((lev - 1) * 2 + d) * P
                scanb[:, o:o + P] = pair
            else:
                o = SCANB["lev0"][0] + d * P
                scanb[:, o:o + P] = -pair.T.astype(np.float32)
                scanb[:, o + 2 * P:o + 3 * P] = -pair.astype(np.float32)
    return fix, scanf, scanb


def kernel(**inputs):
    import concourse.bacc as bacc
    from concourse.bass_utils import run_bass_kernel_spmd

    i = {k: np.asarray(v) for k, v in inputs.items()}
    L = DEPTH

    def tiles(w, n=512):
        v = w.reshape(L, -1, P, w.shape[-1] // n, n)
        return v.transpose(0, 3, 2, 1, 4).reshape(L, v.shape[3], P, -1)

    q0 = 2176
    order = np.concatenate([np.arange(q0), *[q0 + hd * HD + np.arange(HD) for hd in (0, 2, 1, 3)], np.arange(q0 + W, 2688)])
    w_in = np.zeros((L, D, 3072), np.float32)
    w_in[:, :, :2688] = i["w_in"][:, :, order]
    gate = i["w_gate"].reshape(L, KT, P, 4, KT, P).transpose(0, 4, 2, 1, 3, 5).reshape(L, KT, P, SLOT)
    up = np.stack([i["w_e_gate"], i["w_e_up"]], 3).reshape(L, NE, KT, P, 2 * FF).transpose(0, 1, 3, 2, 4).reshape(L, NE, P, SLOT)
    down = i["w_e_down"].reshape(L, 4, KT, P, 2, 512).transpose(0, 4, 1, 3, 2, 5).reshape(L, SLOTS_DOWN, P, SLOT)
    mod = tiles(i["w_mod"])
    behind = np.stack([mod[:, SLOTS_MOD:], gate], 2).reshape(L, SLOTS_BEHIND, P, SLOT)
    stream = np.concatenate([mod[:, :SLOTS_MOD], tiles(w_in), behind, tiles(i["w_out"]), up, down], 1).reshape(-1, P, SLOT)
    stream = np.concatenate([stream, np.zeros((RING, P, SLOT), np.float32)])
    wbranch = i["w_branch"].reshape(L, 4, 2, P, KT, P).transpose(0, 3, 4, 1, 2, 5).reshape(L, P, 8 * D)

    def vec(v):
        return v.reshape(L, -1, P).transpose(0, 2, 1)

    def diagonal(w):
        z = np.zeros((L, 2, 64, 2, W), np.float32)
        for d in range(2):
            z[:, d, :, d] = w[:, d]
        return z.reshape(L, P, 2 * W)

    cols = {
        "norm1": vec(i["norm1_g"]), "norm2": vec(i["norm2_g"]), "bmod": vec(i["b_mod"]), "bgate": vec(i["b_gate"]),
        "gmlp_bs": i["gmlp_bs"].transpose(0, 2, 1),
        "conv_w": i["conv_w"].reshape(L, TAPS, FT, P).transpose(0, 3, 2, 1).reshape(L, P, -1),
        "conv_b": vec(i["conv_b"]), "wsT": i["gmlp_ws"].transpose(0, 3, 1, 2).reshape(L, P, 4 * P),
        "w2": diagonal(i["rwkv_w2"]), "a2": diagonal(i["rwkv_a2"]), "g2": i["rwkv_g2"],
        "ckT": i["cache_k"][0].reshape(L, P, P).transpose(0, 2, 1), "cv": i["cache_v"][0].reshape(L, P, P),
        "router": np.concatenate([i["w_rg"], i["w_re"]], 2).reshape(L, KT, P, 20).transpose(0, 2, 1, 3).reshape(L, P, -1),
        "state": i["state_rwkv"][0].reshape(L, 2, 2, 2, HD, HD).transpose(0, 3, 5, 1, 2, 4).reshape(L, P, 4 * HD),
    }
    rows = {
        "gmlp_g": i["gmlp_ln_g"], "conv_g": i["conv_ln_g"], "conv_lb": i["conv_ln_b"], "w0": i["rwkv_w0"], "a0": i["rwkv_a0"],
        "kkw": i["rwkv_kk"], "ka": i["rwkv_ka"], "rk": i["rwkv_rk"], "lnx_g": i["rwkv_lnx_g"], "lnx_b": i["rwkv_lnx_b"],
        "sink": i["attn_sink"], "br": np.concatenate([i["b_rg"], i["b_re"]], 1),
    }
    fix, scanf, scanb = shape_constants()
    arrays = {
        "stream": stream, "wbranch": wbranch,
        "cols": np.concatenate([cols[n].reshape(L, P, COLS[n][1]) for n in COLS], 2),
        "rows": np.concatenate([rows[n].reshape(L, 1, ROWS[n][1]) for n in ROWS], 2),
        "fix": fix, "scanf": scanf, "scanb": scanb,
        "x": np.concatenate([i["x_prompt"][0], i["x_sample"][0]]).reshape(NB, P, D).transpose(1, 0, 2).reshape(P, NB * D),
        "c": np.stack([i["c_ctx"], i["c"][0]]).reshape(2, KT, P).transpose(2, 1, 0).reshape(P, 2 * KT),
        "final_g": i["final_norm_g"].reshape(1, D),
    }
    outputs = {"y_prompt": (P, D), "y_sample": (LAT * P, D), "new_k": (L, P, P), "new_v": (L, P, P), "new_s": (L, P, 4 * HD)}
    nc = bacc.Bacc("TRN2", target_bir_lowering=False, num_devices=1)
    feed, args = {}, {}
    for name, v in arrays.items():
        v = np.ascontiguousarray(v)
        feed[f"in_{name}"] = v
        args[name] = nc.dram_tensor(f"in_{name}", v.shape, mybir.dt.from_np(v.dtype), kind="ExternalInput").ap()
    for name, shape in outputs.items():
        args[name] = nc.dram_tensor(f"out_{name}", shape, F32, kind="ExternalOutput").ap()
    build(nc, args)
    r = run_bass_kernel_spmd(nc, [feed], core_ids=[0]).results[0]
    s = r["out_new_s"].reshape(L, 2, HD, 2, 2, HD).transpose(0, 3, 4, 1, 5, 2).reshape(1, L, 2, 4, HD, HD)
    return (r["out_y_prompt"].reshape(1, P, D), r["out_y_sample"].reshape(1, LAT * P, D),
            r["out_new_k"].reshape(1, L, P, 2, HD), r["out_new_v"].reshape(1, L, P, 2, HD), s)
```

```python
from contextlib import ExitStack

import numpy as np
import concourse.bass as bass
from concourse import mybir

F32 = mybir.dt.float32
F32R = mybir.dt.float32r
ALU = mybir.AluOpType
ACT = mybir.ActivationFunctionType
AX = mybir.AxisListType

P = 128
D = 1024
DEPTH = 2
KT = D // P
NB = 5
LAT = NB - 1
TOK = NB * P
W = 256
FT = W // P
HD = 64
NE = 16
FF = 256
TAPS = 31
PAD = TAPS // 2
LINE = PAD + P + PAD + LAT * P + PAD
OUTS = LINE - 2 * PAD
LAT_OUT = P + PAD
EG = NE // 4
LEVELS = 7
SLOT = KT * 512
MODS = 12
SLOTS_MOD, SLOTS_IN, SLOTS_BEHIND, SLOTS_BACK, SLOTS_OUT, SLOTS_UP, SLOTS_DOWN = 4, 6, 16, KT, 2, NE, 8
AT_IN = SLOTS_MOD
AT_BEHIND = AT_IN + SLOTS_IN
AT_BACK = AT_BEHIND + SLOTS_BEHIND
AT_OUT = AT_BACK + SLOTS_BACK
AT_UP = AT_OUT + SLOTS_OUT
SLOTS = AT_UP + SLOTS_UP + SLOTS_DOWN
HALVES = 2 * (SLOTS_UP + SLOTS_DOWN)
RING = 2
HALF = TOK // 2
PIECES = KT * 4 * 2
STAGES = 4
STEPS = [(0, 0), (1, 4), (2, 3), (3, 2), (4, 1)]
GMLP_PARTS, CONV_PARTS, LN_PARTS, ATT_PARTS, STEP_PARTS = 4, 22, 4, 5, 19
WA_PARTS = 2
PAIRED = STEP_PARTS - 8 - (LEVELS - 1)
CONV_AT = GMLP_PARTS
LN_AT = CONV_AT + CONV_PARTS
ATT_AT = LN_AT + LN_PARTS
SCAN_AT = ATT_AT + NB * ATT_PARTS
NORM_AT = SCAN_AT + len(STEPS) * STEP_PARTS
RMS_EPS, LN_EPS, GN_EPS = 1e-6, 1e-5, 64e-5
NEG = -1e30
SCALE = HD ** -0.5


def parts_behind():
    parts, turn = [], None
    for n in range(SLOTS_BEHIND // 2 * 9):
        bank = 6 + n % 2
        if n % 9 == 0:
            i = SLOTS_MOD + n // 9
            parts += [("rows", i, 0, bank), ("rows", i, 1, bank)]
            turn = ("cols", i, 0, bank)
        else:
            i = n // 9 * 8 + n % 9 - 1
            parts += [("gate", i, 0, bank), ("gate", i, 1, bank)]
            if turn:
                parts.append(turn)
                turn = None
    return parts


PARTS = parts_behind()
assert len(PARTS) >= NORM_AT


def closed(n):
    return n + (n < len(PARTS) and PARTS[n][2])


def counted(what, n):
    return sum(p[0] == what and (p[2] == 1 or what == "cols") for p in PARTS[:n])


def place_of_half(v):
    return v // (2 * EG + 4), v % (2 * EG + 4)


def use_of_half(v):
    g, at = place_of_half(v)
    if at < 2 * EG:
        return "up_mm", 2 * (2 * EG * g + at + 1)
    c, second = (at - 2 * EG) // 2, at % 2
    return "down_mm", 12 * g + 6 * c + (1 + NB if second else 1)


def level_parts(part, lev):
    lo = part + 8 + min(2 * lev, lev + PAIRED)
    mid = lo + (lev < PAIRED)
    return lo, mid, closed(part + STEP_PARTS) if lev == LEVELS - 2 else mid + 1


def fields(sizes):
    at, out = 0, {}
    for name, n in sizes:
        out[name] = (at, n)
        at += n
    return out, at


COLS, NCOLS = fields([("norm1", KT), ("norm2", KT), ("bmod", 48), ("bgate", 32), ("gmlp_bs", 4), ("conv_w", FT * TAPS),
                      ("conv_b", FT), ("wsT", 4 * P), ("w2", 2 * W), ("a2", 2 * W), ("g2", W), ("ckT", P), ("cv", P),
                      ("router", KT * 20), ("state", 4 * HD)])
ROWS, NROWS = fields([("gmlp_g", W), ("conv_g", W), ("conv_lb", W), ("w0", 2 * W), ("a0", 2 * W), ("kkw", W), ("ka", W),
                      ("rk", W), ("lnx_g", W), ("lnx_b", W), ("sink", 4), ("br", 20)])
FIX, NFIX = fields([("ident", P), ("cos", LAT * HD), ("sin", LAT * HD), ("band", 3 * P), ("iota", 4)])
SCANF, NSCANF = fields([("incl", 2 * P), ("excl", 2 * P), ("halves", 2)])
SCANB, NSCANB = fields([("gram", 4 * P), ("lev", (LEVELS - 1) * 2 * P), ("lev0", 4 * P)])
PER = {
    **{name: 1 for name in (
        "pads_zeroed", "keys_ready", "scan_ready", "state_ready", "vn_done", "gmlp_mm", "oA_done",
        "glu_done", "cin_mm", "cin_done", "cln_done", "conv_done", "convT_mm", "oB_done", "rope_done", "qkT_mm", "qT_done",
        "lora_done", "lorT_mm", "lorT_done", "g_mm", "oC_done", "gelu_done", "bsig_done", "comb_done",
        "combT_mm", "combT_done", "logits_read", "route_max", "route_exp")},
    **{name: 2 for name in ("ssq_done", "mod_scale_done", "mrow_mm", "mrow_done")},
    "pool_chain": 2, "xn_done": 2 * NB, "hT_mm": 2 * KT, "hT_act": KT, "hT_dve": KT,
    "brT_mm": 4, "brT_done": 4,
    **{name: NB for name in ("scores_mm", "smax_done", "probs_done", "probsT_mm", "probsT_done", "att_mm", "att_done")},
    **{name: len(STEPS) for name in (
        "wa_mm", "wa_pre", "wa_done", "decay_mm", "exp_done", "tilde_done", "s0_done", "tildeT_mm", "tildeT_act", "tildeT_dve",
        "gramB_mm", "gramK_mm", "gb_done", "gk_done", "n_mm", "u_mm", "u_done", "sa_mm", "sa_done", "step_mm", "step_done")},
    **{name: len(STEPS) * (LEVELS - 1) for name in ("nl_ready", "x_mm", "xm_done", "y_mm")},
    "t_done": len(STEPS) * LEVELS, "xf_done": len(STEPS) * (LEVELS - 2), "tc_done": len(STEPS) * (LEVELS - 1),
    "var_ready": 5 + len(STEPS), "std_ready": 5 + len(STEPS),
    "slot_loaded": 16 * SLOTS // RING,
    **{name: MODS for name in ("mod_mm", "mod_rows", "modT_mm", "modc_done")},
    "gate_mm": 2 * PIECES, "sig_done": 2 * PIECES, "gates_kept": 16 * PIECES // STAGES,
    "z_mm": 2 * SLOTS_IN * NB, "z_act": SLOTS_IN * NB // 2, "z_dve": SLOTS_IN * NB // 2,
    "proj_mm": KT * 4, "mix_done": KT * 4,
    "wout_mm": SLOTS_OUT * NB, "router_mm": NB, "xo_done": SLOTS_OUT * NB, "down_mm": 48, "xe_done": 6 * NB,
    "mixhi_done": KT, "mixlo_done": KT, "ohi_done": 2 * SLOTS_OUT, "olo_done": 2 * SLOTS_OUT,
    "hhi_done": 1, "hlo_done": 1, "hz_done": 1, "zhi_done": 2 * SLOTS_IN, "zlo_done": 2 * SLOTS_IN,
    **{name: HALVES for name in ("hi_done", "lo_done")},
    "x_done": 2 * NB,
    **{name: NE for name in ("cb_mm", "cb_done")},
    **{name: NE * 4 for name in ("egate_mm", "up_mm", "silu_done", "hid_done")},
    "params_loaded": 2 * 16, "x_kept": 16, "cache_out": 2 * 16, "state_stored": 16, "x_back": 16, "wb0_loaded": 16, "wb1_loaded": 16,
    "dve_chain": 285 + 2 * 4 * NE + 3 * 2 * NB,
}


class Place:

    def __init__(self):
        self.layer, self.seen = 0, {}

    def value(self, name, k):
        return self.layer * PER[name] + k + (1 if name == "x_done" else 0)

    def next(self, name, n=1):
        self.seen[name] = self.seen.get(name, 0) + n
        return self.value(name, self.seen[name])

    def load(self, u):
        return self.layer * PER["slot_loaded"] + 16 * (u // RING + 1)


def build(nc, a):
    ctx = ExitStack()
    with ctx:
        def sb(name, cols, dt=F32):
            return ctx.enter_context(nc.sbuf_tensor(name, [P, cols], dt))

        def sem(name):
            return ctx.enter_context(nc.semaphore(name))

        slot_loaded = [sem(f"slot{u}_loaded") for u in range(RING)]
        att_done = sem("att_done")
        att_mm = sem("att_mm")
        brT_done = sem("brT_done")
        brT_mm = sem("brT_mm")
        bsig_done = sem("bsig_done")
        cache_out = sem("cache_out")
        cb_done = sem("cb_done")
        cb_mm = sem("cb_mm")
        cin_done = sem("cin_done")
        cin_mm = sem("cin_mm")
        cln_done = sem("cln_done")
        combT_done = sem("combT_done")
        combT_mm = sem("combT_mm")
        comb_done = sem("comb_done")
        convT_mm = sem("convT_mm")
        conv_done = sem("conv_done")
        decay_mm = sem("decay_mm")
        down_mm = sem("down_mm")
        dve_chain = sem("dve_chain")
        egate_mm = sem("egate_mm")
        exp_done = sem("exp_done")
        final_chain = sem("final_chain")
        final_done = sem("final_done")
        final_g_loaded = sem("final_g_loaded")
        final_std = sem("final_std")
        final_sums = sem("final_sums")
        final_var = sem("final_var")
        g_mm = sem("g_mm")
        gate_mm = sem("gate_mm")
        gates_kept = [sem(f"gates_kept{i}") for i in range(STAGES)]
        gb_done = sem("gb_done")
        gelu_done = sem("gelu_done")
        gk_done = sem("gk_done")
        glu_done = sem("glu_done")
        gmlp_mm = sem("gmlp_mm")
        gramB_mm = sem("gramB_mm")
        gramK_mm = sem("gramK_mm")
        hT_act = sem("hT_act")
        hT_dve = sem("hT_dve")
        hT_mm = sem("hT_mm")
        hhi_done = sem("hhi_done")
        hi_done = sem("hi_done")
        hid_done = sem("hid_done")
        hlo_done = sem("hlo_done")
        hz_done = sem("hz_done")
        keys_ready = sem("keys_ready")
        lo_done = sem("lo_done")
        logits_read = sem("logits_read")
        lorT_done = sem("lorT_done")
        lorT_mm = sem("lorT_mm")
        lora_done = sem("lora_done")
        mix_done = sem("mix_done")
        modT_mm = sem("modT_mm")
        mixhi_done = sem("mixhi_done")
        mixlo_done = sem("mixlo_done")
        ohi_done = sem("ohi_done")
        olo_done = sem("olo_done")
        mod_mm = sem("mod_mm")
        mod_rows = sem("mod_rows")
        mod_scale_done = sem("mod_scale_done")
        modc_done = sem("modc_done")
        mrow_done = sem("mrow_done")
        mrow_mm = sem("mrow_mm")
        n_mm = sem("n_mm")
        nl_ready = sem("nl_ready")
        oA_done = sem("oA_done")
        oB_done = sem("oB_done")
        oC_done = sem("oC_done")
        pads_zeroed = sem("pads_zeroed")
        params_loaded = sem("params_loaded")
        pool_chain = sem("pool_chain")
        probsT_done = sem("probsT_done")
        probsT_mm = sem("probsT_mm")
        probs_done = sem("probs_done")
        proj_mm = sem("proj_mm")
        qT_done = sem("qT_done")
        qkT_mm = sem("qkT_mm")
        rope_done = sem("rope_done")
        route_exp = sem("route_exp")
        route_max = sem("route_max")
        router_mm = sem("router_mm")
        s0_done = sem("s0_done")
        sa_done = sem("sa_done")
        sa_mm = sem("sa_mm")
        scan_ready = sem("scan_ready")
        scores_mm = sem("scores_mm")
        sig_done = sem("sig_done")
        silu_c_done = sem("silu_c_done")
        silu_done = sem("silu_done")
        smax_done = sem("smax_done")
        ssq_done = sem("ssq_done")
        c_loaded = sem("c_loaded")
        constants_loaded = sem("constants_loaded")
        x_loaded = sem("x_loaded")
        state_ready = sem("state_ready")
        state_stored = sem("state_stored")
        std_ready = sem("std_ready")
        step_done = sem("step_done")
        step_mm = sem("step_mm")
        t_done = sem("t_done")
        tc_done = sem("tc_done")
        tildeT_act = sem("tildeT_act")
        tildeT_dve = sem("tildeT_dve")
        tildeT_mm = sem("tildeT_mm")
        tilde_done = sem("tilde_done")
        u_done = sem("u_done")
        u_mm = sem("u_mm")
        up_mm = sem("up_mm")
        var_ready = sem("var_ready")
        vn_done = sem("vn_done")
        wa_done = sem("wa_done")
        wa_mm = sem("wa_mm")
        wa_pre = sem("wa_pre")
        wb0_loaded = sem("wb0_loaded")
        wb1_loaded = sem("wb1_loaded")
        wout_mm = sem("wout_mm")
        x_back = sem("x_back")
        x_done = sem("x_done")
        x_kept = sem("x_kept")
        x_mm = sem("x_mm")
        xe_done = sem("xe_done")
        xf_done = sem("xf_done")
        xm_done = sem("xm_done")
        xn_done = sem("xn_done")
        xo_done = sem("xo_done")
        y_mm = sem("y_mm")
        y_stored = sem("y_stored")
        z_act = sem("z_act")
        z_dve = sem("z_dve")
        z_mm = sem("z_mm")
        zhi_done = sem("zhi_done")
        zlo_done = sem("zlo_done")
        waits_settled = sem("waits_settled")

        def next_at():
            return -(-nc.sbuf_base // 32) * 32

        x_at = next_at()
        Xt = sb("x", NB * D)
        h_at = next_at()
        Ht = sb("h", KT * TOK)
        ring_at = next_at()
        ring = sb("ring", RING * SLOT)
        arena_at = next_at()
        arena = sb("arena", 20480)
        cols = sb("cols", NCOLS)
        rows_at = next_at()
        rows = sb("rows", NROWS)
        fix = sb("fix", NFIX)
        scanf = sb("scan_sums", NSCANF)
        scanb = sb("scan_masks", NSCANB)
        mbc_at = next_at()
        mbc_t = sb("mod_rows", 2 * D)
        modc_t = sb("mod_cols", 96)
        sml = sb("small", 640)
        ps = ctx.enter_context(nc.psum_tensor("ps", [P, 4096], F32))

        x = Xt[:, :].rearrange("p (b d) -> p b d", b=NB)
        h = Ht[:, :].rearrange("p (k t) -> p k t", k=KT)

        def bank(b, n=512):
            return ps[:, b * 512:b * 512 + n]

        def col(name):
            o, n = COLS[name]
            return cols[:, o:o + n]

        def row(name):
            o, n = ROWS[name]
            return rows[:, o:o + n]

        def fixed(name):
            o, n = FIX[name]
            return fix[:, o:o + n]

        ident = fixed("ident")

        zab = arena[:, 0:NB * 1024].rearrange("p (b c) -> p b c", b=NB)
        zc = arena[:, 5120:5120 + NB * 768].rearrange("p (b c) -> p b c", b=NB)
        zl = arena[:, 8960:8960 + NB * 384].rearrange("p (b c) -> p b c", b=NB)
        lorT = arena[:, 8960:8960 + 3 * TOK].rearrange("p (g t) -> p g t", g=3)
        zd = arena[:, 10880:10880 + NB * 512].rearrange("p (b c) -> p b c", b=NB)
        brT = arena[:, 13440:13440 + 8 * TOK].rearrange("p (k t) -> p k t", k=8)
        stage = arena[:, 18560:18560 + STAGES * HALF].rearrange("p (i t) -> p i t", i=STAGES)
        xn = arena[:, 0:NB * D].rearrange("p (b d) -> p b d", b=NB)
        wb = arena[:, 0:8192].rearrange("p (f n k c) -> p f n k c", f=KT, n=4, k=2)
        mixT = arena[:, 8192:8192 + KT * TOK].rearrange("p (k t) -> p k t", k=KT)
        def split(name, at, n):
            return nc.alloc_sbuf_tensor_at(name, [P, n], F32R, offset=at)

        w_hi = split("w_hi", arena_at, SLOT)[:, :]
        w_lo = split("w_lo", ring_at, RING * SLOT)[:, :]
        hz_hi = split("hz_hi", x_at, KT * TOK)[:, :].rearrange("p (k t) -> p k t", k=KT)
        hz_lo = split("hz_lo", arena_at + 4 * 13312, KT * TOK)[:, :].rearrange("p (k t) -> p k t", k=KT)
        wz_hi = [split("wz_hi0", mbc_at, SLOT // 2)[:, :], split("wz_hi1", arena_at + 4 * 18432, SLOT // 2)[:, :]]
        mix_hi = split("mix_hi", h_at, KT * TOK)[:, :].rearrange("p (k t) -> p k t", k=KT)
        mix_lo = split("mix_lo", arena_at + 4 * 8192, KT * TOK)[:, :].rearrange("p (k t) -> p k t", k=KT)
        wo_hi = [split("wo_hi0", rows_at, SLOT // 2)[:, :], split("wo_hi1", arena_at + 4 * 13440, SLOT // 2)[:, :]]
        h_hi = split("h_hi", arena_at + 4 * 5120, KT * TOK)[:, :].rearrange("p (k t) -> p k t", k=KT)
        h_lo = split("h_lo", h_at, KT * TOK)[:, :].rearrange("p (k t) -> p k t", k=KT)
        hid_hi = split("hid_hi", arena_at + 4 * 10240, KT * TOK)[:, :].rearrange("p (k t) -> p k t", k=KT)
        hid_lo = split("hid_lo", arena_at + 4 * 15360, KT * TOK)[:, :].rearrange("p (k t) -> p k t", k=KT)
        cin = [Xt[:, f * LINE:(f + 1) * LINE] for f in range(FT)]
        cacc = [Xt[:, 1400 + f * OUTS:1400 + (f + 1) * OUTS] for f in range(FT)]
        qkr = Xt[:, 0:NB * 384].rearrange("p (b c) -> p b c", b=NB)
        qT = Xt[:, 1920:1920 + 2 * TOK].rearrange("p (g t) -> p g t", g=2)
        kTz = Xt[:, 3200:3200 + 2 * (P + TOK)].rearrange("p (g t) -> p g t", g=2)
        sc = arena[:, 0:2048].rearrange("p (h s) -> p h s", h=4)
        pT = arena[:, 2048:4096].rearrange("p (s h q) -> p s h q", s=4, h=4)
        ropet = mbc_t[:, 0:LAT * 384].rearrange("p (b c) -> p b c", b=LAT)
        gb = Xt[:, 0:2048].rearrange("p (g e t) -> p g e t", g=8, e=2)
        gk = Xt[:, 2048:4096].rearrange("p (g e t) -> p g e t", g=8, e=2)
        nl = Xt[:, 4096:5120].rearrange("p (g t) -> p g t", g=8)
        Tc = arena[:, 0:512].rearrange("p (g t) -> p g t", g=8)
        Xc = arena[:, 512:1024].rearrange("p (g t) -> p g t", g=8)
        TTc = arena[:, 19840:19840 + 512].rearrange("p (g t) -> p g t", g=8)
        TT = arena[:, 1024:2048].rearrange("p (g t) -> p g t", g=8)
        Xm = arena[:, 2048:3072].rearrange("p (g t) -> p g t", g=8)
        ar = arena[:, 3072:5120].rearrange("p (g r e t) -> p g r e t", g=4, r=2, e=2)
        bT = arena[:, 10880:10880 + 512].rearrange("p (g t) -> p g t", g=4)
        kT = arena[:, 11392:11392 + 512].rearrange("p (g t) -> p g t", g=4)
        sw = arena[:, 11904:11904 + 512].rearrange("p (d c) -> p d c", d=2)
        aa = arena[:, 12416:12416 + 512].rearrange("p (d c) -> p d c", d=2)
        kks = arena[:, 12928:12928 + 512].rearrange("p (d c) -> p d c", d=2)
        rt = mbc_t[:, 0:512].rearrange("p (d c) -> p d c", d=2)
        at_ = mbc_t[:, 512:1024].rearrange("p (d c) -> p d c", d=2)
        bt = mbc_t[:, 1024:1536].rearrange("p (d c) -> p d c", d=2)
        kt_ = mbc_t[:, 1536:2048].rearrange("p (d c) -> p d c", d=2)
        ub = nl[:, 0:4, :].rearrange("p a t -> p (a t)").rearrange("p (g v) -> p g v", g=8)
        sa = nl[:, 4:8, :].rearrange("p a t -> p (a t)").rearrange("p (g v) -> p g v", g=8)
        y = brT[:, 4:6, :].rearrange("p k t -> p (k t)").rearrange("p (b c) -> p b c", b=NB)
        sil = rows[:, 0:640].rearrange("p (i t) -> p i t", i=2)
        cbs = rows[:, 640:640 + 1280].rearrange("p (i t) -> p i t", i=2)
        mrow = mbc_t[:, :].rearrange("p (g d) -> p g d", g=2)
        modc = modc_t[:, :].rearrange("p (j g) -> p j g", g=2)

        off = [0]

        def small(n):
            off[0] += n
            assert off[0] <= 640
            return sml[:, off[0] - n:off[0]]

        cS = small(16).rearrange("p (k g) -> p k g", g=2)
        A1 = small(16).rearrange("p (k g) -> p k g", g=2)
        ssq, rstd = small(NB), small(NB)
        stats, mv = small(NB * 6), small(NB * 2)
        mx, smx, rsm, snk = small(4), small(4), small(4), small(4)
        kss = small(8)
        bon = small(NB * 8).rearrange("p (b d h) -> p b d h", b=NB, d=2)
        S = sb("scan_state", 256)[:, :].rearrange("p (g v) -> p g v", g=4)
        S0 = sb("scan_state_scaled", 256)[:, :].rearrange("p (g v) -> p g v", g=4)
        gm = small(8).rearrange("p (g e) -> p g e", g=4)
        gst = small(20)
        gs2 = small(20)
        lg = small(100).rearrange("p (b e) -> p b e", b=NB)
        t20 = small(20).rearrange("p (b e) -> p b e", b=NB)
        gsel = small(20).rearrange("p (b e) -> p b e", b=NB)
        t16 = small(80).rearrange("p (b g e) -> p b g e", b=NB, g=4)
        ein = small(20).rearrange("p (b e) -> p b e", b=NB)
        oh1 = small(20).rearrange("p (b e) -> p b e", b=NB)
        oh2 = small(20).rearrange("p (b e) -> p b e", b=NB)
        m1, m2_, gw, ix = small(NB), small(NB), small(NB), small(NB)
        comb = arena[:, 4096:4096 + NB * P].rearrange("p (b e) -> p b e", b=NB)
        combT_t = sb("combT", TOK)
        combT = combT_t[:, :]

        state_out = sb("scan_state_out", 256)[:, :].rearrange("p (g v) -> p g v", g=4)
        def half_of(ap, v):
            at = (AT_UP + v // 2) % RING * SLOT + v % 2 * (SLOT // 2)
            return ap[:, at:at + SLOT // 2]

        def half_in(ap, v, first=AT_IN):
            at = (first + v // 2) % RING * SLOT + v % 2 * (SLOT // 2)
            return ap[:, at:at + SLOT // 2]

        def hi_of(v):
            return w_hi[:, v % 2 * (SLOT // 2):(v % 2 + 1) * (SLOT // 2)]

        mod_row = combT_t[0:2, 0:512]
        gates_dram = nc.dram_tensor("gates", [KT, P, 4 * TOK], F32, kind="Internal").ap()
        x_kept_dram = nc.dram_tensor("x_kept", [P, NB * D], F32, kind="Internal").ap()

        def slot(u):
            return ring[:, (u % RING) * SLOT:(u % RING + 1) * SLOT].rearrange("p (k c) -> p k c", k=KT)

        def over(ap, at, n):
            v = ap.unsqueeze(at)
            return v.broadcast_to([n if i == at else c for i, c in enumerate(v.shape)])

        block = ctx.enter_context(nc.Block())

        def z_copies(g, copy):
            j, b = g // NB, g % NB
            parts = {0: [(0, 512, zab, 0)], 1: [(0, 512, zab, 512)], 2: [(0, 512, zc, 0)],
                     3: [(0, 256, zc, 512), (256, 256, zl, 0)], 4: [(0, 128, zl, 256), (128, 384, zd, 0)],
                     5: [(0, 128, zd, 384)]}[j]
            for at, n, dst, to in parts:
                ins = copy(dst[:, b, to:to + n], bank(g % 8)[:, at:at + n])
            return ins

        @block.sync
        def _(sp):
            now = Place()

            def load(u):
                if AT_BACK <= u < AT_OUT:
                    return sp.dma_start(ring[:, (u % RING) * SLOT:(u % RING) * SLOT + 4 * TOK], gates_dram[u - AT_BACK])
                at = u if u < AT_BACK else u - SLOTS_BACK
                src = a["stream"][bass.ds(now.layer * (SLOTS - SLOTS_BACK) + at, 1)].rearrange("o p c -> (o p) c")
                return sp.dma_start(ring[:, (u % RING) * SLOT:(u % RING + 1) * SLOT], src)

            for u in range(RING):
                load(u).then_inc(slot_loaded[u], 16)
            with sp.Fori(0, DEPTH) as layer:
                now.layer = layer
                u = RING
                for _ in range(SLOTS_MOD):
                    sp.wait_ge(mod_mm, now.next("mod_mm"))
                    load(u).then_inc(slot_loaded[u % RING], 16)
                    u += 1
                for _ in range(SLOTS_IN):
                    sp.wait_ge(z_mm, now.next("z_mm", 2 * NB))
                    load(u).then_inc(slot_loaded[u % RING], 16)
                    u += 1
                for f in range(KT):
                    sp.wait_ge(mod_mm, now.next("mod_mm"))
                    load(u).then_inc(slot_loaded[u % RING], 16)
                    u += 1
                    for i in range(8 * f, 8 * f + 8):
                        sp.wait_ge(sig_done, now.next("sig_done", 2))
                        at = i % 8 * HALF
                        sp.dma_start(gates_dram[f, :, at:at + HALF], stage[:, i % STAGES]).then_inc(gates_kept[i % STAGES], 16)
                    if u >= AT_BACK:
                        for i in range(STAGES):
                            sp.wait_ge(gates_kept[i], now.value("gates_kept", 16 * 2 * (u - AT_BACK + 1)))
                            sp.sem_inc(waits_settled, 1)
                    load(u).then_inc(slot_loaded[u % RING], 16)
                    u += 1
                for f in range(KT):
                    sp.wait_ge(mix_done, now.next("mix_done", 4))
                    sp.sem_inc(waits_settled, 1)
                    if u < AT_OUT:
                        for i in range(STAGES):
                            sp.wait_ge(gates_kept[i], now.value("gates_kept", 16 * 2 * (u - AT_BACK + 1)))
                            sp.sem_inc(waits_settled, 1)
                    load(u).then_inc(slot_loaded[u % RING], 16)
                    u += 1
                for _ in range(SLOTS_OUT):
                    sp.wait_ge(wout_mm, now.next("wout_mm", NB))
                    load(u).then_inc(slot_loaded[u % RING], 16)
                    u += 1
                for _ in range(SLOTS_UP + SLOTS_DOWN):
                    name, k = use_of_half(2 * (u - RING - AT_UP) + 1)
                    sp.wait_ge(up_mm if name == "up_mm" else down_mm, now.value(name, k))
                    load(u).then_inc(slot_loaded[u % RING], 16)
                    u += 1
            for u in range(RING):
                sp.wait_ge(slot_loaded[u], 16 * (DEPTH * SLOTS // RING + 1))

        @block.gpsimd
        def _(pool):
            now = Place()
            pool.dma_start(Xt[:, :], a["x"]).then_inc(x_loaded, 16)
            with pool.Fori(0, DEPTH) as layer:
                now.layer = layer
                pool.wait_ge(x_done, now.value("x_done", 0))
                pick = bass.ds(layer, 1)
                pool.sem_inc(waits_settled, 1)
                pool.dma_start(cols[:, :], a["cols"][pick].rearrange("o p c -> (o p) c")).then_inc(params_loaded, 16)
                pool.dma_start(rows[:, :], a["rows"][pick].rearrange("o p c -> (o p) c").broadcast_to([P, NROWS])).then_inc(params_loaded, 16)
                pool.wait_ge(z_act, now.next("z_act", 15))
                pool.wait_ge(z_dve, now.next("z_dve", 15))
                pool.sem_inc(waits_settled, 1)
                for f in range(FT):
                    for at, n in ((0, PAD), (PAD + P, PAD), (LINE - PAD, PAD)):
                        ins = nc.gpsimd.memset(cin[f][:, at:at + n], 0.0)
                ins.then_inc(pads_zeroed, 1)
                pool.sem_inc(waits_settled, 1)
                nc.gpsimd.memset(kTz, 0.0).then_inc(pool_chain, 1)
                pool.wait_ge(pool_chain, now.next("pool_chain"))
                pool.wait_ge(params_loaded, now.next("params_loaded", 32))
                pool.sem_inc(waits_settled, 1)
                nc.gpsimd.tensor_copy(kTz[0:64, 0, 0:P], col("ckT")[0:64, :])
                nc.gpsimd.tensor_copy(kTz[64:128, 1, 0:P], col("ckT")[64:128, :]).then_inc(keys_ready, 1)
                pool.sem_inc(waits_settled, 1)
                pool.dma_start(a["new_k"][pick].rearrange("o p c -> (o p) c"), zd[:, 0, 256:384]).then_inc(cache_out, 16)
                pool.dma_start(a["new_v"][pick].rearrange("o p c -> (o p) c"), zd[:, 0, 384:512]).then_inc(cache_out, 16)
                pool.wait_ge(cache_out, now.next("cache_out", 32))
                pool.wait_ge(brT_done, now.next("brT_done", 3))
                pool.sem_inc(waits_settled, 1)
                nc.gpsimd.memset(Xm, 0.0).then_inc(pool_chain, 1)
                pool.wait_ge(pool_chain, now.next("pool_chain"))
                pool.sem_inc(waits_settled, 1)
                nc.gpsimd.memset(ar[0:64, :, 1], 0.0)
                nc.gpsimd.memset(ar[64:128, :, 0], 0.0).then_inc(scan_ready, 1)
                pool.wait_ge(constants_loaded, 3 * 16)
                for s, blocks in enumerate(STEPS):
                    pool.wait_ge(gb_done, now.next("gb_done"))
                    for lev in range(LEVELS - 1):
                        if lev:
                            pool.wait_ge(x_mm, now.next("x_mm"))
                        for d in range(2):
                            o = SCANB["lev"][0] + (lev * 2 + d) * P
                            ins = nc.gpsimd.tensor_tensor(nl[:, 4 * d:4 * d + 4], gb[:, 4 * d:4 * d + 4, 0, :],
                                                          over(scanb[:, o:o + P], 1, 4), ALU.mult)
                        ins.then_inc(nl_ready, 1)
                    pool.wait_ge(x_mm, now.next("x_mm"))
                    if s == 0:
                        pool.wait_ge(state_ready, now.next("state_ready"))
                        pool.sem_inc(waits_settled, 1)
                        pool.dma_start(a["new_s"][pick].rearrange("o p c -> (o p) c"),
                                                            state_out.rearrange("p g v -> p (g v)")).then_inc(state_stored, 16)
                        pool.wait_ge(state_stored, now.next("state_stored", 16))
                pool.wait_ge(brT_done, now.next("brT_done"))
                pool.sem_inc(waits_settled, 1)
                wbranch = a["wbranch"][pick].rearrange("o p c -> (o p) c")
                pool.dma_start(arena[:, 0:1024], wbranch[:, 0:1024]).then_inc(wb0_loaded, 16)
                pool.dma_start(arena[:, 1024:8192], wbranch[:, 1024:8192]).then_inc(wb1_loaded, 16)
                pool.dma_start(Xt[:, :], x_kept_dram).then_inc(x_back, 16)
                pool.wait_ge(hhi_done, now.next("hhi_done"))
                for b in range(NB):
                    bs = slice(b * P, (b + 1) * P)
                    pool.wait_ge(router_mm, now.next("router_mm"))
                    ins = nc.gpsimd.tensor_tensor(h_lo[:, :, bs], h[:, :, bs], h_hi[:, :, bs].bitcast(F32), ALU.subtract)
                ins.then_inc(hlo_done, 1)
            pool.wait_ge(x_done, 1 + DEPTH * PER["x_done"])
            pool.dma_start(arena[:, 10240:10240 + D], a["final_g"].broadcast_to([P, D])).then_inc(final_g_loaded, 16)
            pool.wait_ge(final_done, 1)
            yv = arena[:, 0:NB * D].rearrange("p (b d) -> p b d", b=NB)
            pool.dma_start(a["y_prompt"], yv[:, 0]).then_inc(y_stored, 16)
            pool.dma_start(a["y_sample"].rearrange("(b p) d -> p b d", p=P), yv[:, 1:NB]).then_inc(y_stored, 16)
            pool.wait_ge(y_stored, 32)

        @block.tensor
        def _(pe):
            now = Place()

            def mm(out, lhsT, rhs, start=True, stop=True):
                return nc.tensor.matmul(out, lhsT, rhs, start=start, stop=stop)

            def transpose(out, in_):
                return nc.tensor.transpose(out, in_, ident)

            def h_transposes():
                pe.wait_ge(xn_done, now.next("xn_done", NB))
                for f in range(KT):
                    if f >= 4:
                        if f % 2 == 0:
                            pe.wait_ge(hT_act, now.next("hT_act"))
                        else:
                            pe.wait_ge(hT_dve, now.next("hT_dve"))
                    for b in range(NB):
                        ins = transpose(ps[:, 1024 * (f % 4) + b * P:1024 * (f % 4) + (b + 1) * P], xn[:, b, f * P:(f + 1) * P])
                    ins.then_inc(hT_mm, 1)
                pe.wait_ge(hT_act, now.next("hT_act", 2))
                pe.wait_ge(hT_dve, now.next("hT_dve", 2))

            def branch_transposes(src):
                for f in range(FT):
                    for b in range(NB):
                        ins = transpose(ps[:, 2048 + 1024 * f + b * P:2048 + 1024 * f + (b + 1) * P], src[:, b, f * P:(f + 1) * P])
                ins.then_inc(brT_mm, 1)

            def mod_row_products(j0):
                for g in range(2):
                    for f in range(KT):
                        ins = mm(ps[:, 2048 + g * D + f * P:2048 + g * D + (f + 1) * P],
                                 modc[:, j0 + f, g:g + 1].broadcast_to([P, P]), ident)
                ins.then_inc(mrow_mm, 1)

            def banks_left(n):
                if counted("gate", n):
                    pe.wait_ge(sig_done, now.value("sig_done", 2 * counted("gate", n)))
                pe.wait_ge(mod_rows, now.value("mod_rows", SLOTS_MOD + counted("rows", n)))
                pe.wait_ge(modc_done, now.value("modc_done", SLOTS_MOD + counted("cols", n)))

            def mod_rows_products(i, u, bk, ks):
                for k in ks:
                    ins = mm(bank(bk)[0:2, :], cS[:, k, :], slot(u)[:, k, :], k == 0, k == KT - 1)
                return ins

            def mod_columns(i, bk):
                pe.wait_ge(mod_rows, now.value("mod_rows", i + 1))
                for j in range(4):
                    ins = mm(bank(bk)[:, 2 * j:2 * j + 2], mod_row[:, j * P:(j + 1) * P], ident[0:2, 0:2])
                ins.then_inc(modT_mm, 1)

            def bank_left(what, i):
                if what == "rows":
                    pe.wait_ge(sig_done, now.value("sig_done", 2 * (8 * (i - SLOTS_MOD) - 1)))
                elif i % 8 == 1:
                    pe.wait_ge(modc_done, now.value("modc_done", SLOTS_MOD + i // 8 + 1))
                elif i >= 2:
                    pe.wait_ge(sig_done, now.value("sig_done", 2 * (i - 1)))

            def behind(lo, hi):
                for what, i, part, bk in PARTS[lo:hi]:
                    ks = range(4 * part, 4 * part + 4)
                    if what == "cols":
                        mod_columns(i, bk)
                        continue
                    f = i - SLOTS_MOD if what == "rows" else i // 8
                    u = AT_BEHIND + 2 * f + (what == "gate")
                    if part == 0:
                        pe.wait_ge(slot_loaded[u % RING], now.load(u))
                        if (what, i) != ("rows", SLOTS_MOD):
                            bank_left(what, i)
                    if what == "rows":
                        ins = mod_rows_products(i, u, bk, ks)
                        if part:
                            ins.then_inc(mod_mm, 1)
                    else:
                        n, at = i % 8 // 2, i % 2 * HALF
                        for k in ks:
                            ins = mm(bank(bk, HALF), slot(u)[:, k, n * P:(n + 1) * P], h[:, k, at:at + HALF], k == 0, k == KT - 1)
                        ins.then_inc(gate_mm, 1)

            pe.wait_ge(silu_c_done, 1)
            with pe.Fori(0, DEPTH) as layer:
                now.layer = layer
                pe.wait_ge(x_done, now.value("x_done", 0))
                pe.wait_ge(slot_loaded[0], now.load(0))
                mod_rows_products(0, 0, 4, range(KT)).then_inc(mod_mm, 1)
                for i in range(1, SLOTS_MOD):
                    pe.wait_ge(slot_loaded[i % RING], now.load(i))
                    mod_rows_products(i, i, 4 + i, range(KT)).then_inc(mod_mm, 1)
                    pe.wait_ge(constants_loaded, 3 * 16)
                    mod_columns(i - 1, 3 + i)
                mod_columns(SLOTS_MOD - 1, 3 + SLOTS_MOD)
                pe.wait_ge(modc_done, now.value("modc_done", SLOTS_MOD))
                h_transposes()
                pe.wait_ge(hz_done, now.next("hz_done"))
                for j in range(SLOTS_IN):
                    n = 512 if j < SLOTS_IN - 1 else P
                    for half in range(2):
                        pe.wait_ge(zlo_done, now.next("zlo_done"))
                        w_parts = [t.rearrange("p (k c) -> p k c", k=4)[:, :, 0:n] for t in (wz_hi[half], half_in(w_lo, 2 * j + half))]
                        for b in range(NB):
                            g = j * NB + b
                            if g >= 8 and half == 0:
                                if g % 2 == 0:
                                    pe.wait_ge(z_act, now.next("z_act"))
                                else:
                                    pe.wait_ge(z_dve, now.next("z_dve"))
                            for k in range(4):
                                kt, bs = 4 * half + k, slice(b * P, (b + 1) * P)
                                mm(bank(g % 8, n), hz_hi[:, kt, bs], w_parts[0][:, k], kt == 0, False)
                                mm(bank(g % 8, n), hz_hi[:, kt, bs], w_parts[1][:, k], False, False)
                                ins = mm(bank(g % 8, n), hz_lo[:, kt, bs], w_parts[0][:, k], False, kt == KT - 1)
                            if half:
                                ins.then_inc(z_mm, 2)
                pe.wait_ge(z_act, now.next("z_act", 4))
                pe.wait_ge(z_dve, now.next("z_dve", 4))
                behind(0, closed(CONV_AT))
                pe.wait_ge(vn_done, now.next("vn_done"))
                wsT = col("wsT").rearrange("p (g t) -> p g t", g=4)
                for g in range(4):
                    ins = mm(bank(g, NB * HD).rearrange("p (b c) -> p b c", b=NB), wsT[:, g], zab[:, :, 256 + g * HD:256 + (g + 1) * HD])
                ins.then_inc(gmlp_mm, 1)
                pe.wait_ge(oA_done, now.next("oA_done"))
                banks_left(closed(CONV_AT))
                branch_transposes(zab[:, :, 0:256])
                pe.wait_ge(glu_done, now.next("glu_done"))
                for f in range(FT):
                    for b in range(NB):
                        ins = transpose(ps[:, 1024 * f + b * P:1024 * f + (b + 1) * P], zab[:, b, 512 + f * P:512 + (f + 1) * P])
                ins.then_inc(cin_mm, 1)
                pe.wait_ge(brT_done, now.next("brT_done"))
                behind(closed(CONV_AT), closed(LN_AT))
                pe.wait_ge(conv_done, now.next("conv_done"))
                for b in range(NB):
                    at = 0 if b == 0 else LAT_OUT + (b - 1) * P
                    for f in range(FT):
                        ins = transpose(ps[:, b * W + f * P:b * W + (f + 1) * P], cacc[f][:, at:at + P])
                ins.then_inc(convT_mm, 1)
                behind(closed(LN_AT), closed(ATT_AT))
                pe.wait_ge(oB_done, now.next("oB_done"))
                banks_left(closed(ATT_AT))
                branch_transposes(zab[:, :, 512:768])
                pe.wait_ge(rope_done, now.next("rope_done"))
                pe.wait_ge(brT_done, now.next("brT_done"))
                for g in range(3):
                    for b in range(NB):
                        src = zd[:, 0] if b == 0 else qkr[:, b]
                        ins = transpose(ps[:, 1024 * g + b * P:1024 * g + (b + 1) * P], src[:, g * P:(g + 1) * P])
                ins.then_inc(qkT_mm, 1)
                pe.wait_ge(qT_done, now.next("qT_done"))

                def scores(b):
                    lo, hi = (0, 0) if b == 0 else (max(1, b - 1), min(LAT, b + 1))
                    nband = (hi - lo + 1) * P
                    for hd in range(4):
                        q = qT[:, hd % 2, b * P:(b + 1) * P]
                        o = 0 if b == 0 else P
                        if b:
                            mm(bank(hd)[:, 0:P], q, kTz[:, hd // 2, 0:P])
                        ins = mm(bank(hd)[:, o:o + nband], q, kTz[:, hd // 2, P + lo * P:P + lo * P + nband])
                    ins.then_inc(scores_mm, 1)
                    return ([] if b == 0 else [None]) + list(range(lo, hi + 1))

                segs = scores(0)
                for b in range(NB):
                    part = ATT_AT + b * ATT_PARTS
                    behind(closed(part), closed(part + 3))
                    pe.wait_ge(probs_done, now.next("probs_done"))
                    for s in range(len(segs)):
                        for hd in range(4):
                            ins = transpose(bank(s)[:, hd * P:(hd + 1) * P], sc[:, hd, s * P:(s + 1) * P])
                    ins.then_inc(probsT_mm, 1)
                    behind(closed(part + 3), closed(part + 5))
                    pe.wait_ge(probsT_done, now.next("probsT_done"))
                    if b:
                        pe.wait_ge(att_done, now.next("att_done"))
                    for hd in range(4):
                        for s, blk in enumerate(segs):
                            kv = hd // 2
                            v = col("cv")[:, kv * HD:(kv + 1) * HD] if blk is None else zd[:, blk, 384 + kv * HD:384 + (kv + 1) * HD]
                            ins = mm(bank(4)[:, hd * HD:(hd + 1) * HD], pT[:, s, hd, :], v, s == 0, s == len(segs) - 1)
                    ins.then_inc(att_mm, 1)
                    if b < NB - 1:
                        segs = scores(b + 1)
                pe.wait_ge(att_done, now.next("att_done"))
                banks_left(closed(SCAN_AT))
                branch_transposes(zd[:, :, 0:256])
                pe.wait_ge(lora_done, now.next("lora_done"))
                pe.wait_ge(brT_done, now.next("brT_done"))
                for g in range(3):
                    for b in range(NB):
                        ins = transpose(ps[:, 1024 * g + b * P:1024 * g + (b + 1) * P], zl[:, b, g * P:(g + 1) * P])
                ins.then_inc(lorT_mm, 1)
                pe.wait_ge(lorT_done, now.next("lorT_done"))
                pe.wait_ge(scan_ready, now.next("scan_ready"))
                for s, blocks in enumerate(STEPS):
                    part = SCAN_AT + s * STEP_PARTS
                    for i, w in enumerate(("w2", "a2")):
                        for d, blk in enumerate(blocks):
                            ins = mm(bank(4 + i)[:, d * W:(d + 1) * W], lorT[:, i, blk * P:(blk + 1) * P], col(w)[:, d * W:(d + 1) * W])
                    ins.then_inc(wa_mm, 1)
                    behind(closed(part), part + WA_PARTS)
                    pe.wait_ge(wa_done, now.next("wa_done"))
                    for i, name in enumerate(("incl", "excl")):
                        for d in range(2):
                            o = SCANF[name][0] + d * P
                            mm(bank(2 + i)[:, d * W:(d + 1) * W], scanf[:, o:o + P], sw[:, d, :])
                    o = SCANF["halves"][0]
                    for g in range(4):
                        ins = mm(bank(4)[:, 2 * g:2 * g + 2], sw[:, g // 2, (g % 2) * P:(g % 2 + 1) * P], scanf[:, o:o + 2])
                    ins.then_inc(decay_mm, 1)
                    behind(part + WA_PARTS, closed(part + 5))
                    pe.wait_ge(tilde_done, now.next("tilde_done"))
                    for i, src in enumerate((at_, rt, bt, kt_)):
                        for g in range(4):
                            ins = transpose(bank(i)[:, g * P:(g + 1) * P], src[:, g // 2, (g % 2) * P:(g % 2 + 1) * P])
                    ins.then_inc(tildeT_mm, 1)
                    behind(closed(part + 5), closed(part + 6))
                    pe.wait_ge(tildeT_act, now.next("tildeT_act"))
                    pe.wait_ge(tildeT_dve, now.next("tildeT_dve"))
                    for half, src, made in ((0, bT, gramB_mm), (2048, kT, gramK_mm)):
                        if made is gramK_mm:
                            banks_left(closed(part + 6))
                        for g in range(4):
                            for par in range(2):
                                o = half + (2 * g + par) * 256
                                ins = mm(ps[:, o:o + 256].rearrange("p (e t) -> p e t", e=2), src[:, g], ar[:, g, par])
                        ins.then_inc(made, 1)
                    pe.wait_ge(gb_done, now.next("gb_done"))
                    for g in range(4):
                        for par in range(2):
                            o = (2 * g + par) * P
                            ins = mm(ps[:, o:o + P], ar[:, g, par, 0, :], bT[:, g])
                    ins.then_inc(n_mm, 1)
                    pe.wait_ge(gk_done, now.next("gk_done"))
                    behind(closed(part + 6), part + 8)
                    for lev in range(LEVELS - 1):
                        pe.wait_ge(t_done, now.next("t_done"))
                        pe.wait_ge(nl_ready, now.next("nl_ready"))
                        for g in range(8):
                            ins = mm(bank(0)[:, g * HD:(g + 1) * HD], nl[:, g], Tc[:, g])
                        ins.then_inc(x_mm, 1)
                        lo, mid, hi = level_parts(part, lev)
                        behind(lo, mid)
                        pe.wait_ge(xm_done, now.next("xm_done"))
                        if lev < LEVELS - 2:
                            for g in range(8):
                                mm(bank(2)[:, g * HD:(g + 1) * HD], TT[:, g], Xc[:, g])
                            pe.wait_ge(xf_done, now.next("xf_done"))
                            pe.wait_ge(tc_done, now.next("tc_done"))
                            for g in range(8):
                                ins = mm(bank(3)[:, g * HD:(g + 1) * HD], Xm[:, g], TTc[:, g])
                        else:
                            pe.wait_ge(tc_done, now.next("tc_done"))
                            pe.sem_inc(waits_settled, 1)
                            for g in range(8):
                                early, late = (slice(0, 64), slice(64, P)) if g < 4 else (slice(64, P), slice(0, 64))
                                ins = mm(bank(3)[early, g * HD:(g + 1) * HD], Xc[late, g], TTc[late, g])
                        ins.then_inc(y_mm, 1)
                        behind(mid, hi)
                    pe.wait_ge(t_done, now.next("t_done"))
                    pe.wait_ge(s0_done, now.next("s0_done"))

                    def v_of(g8):
                        hd = g8 % 4
                        return zc[:, blocks[g8 // 4], 512 + hd * HD:512 + (hd + 1) * HD]

                    for g in range(8):
                        mm(bank(2)[:, g * HD:(g + 1) * HD], ar[:, g // 2, g % 2, 0, :], S0[:, g // 2], True, False)
                        ins = mm(bank(2)[:, g * HD:(g + 1) * HD], gk[:, g, 0, :], v_of(g), False, True)
                    ins.then_inc(u_mm, 1)
                    pe.wait_ge(u_done, now.next("u_done"))
                    for g in range(8):
                        ins = mm(bank(3)[:, g * HD:(g + 1) * HD], TT[:, g], ub[:, g])
                    ins.then_inc(sa_mm, 1)
                    pe.wait_ge(sa_done, now.next("sa_done"))
                    for g in range(8):
                        o = bank(0)[:, g * HD:(g + 1) * HD]
                        mm(o, ar[:, g // 2, g % 2, 1, :], S0[:, g // 2], True, False)
                        mm(o, gb[:, g, 1, :], sa[:, g], False, False)
                        mm(o, gk[:, g, 1, :], v_of(g), False, True)
                    for g in range(8):
                        d, par, hd = g // 4, g % 2, g % 4
                        o = ps[par * 64:(par + 1) * 64, 512 + (g // 2) * HD:512 + (g // 2 + 1) * HD]
                        mm(o, bt[:, d, hd * HD:(hd + 1) * HD], sa[:, g], True, False)
                        ins = mm(o, kt_[:, d, hd * HD:(hd + 1) * HD], v_of(g), False, True)
                    ins.then_inc(step_mm, 1)
                pe.wait_ge(step_done, now.next("step_done", len(STEPS)))
                for b in range(NB):
                    ins = mm(ps[:, b * W:(b + 1) * W], lorT[:, 2, b * P:(b + 1) * P], col("g2"))
                ins.then_inc(g_mm, 1)
                behind(closed(NORM_AT), len(PARTS))
                pe.wait_ge(oC_done, now.next("oC_done"))
                pe.wait_ge(sig_done, now.value("sig_done", 2 * PIECES))
                pe.wait_ge(modc_done, now.value("modc_done", MODS))
                branch_transposes(y)
                pe.wait_ge(brT_done, now.next("brT_done"))
                pe.wait_ge(wb0_loaded, now.next("wb0_loaded", 16))
                for f in range(KT):
                    if f == 1:
                        pe.wait_ge(wb1_loaded, now.next("wb1_loaded", 16))
                    for n in range(4):
                        unit = 4 * f + n
                        if unit >= 4:
                            pe.wait_ge(mix_done, now.next("mix_done"))
                        o = 1024 * (unit % 4)
                        for k in range(FT):
                            for lo, hi in ((0, 512), (512, TOK)):
                                ins = mm(ps[:, o + lo:o + hi], wb[:, f, n, k, :], brT[:, 2 * n + k, lo:hi], k == 0, k == FT - 1)
                        ins.then_inc(proj_mm, 1)
                pe.wait_ge(mix_done, now.next("mix_done", 4))
                mod_row_products(2 * KT)
                pe.wait_ge(mixlo_done, now.next("mixlo_done", KT))
                for c in range(SLOTS_OUT):
                    for half in range(2):
                        pe.wait_ge(olo_done, now.next("olo_done"))
                        w_parts = [t.rearrange("p (k c) -> p k c", k=4) for t in (wo_hi[half], half_in(w_lo, 2 * c + half, AT_OUT))]
                        for b in range(NB):
                            g = c * NB + b
                            if g == 4 and half == 0:
                                pe.wait_ge(mrow_done, now.next("mrow_done"))
                            if g >= 8 and half == 0:
                                pe.wait_ge(xo_done, now.next("xo_done"))
                            for k in range(4):
                                kt, bs = 4 * half + k, slice(b * P, (b + 1) * P)
                                mm(bank(g % 8), mix_hi[:, kt, bs], w_parts[0][:, k], kt == 0, False)
                                mm(bank(g % 8), mix_hi[:, kt, bs], w_parts[1][:, k], False, False)
                                ins = mm(bank(g % 8), mix_lo[:, kt, bs], w_parts[0][:, k], False, kt == KT - 1)
                            if half:
                                ins.then_inc(wout_mm, 1)
                pe.wait_ge(xo_done, now.next("xo_done", 8))
                h_transposes()
                router = col("router").rearrange("p (k e) -> p k e", k=KT)
                for b in range(NB):
                    for k in range(KT):
                        ins = mm(ps[:, b * 20:(b + 1) * 20], h[:, k, b * P:(b + 1) * P], router[:, k, :], k == 0, k == KT - 1)
                    ins.then_inc(router_mm, 1)
                mod_row_products(5 * KT)

                def weight_products(e):
                    for lo, hi in ((0, 512), (512, TOK)):
                        ins = mm(ps[:, 3072 + lo:3072 + hi], ident[:, e:e + 1].broadcast_to([P, P]), combT[:, lo:hi])
                    ins.then_inc(cb_mm, 1)

                pe.wait_ge(logits_read, now.next("logits_read"))
                pe.wait_ge(hlo_done, now.next("hlo_done"))
                v = 0
                for g in range(4):
                    for e in range(g * EG, (g + 1) * EG):
                        if e:
                            pe.wait_ge(cb_done, now.next("cb_done"))
                            weight_products(e)
                        for f in range(2):
                            pe.wait_ge(lo_done, now.next("lo_done"))
                            parts = [t.rearrange("p (k i c) -> p k i c", k=KT, i=2) for t in (hi_of(v), half_of(w_lo, v))]
                            for hf in range(2):
                                unit = 4 * e + 2 * f + hf
                                if unit >= 3 and unit % (4 * EG) >= 3:
                                    pe.wait_ge(hid_done, now.value("hid_done", unit - 2))
                                at = slice(hf * HALF, (hf + 1) * HALF)
                                for i, made in enumerate((egate_mm, up_mm)):
                                    for k in range(KT):
                                        out = bank(2 * (unit % 3) + i, HALF)
                                        mm(out, parts[0][:, k, i, :], h_hi[:, k, at], k == 0, False)
                                        mm(out, parts[0][:, k, i, :], h_lo[:, k, at], False, False)
                                        ins = mm(out, parts[1][:, k, i, :], h_hi[:, k, at], False, k == KT - 1)
                                    ins.then_inc(made, 1)
                            v += 1
                            if unit == 1:
                                pe.wait_ge(mrow_done, now.next("mrow_done"))
                                pe.wait_ge(comb_done, now.next("comb_done"))
                                for b in range(NB):
                                    ins = transpose(ps[:, 2048 + b * P:2048 + (b + 1) * P], comb[:, b, :])
                                ins.then_inc(combT_mm, 1)
                                pe.wait_ge(combT_done, now.next("combT_done"))
                                weight_products(0)
                    pe.wait_ge(hid_done, now.value("hid_done", 4 * EG * (g + 1)))
                    if g == 3:
                        pe.wait_ge(cb_done, now.next("cb_done"))
                    else:
                        pe.wait_ge(cb_done, now.value("cb_done", EG * (g + 1)))
                    for c in range(2):
                        for half in range(2):
                            pe.wait_ge(lo_done, now.next("lo_done"))
                            parts = [t.rearrange("p (k c) -> p k c", k=4) for t in (hi_of(v), half_of(w_lo, v))]
                            for b in range(NB):
                                if c and not half and b >= 3:
                                    if g < 3:
                                        pe.wait_ge(xe_done, now.value("xe_done", 10 * g + b - 2))
                                    else:
                                        pe.wait_ge(x_done, now.value("x_done", b - 2))
                                out = bank((c * NB + b) % 8)
                                for k in range(4):
                                    kt, bs = 4 * half + k, slice(b * P, (b + 1) * P)
                                    mm(out, hid_hi[:, kt, bs], parts[0][:, k, :], kt == 0, False)
                                    mm(out, hid_hi[:, kt, bs], parts[1][:, k, :], False, False)
                                    ins = mm(out, hid_lo[:, kt, bs], parts[0][:, k, :], False, kt == 7)
                                if half or b == NB - 1:
                                    ins.then_inc(down_mm, 1)
                            v += 1
                    if g < 3:
                        pe.wait_ge(xe_done, now.value("xe_done", 10 * (g + 1)))

        @block.scalar
        def _(act):
            now = Place()
            A = nc.scalar.activation

            def squares(behind_w_out=False):
                for b in range(NB):
                    if behind_w_out:
                        act.wait_ge(xo_done, now.next("xo_done", 1 if b else NB + 1))
                    ins = A(xn[:, b, :], x[:, b, :], ACT.Square, accum_out=ssq[:, b:b + 1])
                ins.then_inc(ssq_done, 1)

            def root(ap):
                act.wait_ge(var_ready, now.next("var_ready"))
                A(ap, ap, ACT.Sqrt).then_inc(std_ready, 1)

            def h_scaled(b_at, rounded=None):
                for f in range(0, KT, 2):
                    act.wait_ge(hT_mm, now.next("hT_mm"))
                    if f == 0:
                        act.wait_ge(mod_scale_done, now.next("mod_scale_done"))
                    o = 1024 * (f % 4)
                    for dst in ([rounded] if rounded is not None else []) + [h]:
                        A(dst[:, f, 0:P], ps[:, o:o + P], ACT.Identity, bias=modc[:, b_at + f, 0:1], scale=A1[:, f, 0:1])
                        ins = A(dst[:, f, P:TOK], ps[:, o + P:o + TOK], ACT.Identity, bias=modc[:, b_at + f, 1:2],
                                scale=A1[:, f, 1:2])
                    ins.then_inc(hT_act, 1)
                    act.wait_ge(hT_mm, now.next("hT_mm"))

            def round_in(v):
                j, u = v // 2, AT_IN + v // 2
                if v % 2 == 0:
                    act.wait_ge(slot_loaded[u % RING], now.load(u))
                if v >= 2:
                    act.wait_ge(z_mm, now.value("z_mm", 2 * ((j - 1) * NB + (NB if v % 2 else 1))))
                nc.scalar.copy(wz_hi[v % 2], half_in(ring, v)).then_inc(zhi_done, 1)

            def branch_out(n):
                act.wait_ge(brT_mm, now.next("brT_mm"))
                for f in range(FT):
                    ins = nc.scalar.copy(brT[:, 2 * n + f, :], ps[:, 2048 + 1024 * f:2048 + 1024 * f + TOK])
                ins.then_inc(brT_done, 1)

            def mod_row_out(i, bk):
                act.wait_ge(mod_mm, now.value("mod_mm", i + 1))
                nc.scalar.copy(mod_row, bank(bk)[0:2, :]).then_inc(mod_rows, 1)

            def mod_column_out(i, bk):
                act.wait_ge(modT_mm, now.value("modT_mm", i + 1))
                for j in range(4 * i, 4 * i + 4):
                    ins = A(modc[:, j, :], bank(bk)[:, 2 * (j - 4 * i):2 * (j - 4 * i) + 2], ACT.Identity, bias=col("bmod")[:, j:j + 1])
                ins.then_inc(modc_done, 1)

            def behind_out(lo, hi):
                for what, i, part, bk in PARTS[lo:hi]:
                    if what == "rows" and part:
                        mod_row_out(i, bk)
                    elif what == "cols":
                        mod_column_out(i, bk)
                    elif what == "gate" and part:
                        f, n = i // 8, i % 8 // 2
                        act.wait_ge(gate_mm, now.value("gate_mm", 2 * (i + 1)))
                        if i >= STAGES:
                            act.wait_ge(gates_kept[i % STAGES], now.value("gates_kept", 16 * (i // STAGES)))
                        A(stage[:, i % STAGES], bank(bk, HALF), ACT.Sigmoid,
                          bias=col("bgate")[:, n * KT + f:n * KT + f + 1]).then_inc(sig_done, 2)

            act.dma_start(sml[:, 0:16], a["c"]).then_inc(c_loaded, 16)
            act.dma_start(fix[:, :], a["fix"]).then_inc(constants_loaded, 16)
            act.dma_start(scanf[:, :], a["scanf"]).then_inc(constants_loaded, 16)
            act.dma_start(scanb[:, :], a["scanb"]).then_inc(constants_loaded, 16)
            act.wait_ge(c_loaded, 16)
            A(cS, cS, ACT.Silu).then_inc(silu_c_done, 1)
            with act.Fori(0, DEPTH) as layer:
                now.layer = layer
                act.wait_ge(x_done, now.value("x_done", 0))
                squares()
                act.dma_start(x_kept_dram, Xt[:, :]).then_inc(x_kept, 16)
                root(rstd)
                act.wait_ge(params_loaded, now.next("params_loaded", 32))
                for i in range(SLOTS_MOD):
                    mod_row_out(i, 4 + i)
                    mod_column_out(i, 4 + i)
                round_in(0)
                round_in(1)
                act.wait_ge(x_kept, now.next("x_kept", 16))
                h_scaled(0, hz_hi)
                for g in range(SLOTS_IN * NB):
                    if g % 2 == 0:
                        act.wait_ge(z_mm, now.value("z_mm", 2 * (g + 1)))
                        z_copies(g, nc.scalar.copy).then_inc(z_act, 1)
                    v = 2 * (g // NB) + 2
                    if g % NB == 0 and v < 2 * SLOTS_IN:
                        round_in(v)
                    if g % NB == NB - 1 and v < 2 * SLOTS_IN:
                        round_in(v + 1)
                act.wait_ge(z_act, now.next("z_act", 15))
                act.wait_ge(z_dve, now.next("z_dve", 15))
                A(zab[:, :, 0:512], zab[:, :, 0:512], ACT.Gelu_apprx_tanh).then_inc(gelu_done, 1)
                A(zab[:, :, 768:1024], zab[:, :, 768:1024], ACT.Sigmoid).then_inc(bsig_done, 1)
                A(zl[:, :, 256:384], zl[:, :, 256:384], ACT.Sigmoid)
                A(zl[:, :, 0:128], zl[:, :, 0:128], ACT.Tanh).then_inc(lora_done, 1)
                root(rstd)
                behind_out(0, closed(CONV_AT))
                branch_out(0)
                act.wait_ge(cin_mm, now.next("cin_mm"))
                act.wait_ge(pads_zeroed, now.next("pads_zeroed"))
                for f in range(FT):
                    nc.scalar.copy(cin[f][:, PAD:PAD + P], ps[:, 1024 * f:1024 * f + P])
                    ins = nc.scalar.copy(cin[f][:, PAD + P + PAD:PAD + P + PAD + LAT * P], ps[:, 1024 * f + P:1024 * f + TOK])
                ins.then_inc(cin_done, 1)
                behind_out(closed(CONV_AT), closed(LN_AT))
                root(rstd)
                act.wait_ge(cln_done, now.next("cln_done"))
                A(zab[:, :, 512:768], zab[:, :, 512:768], ACT.Silu).then_inc(oB_done, 1)
                behind_out(closed(LN_AT), closed(ATT_AT))
                branch_out(1)
                act.wait_ge(qkT_mm, now.next("qkT_mm"))
                act.wait_ge(keys_ready, now.next("keys_ready"))
                for g in range(2):
                    nc.scalar.copy(qT[:, g, :], ps[:, 1024 * g:1024 * g + TOK])
                nc.scalar.copy(kTz[0:64, 0, P:P + TOK], ps[0:64, 2048:2048 + TOK])
                nc.scalar.copy(kTz[64:128, 1, P:P + TOK], ps[64:128, 2048:2048 + TOK]).then_inc(qT_done, 1)
                for b in range(NB):
                    n = P if b == 0 else P * (2 + min(LAT, b + 1) - max(1, b - 1))
                    act.wait_ge(smax_done, now.next("smax_done"))
                    for hd in range(4):
                        A(sc[:, hd, 0:n], sc[:, hd, 0:n], ACT.Exp, bias=smx[:, hd:hd + 1], accum_out=rsm[:, hd:hd + 1])
                    A(snk, snk, ACT.Exp).then_inc(probs_done, 1)
                    part = ATT_AT + b * ATT_PARTS
                    behind_out(closed(part), closed(part + ATT_PARTS))
                branch_out(3)
                act.wait_ge(lorT_mm, now.next("lorT_mm"))
                for g in range(3):
                    ins = nc.scalar.copy(lorT[:, g, :], ps[:, 1024 * g:1024 * g + TOK])
                ins.then_inc(lorT_done, 1)
                for s, blocks in enumerate(STEPS):
                    part = SCAN_AT + s * STEP_PARTS
                    root(kss)
                    act.wait_ge(wa_pre, now.next("wa_pre"))
                    A(sw, sw, ACT.Sigmoid)
                    A(aa, aa, ACT.Sigmoid).then_inc(wa_done, 1)
                    behind_out(closed(part), part + WA_PARTS)
                    act.wait_ge(decay_mm, now.next("decay_mm"))
                    A(rt.rearrange("p d c -> p (d c)"), bank(2), ACT.Exp)
                    A(bt.rearrange("p d c -> p (d c)"), bank(2), ACT.Exp, scale=-1.0)
                    A(at_.rearrange("p d c -> p (d c)"), bank(3), ACT.Exp)
                    A(gm.rearrange("p g e -> p (g e)"), bank(4, 8), ACT.Exp).then_inc(exp_done, 1)
                    behind_out(part + WA_PARTS, closed(part + 5))
                    act.wait_ge(tildeT_mm, now.next("tildeT_mm"))
                    for par in range(2):
                        r = slice(64 * par, 64 * par + 64)
                        nc.scalar.copy(ar[r, :, par, 0, :], bank(0)[r].rearrange("p (g t) -> p g t", g=4))
                    nc.scalar.copy(bT, bank(2).rearrange("p (g t) -> p g t", g=4)).then_inc(tildeT_act, 1)
                    behind_out(closed(part + 5), part + 8)
                    for lev in range(LEVELS - 1):
                        act.wait_ge(x_mm, now.next("x_mm"))
                        nc.scalar.copy(Xc.rearrange("p g t -> p (g t)"), bank(0)).then_inc(xm_done, 1)
                        lo, _, hi = level_parts(part, lev)
                        behind_out(lo, hi)
                    act.wait_ge(u_mm, now.next("u_mm"))
                    nc.scalar.copy(ub.rearrange("p g v -> p (g v)"), bank(2)).then_inc(u_done, 1)
                    act.wait_ge(sa_mm, now.next("sa_mm"))
                    nc.scalar.mul(sa.rearrange("p g v -> p (g v)"), bank(3), -1.0).then_inc(sa_done, 1)
                root(gs2)
                behind_out(closed(NORM_AT), len(PARTS))
                branch_out(2)

                def round_out(v):
                    u = AT_OUT + v // 2
                    if v % 2 == 0:
                        act.wait_ge(slot_loaded[u % RING], now.load(u))
                    if v >= 2:
                        act.wait_ge(wout_mm, now.value("wout_mm", 1 if v == 2 else NB))
                    nc.scalar.copy(wo_hi[v % 2], half_in(ring, v, AT_OUT)).then_inc(ohi_done, 1)

                for f in range(KT):
                    act.wait_ge(mix_done, now.value("mix_done", 4 * (f + 1)))
                    nc.scalar.copy(mix_hi[:, f], mixT[:, f]).then_inc(mixhi_done, 1)
                act.wait_ge(proj_mm, now.value("proj_mm", 4 * KT))
                for v in range(2 * SLOTS_OUT):
                    round_out(v)
                    if v == 1:
                        act.wait_ge(mrow_mm, now.next("mrow_mm"))
                        nc.scalar.copy(mrow[:, 0, :], ps[:, 2048:3072])
                        nc.scalar.copy(mrow[:, 1, :], ps[:, 3072:4096]).then_inc(mrow_done, 1)
                squares(behind_w_out=True)
                root(rstd)
                h_scaled(3 * KT)
                act.wait_ge(hT_act, now.next("hT_act", KT))
                act.wait_ge(hT_dve, now.next("hT_dve", KT))
                nc.scalar.copy(h_hi, h).then_inc(hhi_done, 1)

                def round_weights(v):
                    u = AT_UP + v // 2
                    if v % 2 == 0:
                        act.wait_ge(slot_loaded[u % RING], now.load(u))
                    if v >= 2:
                        name, k = use_of_half(v - 2)
                        act.wait_ge(up_mm if name == "up_mm" else down_mm, now.value(name, k))
                    nc.scalar.copy(hi_of(v), half_of(ring, v)).then_inc(hi_done, 1)

                round_weights(0)
                round_weights(1)
                act.wait_ge(mrow_mm, now.next("mrow_mm"))
                nc.scalar.copy(mrow[:, 0, :], ps[:, 2048:3072])
                nc.scalar.copy(mrow[:, 1, :], ps[:, 3072:4096]).then_inc(mrow_done, 1)
                act.wait_ge(route_max, now.next("route_max"))
                A(lg[:, :, 0:4], lg[:, :, 0:4], ACT.Exp)
                A(ein[:, :, 0:1], ein[:, :, 0:1], ACT.Exp).then_inc(route_exp, 1)
                act.wait_ge(combT_mm, now.next("combT_mm"))
                nc.scalar.copy(combT, ps[:, 2048:2048 + TOK]).then_inc(combT_done, 1)

                for v in range(HALVES):
                    if 0 < v < HALVES - 1:
                        round_weights(v + 1)
                    g, at = place_of_half(v)
                    if at >= 2 * EG:
                        continue
                    e, f = g * EG + at // 2, at % 2
                    if f == 0:
                        act.wait_ge(cb_mm, now.next("cb_mm"))
                        if e >= 2:
                            act.wait_ge(hid_done, now.value("hid_done", 4 * (e - 1)))
                        nc.scalar.copy(cbs[:, e % 2, :], ps[:, 3072:3072 + TOK]).then_inc(cb_done, 1)
                    for hf in range(2):
                        unit = 4 * e + 2 * f + hf
                        act.wait_ge(egate_mm, now.next("egate_mm"))
                        if unit >= 2:
                            act.wait_ge(hid_done, now.value("hid_done", unit - 1))
                        A(sil[:, unit % 2, :], bank(2 * (unit % 3), HALF), ACT.Silu).then_inc(silu_done, 1)
            act.wait_ge(x_done, 1 + DEPTH * PER["x_done"])
            for b in range(NB):
                ins = A(xn[:, b, :], x[:, b, :], ACT.Square, accum_out=ssq[:, b:b + 1])
            ins.then_inc(final_sums, 1)
            act.wait_ge(final_var, 1)
            A(rstd, rstd, ACT.Sqrt).then_inc(final_std, 1)

        @block.vector
        def _(dve):
            now = Place()
            V = nc.vector

            def inverse_root(ap):
                dve.wait_ge(std_ready, now.next("std_ready"))
                V.reciprocal(ap, ap).then_inc(dve_chain, 1)
                dve.wait_ge(dve_chain, now.next("dve_chain"))

            def x_scaled():
                dve.wait_ge(ssq_done, now.next("ssq_done"))
                V.tensor_scalar(rstd, ssq, 1.0 / D, RMS_EPS, ALU.mult, ALU.add).then_inc(var_ready, 1)
                inverse_root(rstd)
                for b in range(NB):
                    V.tensor_scalar(xn[:, b, :], x[:, b, :], rstd[:, b:b + 1], None, ALU.mult).then_inc(xn_done, 1)

            def h_scaled(b_at, parts=None):
                for f in range(1, KT, 2):
                    dve.wait_ge(hT_mm, now.next("hT_mm", 2))
                    o = 1024 * (f % 4)
                    for dst in ([parts[0]] if parts else []) + [h]:
                        V.tensor_scalar(dst[:, f, 0:P], ps[:, o:o + P], A1[:, f, 0:1], modc[:, b_at + f, 0:1], ALU.mult, ALU.add)
                        ins = V.tensor_scalar(dst[:, f, P:TOK], ps[:, o + P:o + TOK], A1[:, f, 1:2],
                                              modc[:, b_at + f, 1:2], ALU.mult, ALU.add)
                    ins.then_inc(hT_dve, 1)
                    if parts:
                        dve.wait_ge(hT_dve, now.next("hT_dve"))
                        dve.wait_ge(hT_act, now.next("hT_act"))
                        two = slice(f - 1, f + 1)
                        ins = V.tensor_tensor(parts[1][:, two], h[:, two], parts[0][:, two].bitcast(F32), ALU.subtract)
                if parts:
                    ins.then_inc(hz_done, 1)

            def rest_in(v):
                dve.wait_ge(zhi_done, now.next("zhi_done"))
                V.tensor_tensor(half_in(w_lo, v), half_in(ring, v), wz_hi[v % 2].bitcast(F32), ALU.subtract).then_inc(zlo_done, 1)

            def mod_scale(s_at, norm):
                V.scalar_tensor_tensor(A1, modc[:, s_at:s_at + KT, :], 1.0, over(col(norm), 2, 2),
                                                              ALU.add, ALU.mult).then_inc(mod_scale_done, 1)
                dve.wait_ge(mod_scale_done, now.next("mod_scale_done"))

            def layer_stats(src):
                for b in range(NB):
                    ins = V.bn_stats(stats[:, 6 * b:6 * b + 6], src(b))
                ins.then_inc(dve_chain, 1)
                dve.wait_ge(dve_chain, now.next("dve_chain"))
                dve.sem_inc(waits_settled, 1)
                for b in range(NB):
                    ins = V.bn_aggr(mv[:, 2 * b:2 * b + 2], stats[:, 6 * b:6 * b + 6])
                ins.then_inc(dve_chain, 1)
                dve.wait_ge(dve_chain, now.next("dve_chain"))
                var = mv.rearrange("p (b e) -> p b e", e=2)[:, :, 1]
                V.tensor_scalar(rstd, var, LN_EPS, None, ALU.add).then_inc(var_ready, 1)
                inverse_root(rstd)

            def masked_gram(dst, half):
                for d in range(2):
                    o = SCANB["gram"][0] + 2 * d * P
                    ins = V.tensor_tensor(dst[:, 4 * d:4 * d + 4].rearrange("p g e t -> p g (e t)"),
                                          ps[:, half + 1024 * d:half + 1024 * d + 1024].rearrange("p (g c) -> p g c", g=4),
                                          over(scanb[:, o:o + 2 * P], 1, 4), ALU.mult)
                return ins

            def first_max(vals, n, best, onehot):
                iota = over(fixed("iota")[:, 0:n], 1, NB)
                V.tensor_reduce(best, vals, AX.X, ALU.max).then_inc(dve_chain, 1)
                dve.wait_ge(dve_chain, now.next("dve_chain"))
                V.tensor_tensor(t20, vals, over(best, 2, n), ALU.is_equal).then_inc(dve_chain, 1)
                dve.wait_ge(dve_chain, now.next("dve_chain"))
                V.scalar_tensor_tensor(t20, t20, -16.0, iota, ALU.mult, ALU.add).then_inc(dve_chain, 1)
                dve.wait_ge(dve_chain, now.next("dve_chain"))
                V.tensor_reduce(ix, t20, AX.X, ALU.min).then_inc(dve_chain, 1)
                dve.wait_ge(dve_chain, now.next("dve_chain"))
                V.tensor_tensor(onehot, t20, over(ix, 2, n), ALU.is_equal).then_inc(dve_chain, 1)
                dve.wait_ge(dve_chain, now.next("dve_chain"))

            dve.wait_ge(x_loaded, 16)
            V.memset(stats, 0.0).then_inc(x_done, 1)
            with dve.Fori(0, DEPTH) as layer:
                now.layer = layer
                x_scaled()
                dve.wait_ge(constants_loaded, 3 * 16)
                dve.wait_ge(params_loaded, now.next("params_loaded", 32))
                dve.wait_ge(modc_done, now.next("modc_done", SLOTS_MOD))
                mod_scale(KT, "norm1")
                rest_in(0)
                dve.wait_ge(x_kept, now.next("x_kept", 16))
                h_scaled(0, (hz_hi, hz_lo))
                rest_in(1)
                for g in range(SLOTS_IN * NB):
                    if g % 2:
                        dve.wait_ge(z_mm, now.value("z_mm", 2 * (g + 1)))
                        z_copies(g, V.tensor_copy).then_inc(z_dve, 1)
                    v = 2 * (g // NB) + 2
                    if g % NB == 0 and v < 2 * SLOTS_IN:
                        rest_in(v)
                    if g % NB == NB - 1 and v < 2 * SLOTS_IN:
                        rest_in(v + 1)
                dve.wait_ge(gelu_done, now.next("gelu_done"))
                v = zab[:, :, 256:512]
                layer_stats(lambda b: zab[:, b, 256:512])
                for b in range(NB):
                    ins = V.tensor_scalar(zab[:, b, 256:512], zab[:, b, 256:512], mv[:, 2 * b:2 * b + 1], rstd[:, b:b + 1],
                                          ALU.subtract, ALU.mult)
                ins.then_inc(dve_chain, 1)
                dve.wait_ge(dve_chain, now.next("dve_chain"))
                V.tensor_tensor(v, v, over(row("gmlp_g"), 1, NB), ALU.mult).then_inc(vn_done, 1)
                dve.wait_ge(bsig_done, now.next("bsig_done"))
                V.tensor_tensor(zab[:, :, 512:768], zab[:, :, 512:768], zab[:, :, 768:1024], ALU.mult).then_inc(glu_done, 1)
                dve.wait_ge(gmlp_mm, now.next("gmlp_mm"))
                for g in range(4):
                    u = zab[:, :, g * HD:(g + 1) * HD]
                    ins = V.scalar_tensor_tensor(u, bank(g, NB * HD).rearrange("p (b c) -> p b c", b=NB),
                                                 col("gmlp_bs")[:, g:g + 1], u, ALU.add, ALU.mult)
                ins.then_inc(oA_done, 1)
                dve.wait_ge(cin_done, now.next("cin_done"))
                cw = col("conv_w").rearrange("p (f t) -> p f t", f=FT)
                for t in range(TAPS):
                    for f in range(FT):
                        src = cin[f][:, t:t + OUTS]
                        if t == 0:
                            ins = V.tensor_scalar(cacc[f], src, cw[:, f, 0:1], col("conv_b")[:, f:f + 1], ALU.mult, ALU.add)
                        else:
                            ins = V.scalar_tensor_tensor(cacc[f], src, cw[:, f, t:t + 1], cacc[f], ALU.mult, ALU.add)
                    if t < TAPS - 1:
                        ins.then_inc(dve_chain, 1)
                        dve.wait_ge(dve_chain, now.next("dve_chain"))
                ins.then_inc(conv_done, 1)
                dve.wait_ge(convT_mm, now.next("convT_mm"))
                layer_stats(lambda b: ps[:, b * W:(b + 1) * W])
                for b in range(NB):
                    ins = V.tensor_scalar(zab[:, b, 512:768], ps[:, b * W:(b + 1) * W], mv[:, 2 * b:2 * b + 1],
                                          rstd[:, b:b + 1], ALU.subtract, ALU.mult)
                ins.then_inc(dve_chain, 1)
                dve.wait_ge(dve_chain, now.next("dve_chain"))
                ob = zab[:, :, 512:768]
                V.tensor_tensor(ob, ob, over(row("conv_g"), 1, NB), ALU.mult).then_inc(dve_chain, 1)
                dve.wait_ge(dve_chain, now.next("dve_chain"))
                V.tensor_tensor(ob, ob, over(row("conv_lb"), 1, NB), ALU.add).then_inc(cln_done, 1)
                cos = fixed("cos").rearrange("p (b c) -> p b c", b=LAT)
                sin = fixed("sin").rearrange("p (b a e c) -> p b a e c", b=LAT, a=2, e=2)
                zq = zd[:, 1:NB, 0:384]
                zq5 = zq.rearrange("p b (h a e c) -> p b h a e c", h=6, a=2, e=2)
                rp5 = ropet.rearrange("p b (h a e c) -> p b h a e c", h=6, a=2, e=2)
                for ax in range(2):
                    for e in range(2):
                        V.tensor_tensor(rp5[:, :, :, ax, e, :], zq5[:, :, :, ax, 1 - e, :], over(sin[:, :, ax, e, :], 2, 6), ALU.mult)
                V.tensor_tensor(qkr[:, 1:NB].rearrange("p b (h c) -> p b h c", h=6), zq.rearrange("p b (h c) -> p b h c", h=6),
                                       over(cos, 2, 6), ALU.mult).then_inc(dve_chain, 1)
                dve.wait_ge(dve_chain, now.next("dve_chain"))
                V.tensor_tensor(qkr[:, 1:NB], qkr[:, 1:NB], ropet, ALU.add).then_inc(rope_done, 1)
                dve.wait_ge(brT_done, now.next("brT_done", 2))
                for b in range(NB):
                    lo, hi = (0, 0) if b == 0 else (max(1, b - 1), min(LAT, b + 1))
                    nband = (hi - lo + 1) * P
                    n = nband + (P if b else 0)
                    S4 = ps[:, 0:2048].rearrange("p (h s) -> p h s", h=4)
                    dve.wait_ge(scores_mm, now.next("scores_mm"))
                    if b == 0:
                        V.tensor_scalar(sc[:, :, 0:n], S4[:, :, 0:n], SCALE, None, ALU.mult).then_inc(dve_chain, 1)
                        dve.wait_ge(dve_chain, now.next("dve_chain"))
                    else:
                        V.tensor_scalar(sc[:, :, 0:P], S4[:, :, 0:P], SCALE, None, ALU.mult)
                        o = (lo - b + 1) * P
                        V.scalar_tensor_tensor(sc[:, :, P:n], S4[:, :, P:n], SCALE, over(fixed("band")[:, o:o + nband], 1, 4),
                                                      ALU.mult, ALU.add).then_inc(dve_chain, 1)
                        dve.wait_ge(dve_chain, now.next("dve_chain"))
                    V.tensor_reduce(mx, sc[:, :, 0:n], AX.X, ALU.max).then_inc(dve_chain, 1)
                    dve.wait_ge(dve_chain, now.next("dve_chain"))
                    V.tensor_tensor(mx, mx, row("sink"), ALU.max).then_inc(dve_chain, 1)
                    dve.wait_ge(dve_chain, now.next("dve_chain"))
                    V.tensor_tensor(snk, row("sink"), mx, ALU.subtract)
                    V.tensor_scalar(smx, mx, -1.0, None, ALU.mult).then_inc(smax_done, 1)
                    dve.wait_ge(probs_done, now.next("probs_done"))
                    V.tensor_tensor(rsm, rsm, snk, ALU.add).then_inc(dve_chain, 1)
                    dve.wait_ge(dve_chain, now.next("dve_chain"))
                    V.reciprocal(rsm, rsm).then_inc(dve_chain, 1)
                    dve.wait_ge(dve_chain, now.next("dve_chain"))
                    dve.wait_ge(probsT_mm, now.next("probsT_mm"))
                    V.tensor_copy(pT[:, 0:n // P].rearrange("p s h q -> p (s h q)"), ps[:, 0:4 * n]).then_inc(probsT_done, 1)
                    dve.wait_ge(att_mm, now.next("att_mm"))
                    V.tensor_tensor(zd[:, b, 0:256].rearrange("p (h c) -> p h c", h=4),
                                                     bank(4, 256).rearrange("p (h c) -> p h c", h=4), over(rsm, 2, HD), ALU.mult).then_inc(att_done, 1)
                dve.wait_ge(scan_ready, now.next("scan_ready"))
                dve.wait_ge(cache_out, now.next("cache_out", 32))
                heads8 = "p d (h c) -> p (d h) c"
                for s, blocks in enumerate(STEPS):
                    if s == 0:
                        V.memset(S, 0.0).then_inc(dve_chain, 1)
                        dve.wait_ge(dve_chain, now.next("dve_chain"))
                    if s == 1:
                        V.tensor_copy(S.rearrange("p g v -> p (g v)"), col("state")).then_inc(dve_chain, 1)
                        dve.wait_ge(dve_chain, now.next("dve_chain"))
                    for d, blk in enumerate(blocks):
                        ins = V.tensor_tensor(kks[:, d], zc[:, blk, 256:512], row("kkw"), ALU.mult)
                    ins.then_inc(dve_chain, 1)
                    dve.wait_ge(dve_chain, now.next("dve_chain"))
                    V.tensor_tensor(kt_, kks, kks, ALU.mult).then_inc(dve_chain, 1)
                    dve.wait_ge(dve_chain, now.next("dve_chain"))
                    V.tensor_reduce(kss, kt_.rearrange(heads8, h=4), AX.X, ALU.add).then_inc(var_ready, 1)
                    dve.wait_ge(wa_mm, now.next("wa_mm"))
                    V.tensor_tensor(sw.rearrange("p d c -> p (d c)"), bank(4), row("w0"), ALU.add)
                    V.tensor_tensor(aa.rearrange("p d c -> p (d c)"), bank(5), row("a0"), ALU.add).then_inc(wa_pre, 1)
                    dve.wait_ge(std_ready, now.next("std_ready"))
                    V.tensor_scalar(kss, kss, 1e-12, None, ALU.max).then_inc(dve_chain, 1)
                    dve.wait_ge(dve_chain, now.next("dve_chain"))
                    V.reciprocal(kss, kss).then_inc(dve_chain, 1)
                    dve.wait_ge(dve_chain, now.next("dve_chain"))
                    V.tensor_tensor(kks.rearrange(heads8, h=4), kks.rearrange(heads8, h=4), over(kss, 2, HD), ALU.mult).then_inc(dve_chain, 1)
                    dve.wait_ge(dve_chain, now.next("dve_chain"))
                    dve.wait_ge(wa_done, now.next("wa_done"))
                    V.scalar_tensor_tensor(kt_, aa, -1.0, over(row("ka"), 1, 2), ALU.add, ALU.mult).then_inc(dve_chain, 1)
                    dve.wait_ge(dve_chain, now.next("dve_chain"))
                    for d, blk in enumerate(blocks):
                        ins = V.scalar_tensor_tensor(kt_[:, d], kt_[:, d], 1.0, zc[:, blk, 256:512], ALU.add, ALU.mult)
                    ins.then_inc(dve_chain, 1)
                    dve.wait_ge(dve_chain, now.next("dve_chain"))
                    tmp = Tc.rearrange("p a t -> p (a t)").rearrange("p (d c) -> p d c", d=2)
                    V.tensor_tensor(tmp, kt_, over(row("rk"), 1, 2), ALU.mult).then_inc(dve_chain, 1)
                    dve.wait_ge(dve_chain, now.next("dve_chain"))
                    for d, blk in enumerate(blocks):
                        ins = V.tensor_tensor(tmp[:, d], tmp[:, d], zc[:, blk, 0:256], ALU.mult)
                    ins.then_inc(dve_chain, 1)
                    dve.wait_ge(dve_chain, now.next("dve_chain"))
                    for d, blk in enumerate(blocks):
                        V.tensor_reduce(bon[:, blk, d], tmp[:, d].rearrange("p (h c) -> p h c", h=4), AX.X, ALU.add)
                    V.tensor_tensor(aa, aa, kks, ALU.mult).then_inc(dve_chain, 1)
                    dve.wait_ge(dve_chain, now.next("dve_chain"))
                    dve.wait_ge(exp_done, now.next("exp_done"))
                    for d, blk in enumerate(blocks):
                        V.tensor_tensor(rt[:, d], rt[:, d], zc[:, blk, 0:256], ALU.mult)
                    V.tensor_tensor(at_, at_, kks, ALU.mult)
                    V.tensor_tensor(kt_, kt_, bt, ALU.mult).then_inc(dve_chain, 1)
                    dve.wait_ge(dve_chain, now.next("dve_chain"))
                    V.tensor_tensor(bt, bt, aa, ALU.mult).then_inc(tilde_done, 1)
                    for d in range(2):
                        ins = V.tensor_tensor(S0[:, 2 * d:2 * d + 2], S[:, 2 * d:2 * d + 2], over(gm[:, 2 * d:2 * d + 2, d], 2, HD), ALU.mult)
                    ins.then_inc(s0_done, 1)
                    dve.wait_ge(tildeT_mm, now.next("tildeT_mm"))
                    for par in range(2):
                        r = slice(64 * par, 64 * par + 64)
                        V.tensor_copy(ar[r, :, par, 1, :], bank(1)[r].rearrange("p (g t) -> p g t", g=4))
                    V.tensor_copy(kT, bank(3).rearrange("p (g t) -> p g t", g=4)).then_inc(tildeT_dve, 1)
                    dve.wait_ge(gramB_mm, now.next("gramB_mm"))
                    masked_gram(gb, 0).then_inc(gb_done, 1)
                    dve.wait_ge(gramK_mm, now.next("gramK_mm"))
                    masked_gram(gk, 2048).then_inc(gk_done, 1)
                    dve.wait_ge(gb_done, now.next("gb_done"))
                    lv = SCANB["lev0"][0]
                    for d in range(2):
                        V.tensor_tensor(TT[:, 4 * d:4 * d + 4], gb[:, 4 * d:4 * d + 4, 0, :],
                                        over(scanb[:, lv + (2 + d) * P:lv + (3 + d) * P], 1, 4), ALU.mult)
                    dve.wait_ge(n_mm, now.next("n_mm"))
                    blocks64 = (slice(0, 64), slice(64, P))
                    for r in blocks64:
                        for d in range(2):
                            ins = V.tensor_tensor(Tc[r, 4 * d:4 * d + 4], bank(d)[r].rearrange("p (g t) -> p g t", g=4)[:, :, r],
                                                  over(scanb[r, lv + d * P + r.start:lv + d * P + r.stop], 1, 4), ALU.mult)
                    ins.then_inc(dve_chain, 1)
                    dve.wait_ge(dve_chain, now.next("dve_chain"))
                    V.tensor_tensor(TT, TT, over(ident, 1, 8), ALU.add)
                    for r in blocks64:
                        ins = V.tensor_tensor(Tc[r], Tc[r], over(ident[r, r], 1, 8), ALU.add)
                    ins.then_inc(t_done, 1)
                    dve.wait_ge(t_done, now.next("t_done"))
                    for r in blocks64:
                        ins = V.tensor_copy(TTc[r], TT[r, :, r])
                    ins.then_inc(tc_done, 1)
                    for lev in range(LEVELS - 1):
                        by_problem = [bank(i).rearrange("p (g t) -> p g t", g=8) for i in range(4)]
                        if lev < LEVELS - 2:
                            dve.wait_ge(xm_done, now.value("xm_done", s * (LEVELS - 1) + lev + 1))
                            for r in blocks64:
                                ins = V.tensor_copy(Xm[r, :, r], Xc[r])
                            ins.then_inc(xf_done, 1)
                        dve.wait_ge(y_mm, now.next("y_mm"))
                        dve.wait_ge(tc_done, now.next("tc_done"))
                        if lev < LEVELS - 2:
                            V.tensor_tensor(Tc, Tc, by_problem[2], ALU.subtract)
                            for r in blocks64:
                                ins = V.tensor_tensor(TT[r, :, r], TT[r, :, r], by_problem[3][r], ALU.subtract)
                            ins.then_inc(t_done, 1)
                            V.tensor_tensor(TTc, TTc, by_problem[3], ALU.subtract).then_inc(tc_done, 1)
                        else:
                            for d in range(2):
                                early, late = blocks64 if d == 0 else blocks64[::-1]
                                ins = V.tensor_scalar(TT[early, 4 * d:4 * d + 4, late], by_problem[3][early, 4 * d:4 * d + 4],
                                                      -1.0, None, ALU.mult)
                            ins.then_inc(t_done, 1)
                        dve.wait_ge(t_done, now.next("t_done"))
                    dve.wait_ge(step_mm, now.next("step_mm"))
                    for d, blk in enumerate(blocks):
                        first = (s < 3) and not (s == 0 and d == 1)
                        if s == 0 and d == 1:
                            ins.then_inc(dve_chain, 1)
                            dve.wait_ge(dve_chain, now.next("dve_chain"))
                        src = bank(0)[:, d * W:(d + 1) * W]
                        if first:
                            ins = V.tensor_copy(y[:, blk], src)
                        else:
                            ins = V.tensor_tensor(y[:, blk], y[:, blk], src, ALU.add)
                    V.tensor_tensor(S0, S0, bank(1, 256).rearrange("p (g v) -> p g v", g=4), ALU.add).then_inc(dve_chain, 1)
                    dve.wait_ge(dve_chain, now.next("dve_chain"))
                    dst = state_out if s == 0 else S
                    for d in range(2):
                        ins = V.tensor_tensor(dst[:, 2 * d:2 * d + 2], S0[:, 2 * d:2 * d + 2],
                                              over(gm[:, 2 * d:2 * d + 2, 1 - d], 2, HD), ALU.mult)
                        if d == 0:
                            ins.then_inc(dve_chain, 1)
                            dve.wait_ge(dve_chain, now.next("dve_chain"))
                    if s == 0:
                        ins.then_inc(state_ready, 1)
                        dve.wait_ge(state_ready, now.next("state_ready"))
                        V.memset(stats, 0.0).then_inc(step_done, 1)
                    else:
                        ins.then_inc(step_done, 1)
                    dve.wait_ge(step_done, now.next("step_done"))
                y20 = y.rearrange("p b (h c) -> p (b h) c", h=4)
                tmp = Xt[:, 0:NB * W].rearrange("p (b c) -> p b c", b=NB)
                tmp20 = tmp.rearrange("p b (h c) -> p (b h) c", h=4)
                V.tensor_reduce(gst, y20, AX.X, ALU.add).then_inc(dve_chain, 1)
                dve.wait_ge(dve_chain, now.next("dve_chain"))
                V.tensor_scalar(gst, gst, 1.0 / HD, None, ALU.mult).then_inc(dve_chain, 1)
                dve.wait_ge(dve_chain, now.next("dve_chain"))
                V.tensor_tensor(y20, y20, over(gst, 2, HD), ALU.subtract).then_inc(dve_chain, 1)
                dve.wait_ge(dve_chain, now.next("dve_chain"))
                V.tensor_tensor(tmp, y, y, ALU.mult).then_inc(dve_chain, 1)
                dve.wait_ge(dve_chain, now.next("dve_chain"))
                V.tensor_reduce(gs2, tmp20, AX.X, ALU.add).then_inc(dve_chain, 1)
                dve.wait_ge(dve_chain, now.next("dve_chain"))
                V.tensor_scalar(gs2, gs2, 1.0 / HD, GN_EPS, ALU.mult, ALU.add).then_inc(var_ready, 1)
                inverse_root(gs2)
                V.tensor_tensor(y20, y20, over(gs2, 2, HD), ALU.mult).then_inc(dve_chain, 1)
                dve.wait_ge(dve_chain, now.next("dve_chain"))
                V.tensor_tensor(y, y, over(row("lnx_g"), 1, NB), ALU.mult).then_inc(dve_chain, 1)
                dve.wait_ge(dve_chain, now.next("dve_chain"))
                V.tensor_tensor(y, y, over(row("lnx_b"), 1, NB), ALU.add).then_inc(dve_chain, 1)
                dve.wait_ge(dve_chain, now.next("dve_chain"))
                V.tensor_tensor(bon[:, :, 0], bon[:, :, 0], bon[:, :, 1], ALU.add).then_inc(dve_chain, 1)
                dve.wait_ge(dve_chain, now.next("dve_chain"))
                for b in range(NB):
                    ins = V.tensor_tensor(tmp[:, b].rearrange("p (h c) -> p h c", h=4), zc[:, b, 512:768].rearrange("p (h c) -> p h c", h=4),
                                          over(bon[:, b, 0], 2, HD), ALU.mult)
                ins.then_inc(dve_chain, 1)
                dve.wait_ge(dve_chain, now.next("dve_chain"))
                V.tensor_tensor(y, y, tmp, ALU.add).then_inc(dve_chain, 1)
                dve.wait_ge(dve_chain, now.next("dve_chain"))
                dve.wait_ge(g_mm, now.next("g_mm"))
                V.tensor_tensor(y, y, ps[:, 0:NB * W].rearrange("p (b c) -> p b c", b=NB), ALU.mult).then_inc(oC_done, 1)
                dve.wait_ge(brT_done, now.next("brT_done", 2))

                def mix_rest(f):
                    dve.wait_ge(mixhi_done, now.next("mixhi_done"))
                    V.tensor_tensor(mix_lo[:, f], mixT[:, f], mix_hi[:, f].bitcast(F32), ALU.subtract).then_inc(mixlo_done, 1)

                for unit in range(4 * KT):
                    f, n = unit // 4, unit % 4
                    u = AT_BACK + f
                    if n == 0:
                        dve.wait_ge(slot_loaded[u % RING], now.load(u))
                    gate = ring[:, (u % RING) * SLOT + n * TOK:(u % RING) * SLOT + (n + 1) * TOK]
                    dve.wait_ge(proj_mm, now.next("proj_mm"))
                    o = 1024 * (unit % 4)
                    if n == 0:
                        V.tensor_tensor(mixT[:, f, :], gate, ps[:, o:o + TOK], ALU.mult).then_inc(mix_done, 1)
                    else:
                        V.tensor_tensor(gate, gate, ps[:, o:o + TOK], ALU.mult).then_inc(dve_chain, 1)
                        dve.wait_ge(dve_chain, now.next("dve_chain"))
                        V.tensor_tensor(mixT[:, f, :], mixT[:, f, :], gate, ALU.add).then_inc(mix_done, 1)
                    dve.wait_ge(mix_done, now.next("mix_done"))
                    if n == 0 and f or unit == 4 * KT - 1:
                        mix_rest(f - 1 if n == 0 else f)

                def add_to_x(g):
                    c, b = g // NB, g % NB
                    acc, xv = bank(g % 8), x[:, b, c * 512:(c + 1) * 512]
                    V.tensor_tensor(acc, acc, mrow[:, 0 if b == 0 else 1, c * 512:(c + 1) * 512], ALU.mult).then_inc(dve_chain, 1)
                    dve.wait_ge(dve_chain, now.next("dve_chain"))
                    return V.tensor_tensor(xv, xv, acc, ALU.add)

                def rest_out(v):
                    dve.wait_ge(ohi_done, now.next("ohi_done"))
                    V.tensor_tensor(half_in(w_lo, v, AT_OUT), half_in(ring, v, AT_OUT), wo_hi[v % 2].bitcast(F32),
                                    ALU.subtract).then_inc(olo_done, 1)

                rest_out(0)
                rest_out(1)
                dve.wait_ge(mrow_done, now.next("mrow_done"))
                dve.wait_ge(x_back, now.next("x_back", 16))
                for g in range(10):
                    dve.wait_ge(wout_mm, now.next("wout_mm"))
                    add_to_x(g).then_inc(xo_done, 1)
                    if g == 0:
                        rest_out(2)
                    if g == NB - 1:
                        rest_out(3)
                dve.wait_ge(xo_done, now.next("xo_done", 10))
                x_scaled()
                dve.wait_ge(modc_done, now.next("modc_done", MODS - SLOTS_MOD))
                mod_scale(4 * KT, "norm2")
                h_scaled(3 * KT)
                def weights_rest(v):
                    dve.wait_ge(hi_done, now.next("hi_done"))
                    V.tensor_tensor(half_of(w_lo, v), half_of(ring, v), hi_of(v).bitcast(F32), ALU.subtract).then_inc(lo_done, 1)

                weights_rest(0)
                weights_rest(1)
                dve.wait_ge(router_mm, now.next("router_mm", NB))
                V.tensor_tensor(lg, ps[:, 0:100].rearrange("p (b e) -> p b e", b=NB), over(row("br"), 1, NB), ALU.add).then_inc(logits_read, 1)
                dve.wait_ge(logits_read, now.next("logits_read"))
                first_max(lg[:, :, 0:4], 4, m1, gsel)
                elog = lg[:, :, 4:20].rearrange("p b (g e) -> p b g e", g=4)
                for b in range(NB):
                    V.tensor_tensor(lg[:, b, 0:4], lg[:, b, 0:4], m1[:, b:b + 1].broadcast_to([P, 4]), ALU.subtract)
                    ins = V.tensor_tensor(t16[:, b], elog[:, b], over(gsel[:, b], 2, 4), ALU.mult)
                ins.then_inc(dve_chain, 1)
                dve.wait_ge(dve_chain, now.next("dve_chain"))
                for b in range(NB):
                    ins = V.tensor_reduce(ein[:, b], t16[:, b].rearrange("p g e -> p e g"), AX.X, ALU.add)
                ins.then_inc(dve_chain, 1)
                dve.wait_ge(dve_chain, now.next("dve_chain"))
                first_max(ein, 4, m1, oh1)
                V.scalar_tensor_tensor(ein, oh1, NEG, ein, ALU.mult, ALU.add).then_inc(dve_chain, 1)
                dve.wait_ge(dve_chain, now.next("dve_chain"))
                first_max(ein, 4, m2_, oh2)
                V.tensor_tensor(ein[:, :, 0], m2_, m1, ALU.subtract).then_inc(route_max, 1)
                dve.wait_ge(route_exp, now.next("route_exp"))
                V.tensor_reduce(gw, lg[:, :, 0:4], AX.X, ALU.add)
                V.tensor_scalar(m1, ein[:, :, 0], 1.0, None, ALU.add).then_inc(dve_chain, 1)
                dve.wait_ge(dve_chain, now.next("dve_chain"))
                V.tensor_tensor(gw, gw, m1, ALU.mult).then_inc(dve_chain, 1)
                dve.wait_ge(dve_chain, now.next("dve_chain"))
                V.reciprocal(gw, gw).then_inc(dve_chain, 1)
                dve.wait_ge(dve_chain, now.next("dve_chain"))
                V.tensor_tensor(m2_, gw, ein[:, :, 0], ALU.mult).then_inc(dve_chain, 1)
                dve.wait_ge(dve_chain, now.next("dve_chain"))
                V.tensor_tensor(oh1, oh1, over(gw, 2, 4), ALU.mult)
                V.tensor_tensor(oh2, oh2, over(m2_, 2, 4), ALU.mult).then_inc(dve_chain, 1)
                dve.wait_ge(dve_chain, now.next("dve_chain"))
                V.tensor_tensor(oh1, oh1, oh2, ALU.add).then_inc(dve_chain, 1)
                dve.wait_ge(dve_chain, now.next("dve_chain"))
                V.memset(comb, 0.0).then_inc(dve_chain, 1)
                dve.wait_ge(dve_chain, now.next("dve_chain"))
                for b in range(NB):
                    ins = V.tensor_tensor(comb[:, b, 0:16].rearrange("p (g e) -> p g e", g=4), over(gsel[:, b], 2, 4),
                                          over(oh1[:, b], 1, 4), ALU.mult)
                ins.then_inc(comb_done, 1)
                for v in range(HALVES):
                    if 0 < v < HALVES - 1:
                        weights_rest(v + 1)
                    g, at = place_of_half(v)
                    if at < 2 * EG:
                        e, f = g * EG + at // 2, at % 2
                        for hf in range(2):
                            unit = 4 * e + 2 * f + hf
                            s_ = sil[:, unit % 2, :]
                            tokens = slice(hf * HALF, (hf + 1) * HALF)
                            place = [t[:, 2 * (e % EG) + f, tokens] for t in (hid_hi, hid_lo)]
                            dve.wait_ge(silu_done, now.next("silu_done"))
                            dve.wait_ge(up_mm, now.next("up_mm"))
                            V.tensor_tensor(s_, s_, bank(2 * (unit % 3) + 1, HALF), ALU.mult).then_inc(dve_chain, 1)
                            dve.wait_ge(dve_chain, now.next("dve_chain"))
                            if f == 0 and hf == 0:
                                dve.wait_ge(cb_done, now.next("cb_done"))
                            V.tensor_tensor(s_, s_, cbs[:, e % 2, tokens], ALU.mult).then_inc(dve_chain, 1)
                            dve.wait_ge(dve_chain, now.next("dve_chain"))
                            V.tensor_copy(place[0], s_).then_inc(dve_chain, 1)
                            dve.wait_ge(dve_chain, now.next("dve_chain"))
                            V.tensor_tensor(place[1], s_, place[0].bitcast(F32), ALU.subtract).then_inc(hid_done, 1)
                    elif at % 2:
                        c = (at - 2 * EG) // 2
                        if v == 2 * EG + 1:
                            dve.wait_ge(mrow_done, now.next("mrow_done"))
                        if g and c == 0:
                            dve.wait_ge(xe_done, now.value("xe_done", 10 * g))
                        for b in range(NB):
                            dve.wait_ge(down_mm, now.value("down_mm", 12 * g + 6 * c + 1 + b + 1))
                            if g < 3:
                                add_to_x(c * NB + b).then_inc(xe_done, 1)
                            else:
                                add_to_x(c * NB + b).then_inc(x_done, 1)
                dve.wait_ge(x_done, now.next("x_done", 10))
            dve.wait_ge(final_sums, 1)
            V.tensor_scalar(rstd, ssq, 1.0 / D, RMS_EPS, ALU.mult, ALU.add).then_inc(final_var, 1)
            dve.wait_ge(final_std, 1)
            V.reciprocal(rstd, rstd).then_inc(final_chain, 1)
            dve.wait_ge(final_chain, 1)
            dve.wait_ge(final_g_loaded, 16)
            for b in range(NB):
                ins = V.scalar_tensor_tensor(xn[:, b, :], x[:, b, :], rstd[:, b:b + 1], arena[:, 10240:10240 + D],
                                             ALU.mult, ALU.mult)
            ins.then_inc(final_done, 1)




def shape_constants():
    t = np.arange(P)
    fix = np.zeros((P, NFIX), np.float32)
    o = FIX["ident"][0]
    fix[:, o:o + P] = np.eye(P)
    half = HD // 4
    inv = 10000.0 ** (-np.arange(half, dtype=np.float32) / np.float32(half))
    tok = np.arange(LAT * P)
    ang = np.stack([(tok // 64)[:, None] * inv, (tok % 64)[:, None] * inv], 1).astype(np.float32)
    cos, sin = np.cos(ang), np.sin(ang)
    c = np.stack([cos, cos], 2).reshape(LAT, P, HD).transpose(1, 0, 2)
    s = np.stack([-sin, sin], 2).reshape(LAT, P, HD).transpose(1, 0, 2)
    for name, v in (("cos", c), ("sin", s)):
        o, n = FIX[name]
        fix[:, o:o + n] = v.reshape(P, n)
    o = FIX["band"][0]
    fix[:, o:o + P] = np.where(t[None, :] >= t[:, None], 0.0, NEG)
    fix[:, o + 2 * P:o + 3 * P] = np.where(t[None, :] <= t[:, None], 0.0, NEG)
    o = FIX["iota"][0]
    fix[:, o:o + 4] = np.arange(4)
    scanf = np.zeros((P, NSCANF), np.float32)
    s_, t_ = t[:, None], t[None, :]
    rate = -np.exp(-0.5)
    for d in range(2):
        lead = (s_ < 64) if d == 0 else (s_ >= 64)
        up, before = (s_ <= t_, s_ < t_) if d == 0 else (s_ >= t_, s_ > t_)
        for name, m in (("incl", up), ("excl", before)):
            o = SCANF[name][0] + d * P
            scanf[:, o:o + P] = rate * (m.astype(np.float32) - lead.astype(np.float32))
    o = SCANF["halves"][0]
    scanf[:, o] = rate * (t < 64)
    scanf[:, o + 1] = rate * (t >= 64)
    scanb = np.zeros((P, NSCANB), np.float32)
    for d in range(2):
        strict, incl = (s_ < t_, s_ <= t_) if d == 0 else (s_ > t_, s_ >= t_)
        o = SCANB["gram"][0] + 2 * d * P
        scanb[:, o:o + P], scanb[:, o + P:o + 2 * P] = strict, incl
        for lev in range(LEVELS):
            m = 1 << lev
            pair = (s_ // (2 * m) == t_ // (2 * m)) & (s_ // m != t_ // m) & strict
            if lev:
                o = SCANB["lev"][0] + ((lev - 1) * 2 + d) * P
                scanb[:, o:o + P] = pair
            else:
                o = SCANB["lev0"][0] + d * P
                scanb[:, o:o + P] = -pair.T.astype(np.float32)
                scanb[:, o + 2 * P:o + 3 * P] = -pair.astype(np.float32)
    return fix, scanf, scanb


def kernel(**inputs):
    import concourse.bacc as bacc
    from concourse.bass_utils import run_bass_kernel_spmd

    i = {k: np.asarray(v) for k, v in inputs.items()}
    L = DEPTH

    def tiles(w, n=512):
        v = w.reshape(L, -1, P, w.shape[-1] // n, n)
        return v.transpose(0, 3, 2, 1, 4).reshape(L, v.shape[3], P, -1)

    q0 = 2176
    order = np.concatenate([np.arange(q0), *[q0 + hd * HD + np.arange(HD) for hd in (0, 2, 1, 3)], np.arange(q0 + W, 2688)])
    w_in = np.zeros((L, D, 3072), np.float32)
    w_in[:, :, :2688] = i["w_in"][:, :, order]
    gate = i["w_gate"].reshape(L, KT, P, 4, KT, P).transpose(0, 4, 2, 1, 3, 5).reshape(L, KT, P, SLOT)
    up = np.stack([i["w_e_gate"], i["w_e_up"]], 3).reshape(L, NE, KT, P, 2, 2, P).transpose(0, 1, 3, 5, 2, 4, 6)
    up = up.reshape(L, 4, EG, P, SLOT)
    down = i["w_e_down"].reshape(L, 4, KT, P, 2, 512).transpose(0, 1, 4, 3, 2, 5).reshape(L, 4, 2, P, SLOT)
    experts = np.concatenate([up, down], 2).reshape(L, SLOTS_UP + SLOTS_DOWN, P, SLOT)
    mod = tiles(i["w_mod"])
    behind = np.stack([mod[:, SLOTS_MOD:], gate], 2).reshape(L, SLOTS_BEHIND, P, SLOT)
    stream = np.concatenate([mod[:, :SLOTS_MOD], tiles(w_in), behind, tiles(i["w_out"]), experts], 1).reshape(-1, P, SLOT)
    stream = np.concatenate([stream, np.zeros((RING, P, SLOT), np.float32)])
    wbranch = i["w_branch"].reshape(L, 4, 2, P, KT, P).transpose(0, 3, 4, 1, 2, 5).reshape(L, P, 8 * D)

    def vec(v):
        return v.reshape(L, -1, P).transpose(0, 2, 1)

    def diagonal(w):
        z = np.zeros((L, 2, 64, 2, W), np.float32)
        for d in range(2):
            z[:, d, :, d] = w[:, d]
        return z.reshape(L, P, 2 * W)

    cols = {
        "norm1": vec(i["norm1_g"]), "norm2": vec(i["norm2_g"]), "bmod": vec(i["b_mod"]), "bgate": vec(i["b_gate"]),
        "gmlp_bs": i["gmlp_bs"].transpose(0, 2, 1),
        "conv_w": i["conv_w"].reshape(L, TAPS, FT, P).transpose(0, 3, 2, 1).reshape(L, P, -1),
        "conv_b": vec(i["conv_b"]), "wsT": i["gmlp_ws"].transpose(0, 3, 1, 2).reshape(L, P, 4 * P),
        "w2": diagonal(i["rwkv_w2"]), "a2": diagonal(i["rwkv_a2"]), "g2": i["rwkv_g2"],
        "ckT": i["cache_k"][0].reshape(L, P, P).transpose(0, 2, 1), "cv": i["cache_v"][0].reshape(L, P, P),
        "router": np.concatenate([i["w_rg"], i["w_re"]], 2).reshape(L, KT, P, 20).transpose(0, 2, 1, 3).reshape(L, P, -1),
        "state": i["state_rwkv"][0].reshape(L, 2, 2, 2, HD, HD).transpose(0, 3, 5, 1, 2, 4).reshape(L, P, 4 * HD),
    }
    rows = {
        "gmlp_g": i["gmlp_ln_g"], "conv_g": i["conv_ln_g"], "conv_lb": i["conv_ln_b"], "w0": i["rwkv_w0"], "a0": i["rwkv_a0"],
        "kkw": i["rwkv_kk"], "ka": i["rwkv_ka"], "rk": i["rwkv_rk"], "lnx_g": i["rwkv_lnx_g"], "lnx_b": i["rwkv_lnx_b"],
        "sink": i["attn_sink"], "br": np.concatenate([i["b_rg"], i["b_re"]], 1),
    }
    fix, scanf, scanb = shape_constants()
    arrays = {
        "stream": stream, "wbranch": wbranch,
        "cols": np.concatenate([cols[n].reshape(L, P, COLS[n][1]) for n in COLS], 2),
        "rows": np.concatenate([rows[n].reshape(L, 1, ROWS[n][1]) for n in ROWS], 2),
        "fix": fix, "scanf": scanf, "scanb": scanb,
        "x": np.concatenate([i["x_prompt"][0], i["x_sample"][0]]).reshape(NB, P, D).transpose(1, 0, 2).reshape(P, NB * D),
        "c": np.stack([i["c_ctx"], i["c"][0]]).reshape(2, KT, P).transpose(2, 1, 0).reshape(P, 2 * KT),
        "final_g": i["final_norm_g"].reshape(1, D),
    }
    outputs = {"y_prompt": (P, D), "y_sample": (LAT * P, D), "new_k": (L, P, P), "new_v": (L, P, P), "new_s": (L, P, 4 * HD)}
    nc = bacc.Bacc("TRN2", target_bir_lowering=False, num_devices=1)
    feed, args = {}, {}
    for name, v in arrays.items():
        v = np.ascontiguousarray(v)
        feed[f"in_{name}"] = v
        args[name] = nc.dram_tensor(f"in_{name}", v.shape, mybir.dt.from_np(v.dtype), kind="ExternalInput").ap()
    for name, shape in outputs.items():
        args[name] = nc.dram_tensor(f"out_{name}", shape, F32, kind="ExternalOutput").ap()
    build(nc, args)
    r = run_bass_kernel_spmd(nc, [feed], core_ids=[0]).results[0]
    s = r["out_new_s"].reshape(L, 2, HD, 2, 2, HD).transpose(0, 3, 4, 1, 5, 2).reshape(1, L, 2, 4, HD, HD)
    return (r["out_y_prompt"].reshape(1, P, D), r["out_y_sample"].reshape(1, LAT * P, D),
            r["out_new_k"].reshape(1, L, P, 2, HD), r["out_new_v"].reshape(1, L, P, 2, HD), s)
```
